# Optimizing a Trainium2 kernel written in Bass

```python
import jax, jax.numpy as jnp
from jax import lax
import numpy as np

D_MODEL = 1024
BATCH = 1
SEQ = 256
DEPTH = 2

N_MEM = 256
XA_HEADS = 4
XA_HD = D_MODEL // XA_HEADS
W_A = D_MODEL
H_A = 8
HD_A = W_A // H_A
CONV_A = 4
C_RG = 8.0
W_B = D_MODEL // 2
POOL_WINDOWS = (2, 4, 8, 16)
G_B = len(POOL_WINDOWS)
HD_B = W_B // G_B
IN_AB = 2 * W_A + W_B
OUT_AB = W_A + W_B
CONV_C = 31
D_FF = 3 * D_MODEL
CONV_F = 3
EPS = 1e-6
N_EVEN = (DEPTH + 1) // 2
N_ODD = DEPTH // 2


def rms_norm(x, g):
    xf = x.astype(jnp.float32)
    y = xf * lax.rsqrt(jnp.mean(xf * xf, axis=-1, keepdims=True) + EPS)
    return (y * g.astype(jnp.float32)).astype(x.dtype)

def layer_norm(x, g, b):
    xf = x.astype(jnp.float32)
    mu = jnp.mean(xf, axis=-1, keepdims=True)
    var = jnp.mean(jnp.square(xf - mu), axis=-1, keepdims=True)
    y = (xf - mu) * lax.rsqrt(var + EPS)
    return (y * g.astype(jnp.float32) + b.astype(jnp.float32)).astype(x.dtype)

def causal_dwconv(x, w, b):
    K, C = w.shape
    y = lax.conv_general_dilated(
        x, w[:, None, :], window_strides=(1,), padding=[(K - 1, 0)],
        dimension_numbers=("NWC", "WIO", "NWC"), feature_group_count=C)
    return y + b

def rg_lru(x, w_gx, b_gx, w_ga, b_ga, lam):
    Bn, S, W = x.shape
    xh = x.reshape(Bn, S, H_A, HD_A)
    gate_x = jax.nn.sigmoid(jnp.einsum('bshi,hij->bshj', xh, w_gx).reshape(Bn, S, W) + b_gx)
    gate_a = jax.nn.sigmoid(jnp.einsum('bshi,hij->bshj', xh, w_ga).reshape(Bn, S, W) + b_ga)
    log_a = -C_RG * gate_a.astype(jnp.float32) * jax.nn.softplus(-lam.astype(jnp.float32))
    a = jnp.exp(log_a)
    mult = jnp.sqrt(-jnp.expm1(2.0 * log_a))
    bx = mult * (gate_x * x).astype(jnp.float32)

    def combine(lhs, rhs):
        a_l, b_l = lhs
        a_r, b_r = rhs
        return a_l * a_r, a_r * b_l + b_r

    _, h = lax.associative_scan(combine, (a, bx), axis=1)
    return h.astype(x.dtype)

def multi_scale_pool(u, w_g, b_g, scale):
    Bn, S, W = u.shape
    uf = u.astype(jnp.float32)
    csum = jnp.cumsum(uf, axis=1)
    t = jnp.arange(1, S + 1, dtype=jnp.float32)[:, None]
    outs = []
    for g, w in enumerate(POOL_WINDOWS):
        sl = slice(g * HD_B, (g + 1) * HD_B)
        cg = csum[..., sl]
        lagged = jnp.pad(cg[:, :S - w], ((0, 0), (w, 0), (0, 0)))
        mean = (cg - lagged) / jnp.minimum(t, float(w))
        outs.append(mean - uf[..., sl])
    p = jnp.stack(outs, axis=2).astype(u.dtype)
    y = jnp.einsum('bsgi,gij->bsgj', p, w_g).reshape(Bn, S, W) + b_g
    return y * scale

def mixer_ab(x, norm, w_in, conv_w, conv_b, w_gx, b_gx, w_ga, b_ga, lam, w_pool, b_pool, pool_scale, w_out):
    z = rms_norm(x, norm) @ w_in
    z_gate = z[..., :W_A]
    z_rec = z[..., W_A:2 * W_A]
    z_pool = z[..., 2 * W_A:]
    xr = causal_dwconv(z_rec, conv_w, conv_b)
    y_a = jax.nn.gelu(z_gate) * rg_lru(xr, w_gx, b_gx, w_ga, b_ga, lam)
    y_b = multi_scale_pool(z_pool, w_pool, b_pool, pool_scale)
    return jnp.concatenate([y_a, y_b], axis=-1) @ w_out

def conformer_conv(x, norm, w1, b1, dw_w, dw_b, ln_g, ln_b, w2, b2):
    h = rms_norm(x, norm) @ w1 + b1
    h = jax.nn.glu(h, axis=-1)
    h = causal_dwconv(h, dw_w, dw_b)
    h = jax.nn.silu(layer_norm(h, ln_g, ln_b))
    return h @ w2 + b2

def cross_attn(x, mem, norm, mem_norm, wq, wk, wv, wo):
    Bn, S, _ = x.shape
    M = mem.shape[1]
    q = (rms_norm(x, norm) @ wq).reshape(Bn, S, XA_HEADS, XA_HD)
    m = rms_norm(mem, mem_norm)
    k = (m @ wk).reshape(Bn, M, XA_HEADS, XA_HD)
    v = (m @ wv).reshape(Bn, M, XA_HEADS, XA_HD)
    s = jnp.einsum('bqhd,bkhd->bhqk', q, k).astype(jnp.float32) * (XA_HD ** -0.5)
    p = jax.nn.softmax(s, axis=-1).astype(x.dtype)
    o = jnp.einsum('bhqk,bkhd->bqhd', p, v).reshape(Bn, S, D_MODEL)
    return o @ wo

def conv_ffn(x, norm, w_up, dw_w, dw_b, w_down):
    h = rms_norm(x, norm) @ w_up
    g = causal_dwconv(h[..., :D_FF], dw_w, dw_b)
    u = h[..., D_FF:]
    return (jax.nn.gelu(g) * u) @ w_down

def first_inputs(seed: int = 0) -> dict:
    key = jax.random.key(seed)
    keys = iter(jax.random.split(key, 48))

    def nrm(shape, scale):
        return jax.random.normal(next(keys), shape, jnp.float32) * scale

    def gain(shape):
        return 1.0 + 0.02 * jax.random.normal(next(keys), shape, jnp.float32)

    L, NE, NO, D = DEPTH, N_EVEN, N_ODD, D_MODEL
    u = jax.random.uniform(next(keys), (NE, W_A), jnp.float32, 0.9, 0.999) ** (1.0 / C_RG)
    lam = jnp.log(u) - jnp.log1p(-u)
    return {
        "x": jax.random.normal(next(keys), (BATCH, SEQ, D), jnp.float32),
        "mem": jax.random.normal(next(keys), (BATCH, N_MEM, D), jnp.float32),
        "ab_norm": gain((NE, D)),
        "ab_w_in": nrm((NE, D, IN_AB), D ** -0.5),
        "a_conv_w": nrm((NE, CONV_A, W_A), CONV_A ** -0.5),
        "a_conv_b": nrm((NE, W_A), 0.01),
        "a_gate_x_w": nrm((NE, H_A, HD_A, HD_A), HD_A ** -0.5),
        "a_gate_x_b": nrm((NE, W_A), 0.01),
        "a_gate_a_w": nrm((NE, H_A, HD_A, HD_A), HD_A ** -0.5),
        "a_gate_a_b": nrm((NE, W_A), 0.01),
        "a_lambda": lam,
        "b_group_w": nrm((NE, G_B, HD_B, HD_B), HD_B ** -0.5),
        "b_group_b": nrm((NE, W_B), 0.01),
        "b_scale": 1.0 + 0.1 * jax.random.normal(next(keys), (NE, W_B), jnp.float32),
        "ab_w_out": nrm((NE, OUT_AB, D), OUT_AB ** -0.5),
        "c_norm": gain((NO, D)),
        "c_w_pw1": nrm((NO, D, 2 * D), D ** -0.5),
        "c_b_pw1": nrm((NO, 2 * D), 0.01),
        "c_dw_w": nrm((NO, CONV_C, D), CONV_C ** -0.5),
        "c_dw_b": nrm((NO, D), 0.01),
        "c_ln_g": gain((NO, D)),
        "c_ln_b": nrm((NO, D), 0.01),
        "c_w_pw2": nrm((NO, D, D), D ** -0.5),
        "c_b_pw2": nrm((NO, D), 0.01),
        "xa_norm": gain((L, D)),
        "xa_mem_norm": gain((L, D)),
        "xa_wq": nrm((L, D, D), D ** -0.5),
        "xa_wk": nrm((L, D, D), D ** -0.5),
        "xa_wv": nrm((L, D, D), D ** -0.5),
        "xa_wo": nrm((L, D, D), D ** -0.5),
        "f_norm": gain((L, D)),
        "f_w_up": nrm((L, D, 2 * D_FF), D ** -0.5),
        "f_dw_w": nrm((L, CONV_F, D_FF), CONV_F ** -0.5),
        "f_dw_b": nrm((L, D_FF), 0.01),
        "f_w_down": nrm((L, D_FF, D), D_FF ** -0.5),
        "final_norm": gain((D,)),
    }

def first_block(x, mem, ab_norm, ab_w_in, a_conv_w, a_conv_b, a_gate_x_w, a_gate_x_b,
              a_gate_a_w, a_gate_a_b, a_lambda, b_group_w, b_group_b, b_scale, ab_w_out,
              c_norm, c_w_pw1, c_b_pw1, c_dw_w, c_dw_b, c_ln_g, c_ln_b, c_w_pw2, c_b_pw2,
              xa_norm, xa_mem_norm, xa_wq, xa_wk, xa_wv, xa_wo,
              f_norm, f_w_up, f_dw_w, f_dw_b, f_w_down, final_norm):
    for layer in range(DEPTH):
        if layer % 2 == 0:
            i = layer // 2
            x = x + mixer_ab(x, ab_norm[i], ab_w_in[i], a_conv_w[i], a_conv_b[i],
                             a_gate_x_w[i], a_gate_x_b[i], a_gate_a_w[i], a_gate_a_b[i],
                             a_lambda[i], b_group_w[i], b_group_b[i], b_scale[i], ab_w_out[i])
        else:
            j = layer // 2
            x = x + conformer_conv(x, c_norm[j], c_w_pw1[j], c_b_pw1[j], c_dw_w[j], c_dw_b[j],
                                   c_ln_g[j], c_ln_b[j], c_w_pw2[j], c_b_pw2[j])
        x = x + cross_attn(x, mem, xa_norm[layer], xa_mem_norm[layer], xa_wq[layer],
                           xa_wk[layer], xa_wv[layer], xa_wo[layer])
        x = x + conv_ffn(x, f_norm[layer], f_w_up[layer], f_dw_w[layer], f_dw_b[layer],
                         f_w_down[layer])
    return rms_norm(x, final_norm)


DEPTH_2 = 1

HEAD_DIM = 64
BLOCK = 128
DIL_PATTERNS = ((128, 1), (512, 4), (2048, 16))
N_DIL_GROUPS = 3
DIL_HEADS_PER_GROUP = 8
DIL_HEADS = N_DIL_GROUPS * DIL_HEADS_PER_GROUP
DIL_WIDTH = DIL_HEADS * HEAD_DIM
DIL_MERGED = DIL_HEADS_PER_GROUP * HEAD_DIM
SWA_WINDOW = 128
SWA_Q_HEADS = 16
SWA_KV_HEADS = 2
SWA_Q_WIDTH = SWA_Q_HEADS * HEAD_DIM
SWA_KV_WIDTH = SWA_KV_HEADS * HEAD_DIM
IN_WIDTHS = (DIL_WIDTH, DIL_WIDTH, DIL_WIDTH, SWA_Q_WIDTH, SWA_KV_WIDTH, SWA_KV_WIDTH, D_MODEL, D_MODEL)
IN_WIDTH = sum(IN_WIDTHS)
MOE_GROUPS = 4
EXPERTS_PER_GROUP = 8
N_EXPERTS = MOE_GROUPS * EXPERTS_PER_GROUP
TOP_K = 2
D_EXPERT = 512
RMS_EPS = 1e-6


def rmsnorm(x, gain):
    x32 = x.astype(jnp.float32)
    y = x32 * lax.rsqrt(jnp.mean(x32 * x32, axis=-1, keepdims=True) + RMS_EPS)
    return (y * gain.astype(jnp.float32)).astype(x.dtype)

def alibi_slopes(n):
    return (2.0 ** (-8.0 * np.arange(1, n + 1) / n)).astype(np.float32)

def split_cols(proj, widths):
    offs = [0]
    for w in widths:
        offs.append(offs[-1] + w)
    return [proj[..., offs[i]:offs[i + 1]] for i in range(len(widths))]

def banded_attention(q, k, v, slopes, max_back, unit, sinks=None):
    b, s, l, hq, hd = q.shape
    hkv = k.shape[3]
    rep = hq // hkv
    nb = -(-l // BLOCK)
    lp = nb * BLOCK
    pad = [(0, 0), (0, 0), (0, lp - l), (0, 0), (0, 0)]
    qb = jnp.pad(q, pad).reshape(b, s, nb, BLOCK, hkv, rep, hd)
    kb = jnp.pad(k, pad).reshape(b, s, nb, BLOCK, hkv, hd)
    vb = jnp.pad(v, pad).reshape(b, s, nb, BLOCK, hkv, hd)

    def with_prev(z):
        prev = jnp.pad(z[:, :, :-1], [(0, 0), (0, 0), (1, 0), (0, 0), (0, 0), (0, 0)])
        return jnp.concatenate([prev, z], axis=3)

    kk, vv = with_prev(kb), with_prev(vb)
    scores = jnp.einsum('bsnqgrd,bsnkgd->bsngrqk', qb, kk,
                        preferred_element_type=jnp.float32) * (hd ** -0.5)
    a = np.arange(BLOCK)[:, None]
    c = np.arange(2 * BLOCK)[None, :]
    delta = a + BLOCK - c
    band = (delta >= 0) & (delta <= max_back)
    valid = band[None] & ((np.arange(nb)[:, None, None] > 0) | (c >= BLOCK)[None])
    bias = (-slopes.reshape(hkv, rep)[:, :, None, None] * (delta * unit)[None, None]).astype(np.float32)
    scores = jnp.where(valid[None, None, :, None, None], scores + bias, -jnp.inf)
    m = scores.max(axis=-1)
    if sinks is not None:
        sink = sinks.astype(jnp.float32).reshape(hkv, rep)[:, :, None]
        m = jnp.maximum(m, sink)
    p = jnp.exp(scores - m[..., None])
    denom = p.sum(axis=-1)
    if sinks is not None:
        denom = denom + jnp.exp(sink - m)
    out = jnp.einsum('bsngrqk,bsnkgd->bsnqgrd', p, vv.astype(jnp.float32))
    denom_t = jnp.moveaxis(denom, -1, 3)
    out = (out / denom_t[..., None]).reshape(b, s, lp, hq, hd)[:, :, :l]
    lse = (jnp.moveaxis(m, -1, 3) + jnp.log(denom_t)).reshape(b, s, lp, hq)[:, :, :l]
    return out.astype(q.dtype), lse

def dilated_attention(q, k, v):
    b, t = q.shape[:2]
    slopes = alibi_slopes(DIL_HEADS)
    outs, lses = [], []
    for gi, (window, dil) in enumerate(DIL_PATTERNS):
        lo, hi = gi * DIL_HEADS_PER_GROUP, (gi + 1) * DIL_HEADS_PER_GROUP
        l = t // dil

        def to_streams(z):
            return z[:, :, lo:hi].reshape(b, l, dil, DIL_HEADS_PER_GROUP, HEAD_DIM).transpose(0, 2, 1, 3, 4)

        o, lse = banded_attention(to_streams(q), to_streams(k), to_streams(v),
                                  slopes[lo:hi], window // dil, dil)
        outs.append(o.transpose(0, 2, 1, 3, 4).reshape(b, t, DIL_HEADS_PER_GROUP, HEAD_DIM))
        lses.append(lse.transpose(0, 2, 1, 3).reshape(b, t, DIL_HEADS_PER_GROUP))
    alpha = jax.nn.softmax(jnp.stack(lses, axis=2), axis=2)
    y = jnp.einsum('btgh,btghd->bthd', alpha.astype(q.dtype), jnp.stack(outs, axis=2))
    return y.reshape(b, t, DIL_MERGED)

def swa_sink_attention(q, k, v, sinks):
    b, t = q.shape[:2]
    out, _ = banded_attention(q[:, None], k[:, None], v[:, None], alibi_slopes(SWA_Q_HEADS),
                              SWA_WINDOW - 1, 1, sinks=sinks)
    return out[:, 0].reshape(b, t, SWA_Q_WIDTH)

def hier_moe(h, w_group, b_group, w_router, b_router, w_e_gate, w_e_up, w_e_down):
    b, t, d = h.shape
    hf = h.reshape(b * t, d)
    g_logits = (hf @ w_group).astype(jnp.float32) + b_group.astype(jnp.float32)
    g_probs = jax.nn.softmax(g_logits, axis=-1)
    g_top = jnp.argmax(g_logits, axis=-1)
    g_w = jnp.take_along_axis(g_probs, g_top[:, None], axis=1)
    e_logits = ((hf @ w_router).astype(jnp.float32) + b_router.astype(jnp.float32)).reshape(
        -1, MOE_GROUPS, EXPERTS_PER_GROUP)
    e_logits = jnp.take_along_axis(e_logits, g_top[:, None, None], axis=1)[:, 0]
    e_w, e_idx = lax.top_k(jax.nn.softmax(e_logits, axis=-1), TOP_K)
    e_w = e_w / e_w.sum(axis=-1, keepdims=True)
    ids = g_top[:, None] * EXPERTS_PER_GROUP + e_idx
    gates = jnp.einsum('nk,nke->ne', g_w * e_w, jax.nn.one_hot(ids, N_EXPERTS, dtype=jnp.float32))
    out = jnp.zeros_like(hf)
    for e in range(N_EXPERTS):
        a = jax.nn.silu(hf @ w_e_gate[e]) * (hf @ w_e_up[e])
        out = out + gates[:, e:e + 1].astype(hf.dtype) * (a @ w_e_down[e])
    return out.reshape(b, t, d)

def second_inputs(seed: int = 0) -> dict:
    key = jax.random.key(seed)
    ks = jax.random.split(key, 20)
    f32 = jnp.float32

    def nrm(k, shape, fan_in):
        return jax.random.normal(k, shape, f32) * (fan_in ** -0.5)

    return {
        'x': jax.random.normal(ks[0], (BATCH, SEQ, D_MODEL), f32),
        'g_mix': 1.0 + 0.05 * jax.random.normal(ks[1], (DEPTH_2, D_MODEL), f32),
        'w_in': nrm(ks[2], (DEPTH_2, D_MODEL, IN_WIDTH), D_MODEL),
        'sinks': jax.random.normal(ks[3], (DEPTH_2, SWA_Q_HEADS), f32),
        'w_br_dil': nrm(ks[4], (DEPTH_2, DIL_MERGED, D_MODEL), DIL_MERGED),
        'w_br_swa': nrm(ks[5], (DEPTH_2, SWA_Q_WIDTH, D_MODEL), SWA_Q_WIDTH),
        'w_out': nrm(ks[6], (DEPTH_2, D_MODEL, D_MODEL), D_MODEL),
        'g_ffn': 1.0 + 0.05 * jax.random.normal(ks[7], (DEPTH_2, D_MODEL), f32),
        'w_group': nrm(ks[8], (DEPTH_2, D_MODEL, MOE_GROUPS), D_MODEL),
        'b_group': 0.01 * jax.random.normal(ks[9], (DEPTH_2, MOE_GROUPS), f32),
        'w_router': nrm(ks[10], (DEPTH_2, D_MODEL, N_EXPERTS), D_MODEL),
        'b_router': 0.01 * jax.random.normal(ks[11], (DEPTH_2, N_EXPERTS), f32),
        'w_e_gate': nrm(ks[12], (DEPTH_2, N_EXPERTS, D_MODEL, D_EXPERT), D_MODEL),
        'w_e_up': nrm(ks[13], (DEPTH_2, N_EXPERTS, D_MODEL, D_EXPERT), D_MODEL),
        'w_e_down': nrm(ks[14], (DEPTH_2, N_EXPERTS, D_EXPERT, D_MODEL), D_EXPERT),
        'g_final': 1.0 + 0.05 * jax.random.normal(ks[15], (D_MODEL,), f32),
    }

def second_block(x, g_mix, w_in, sinks, w_br_dil, w_br_swa, w_out, g_ffn, w_group, b_group,
              w_router, b_router, w_e_gate, w_e_up, w_e_down, g_final):
    b, t, _ = x.shape
    for l in range(DEPTH_2):
        h = rmsnorm(x, g_mix[l])
        proj = h @ w_in[l]
        q_d, k_d, v_d, q_s, k_s, v_s, gate_d, gate_s = split_cols(proj, IN_WIDTHS)
        y_dil = dilated_attention(q_d.reshape(b, t, DIL_HEADS, HEAD_DIM),
                                  k_d.reshape(b, t, DIL_HEADS, HEAD_DIM),
                                  v_d.reshape(b, t, DIL_HEADS, HEAD_DIM))
        y_swa = swa_sink_attention(q_s.reshape(b, t, SWA_Q_HEADS, HEAD_DIM),
                                   k_s.reshape(b, t, SWA_KV_HEADS, HEAD_DIM),
                                   v_s.reshape(b, t, SWA_KV_HEADS, HEAD_DIM), sinks[l])
        mixed = (jax.nn.sigmoid(gate_d) * (y_dil @ w_br_dil[l])
                 + jax.nn.sigmoid(gate_s) * (y_swa @ w_br_swa[l]))
        x = x + mixed @ w_out[l]
        x = x + hier_moe(rmsnorm(x, g_ffn[l]), w_group[l], b_group[l], w_router[l], b_router[l],
                         w_e_gate[l], w_e_up[l], w_e_down[l])
    return rmsnorm(x, g_final)


def setup_inputs(seed=0):
    out = dict(first_inputs(seed))
    for name, value in second_inputs(seed + 1).items():
        if name != "x":
            out[name + "_2"] = value
    return out


def reference(
    x, mem, ab_norm, ab_w_in, a_conv_w, a_conv_b, a_gate_x_w, a_gate_x_b, a_gate_a_w,
    a_gate_a_b, a_lambda, b_group_w, b_group_b, b_scale, ab_w_out, c_norm, c_w_pw1, c_b_pw1,
    c_dw_w, c_dw_b, c_ln_g, c_ln_b, c_w_pw2, c_b_pw2, xa_norm, xa_mem_norm, xa_wq, xa_wk, xa_wv,
    xa_wo, f_norm, f_w_up, f_dw_w, f_dw_b, f_w_down, final_norm, g_mix_2, w_in_2, sinks_2,
    w_br_dil_2, w_br_swa_2, w_out_2, g_ffn_2, w_group_2, b_group_2, w_router_2, b_router_2,
    w_e_gate_2, w_e_up_2, w_e_down_2, g_final_2,
):
    x = first_block(
        x, mem, ab_norm, ab_w_in, a_conv_w, a_conv_b, a_gate_x_w, a_gate_x_b, a_gate_a_w,
        a_gate_a_b, a_lambda, b_group_w, b_group_b, b_scale, ab_w_out, c_norm, c_w_pw1, c_b_pw1,
        c_dw_w, c_dw_b, c_ln_g, c_ln_b, c_w_pw2, c_b_pw2, xa_norm, xa_mem_norm, xa_wq, xa_wk,
        xa_wv, xa_wo, f_norm, f_w_up, f_dw_w, f_dw_b, f_w_down, final_norm,
    )
    return second_block(
        x, g_mix_2, w_in_2, sinks_2, w_br_dil_2, w_br_swa_2, w_out_2, g_ffn_2, w_group_2,
        b_group_2, w_router_2, b_router_2, w_e_gate_2, w_e_up_2, w_e_down_2, g_final_2,
    )


_drawn_inputs = setup_inputs


def setup_inputs(seed=0):
    import zlib

    import numpy as np

    out = dict(_drawn_inputs(seed))
    spreads = {}
    factors = {'a_gate_x_b': 8.0,
     'a_gate_a_b': 8.0,
     'c_norm': 8.501,
     'c_b_pw1': 14.597,
     'c_ln_b': 7.907,
     'c_b_pw2': 2.7,
     'xa_norm': 8.0,
     'xa_mem_norm': 6.512,
     'f_dw_b': 8.106,
     'b_group_2': 8.0,
     'b_router_2': 2.939,
     'c_dw_b': 8.0,
     'c_ln_g': 3.129}
    for name, (base, spread) in spreads.items():
        noise = np.random.default_rng([zlib.crc32(name.encode()), seed]).standard_normal(out[name].shape)
        drawn = base * np.exp(spread * noise) if base else spread * noise
        out[name] = __import__('jax').numpy.asarray(drawn.astype(out[name].dtype))
    for name, factor in factors.items():
        out[name] = (out[name] * factor).astype(out[name].dtype)
    return out
```

```python
from contextlib import ExitStack, contextmanager

import numpy as np

import concourse.bass as bass
from concourse import mybir

F32 = mybir.dt.float32
F32R = mybir.dt.float32r
ACT = mybir.ActivationFunctionType
ALU = mybir.AluOpType
AX = mybir.AxisListType

P = 128
T = 256
TT = T // P
D = 1024
KC = D // P
SLAB = 1024
EPS = 1e-6
NEG = -1e30
FF = 3 * D
FJ = FF // P
NE = 32
DE = 512
MJ = NE * DE // P
CONV_A, CONV_C, CONV_F = 4, 31, 3
XH = 4
POOLS = (2, 4, 8, 16)
RAW = 12
SPLIT = 4
AHEAD = 3
SLOPES_DIL = [2.0 ** (-8.0 * (h + 1) / 24) for h in range(24)]
SLOPES_SWA = [2.0 ** (-8.0 * (h + 1) / 16) for h in range(16)]

PHASES = [("abin", 20), ("k0", 8), ("gates", 4), ("v0", 8), ("about", 12), ("q0", 8), ("wo0", 8),
          ("f0", 3 * FJ), ("pw1", 16), ("k1", 8), ("v1", 8), ("pw2", 8), ("q1", 8), ("wo1", 8),
          ("f1", 3 * FJ), ("win", 62), ("brd", 4), ("brs", 8), ("wout", 8), ("moe", 3 * MJ)]
S0, _n = {}, 0
for _name, _k in PHASES:
    S0[_name] = _n
    _n += _k
NSLAB = _n

COLS = [("ab_norm", 8), ("a_conv_w", 8 * CONV_A), ("a_conv_b", 8), ("a_gate_x_b", 8), ("a_gate_a_b", 8),
        ("a_lambda", 8), ("b_group_b", 4), ("b_scale", 4), ("c_norm", 8), ("c_b_pw1", 16),
        ("c_dw_w", 8 * CONV_C), ("c_dw_b", 8), ("c_ln_g", 8), ("c_ln_b", 8), ("c_b_pw2", 8),
        ("xa_norm0", 8), ("xa_norm1", 8), ("mem_norm0", 8), ("mem_norm1", 8), ("f_norm0", 8), ("f_norm1", 8),
        ("f_dw_w0", FJ * CONV_F), ("f_dw_w1", FJ * CONV_F), ("f_dw_b0", FJ), ("f_dw_b1", FJ),
        ("final_norm", 8), ("g_mix", 8), ("g_ffn", 8), ("g_final", 8), ("sinks", 16), ("r_bias", 36)]
C0, _n = {}, 0
for _name, _k in COLS:
    C0[_name] = _n
    _n += _k
NCOL = _n

USES, USE0 = [], {}


def _uses(name, who):
    USE0[name] = len(USES)
    USES.extend(who)


def _attn_uses(n):
    out = []
    for h in range(n + 1):
        if h < n:
            out += ["a", "a"]
        if h >= 1:
            out += ["a", "a", "v"]
    return out


HEADS2 = [("d", h) for h in range(8)] + [("s", h) for h in range(16)]


def groups(kind):
    return 3 if kind == "d" else 1


def _attn2_uses():
    out = []
    for n in range(len(HEADS2) + 1):
        if n < len(HEADS2):
            out += ["v"] * (2 * groups(HEADS2[n][0]))
        if n >= 1:
            out += ["a"] * groups(HEADS2[n - 1][0]) + ["v"]
    return out


_uses("abin", "v" * 20)
_uses("k0", "v" * 8)
_uses("gates", "aav" * 4)
_uses("v0", "v" * 4)
_uses("q0", "v" * 8)
_uses("x0", _attn_uses(XH))
_uses("f0", "vv" * FJ)
_uses("pw1", "v" * 16)
_uses("k1", "v" * 8)
_uses("v1", "v" * 4)
_uses("q1", "v" * 8)
_uses("x1", _attn_uses(XH))
_uses("f1", "vv" * FJ)
_uses("win", "v" * (32 + 6 + 3 + 16))
_uses("attn2", _attn2_uses())
_uses("gb", "a" * NE)
_uses("moe", "av" * MJ)


def emptied(u, who=None):
    who = who or USES[u]
    return sum(1 for w in USES[:u + 1] if w == who)


MM0 = {}
_n = 0
for _name, _k in (("x0", len(_attn_uses(XH))), ("x1", len(_attn_uses(XH))), ("attn2", len(_attn2_uses())),
                 ("gb", NE)):
    MM0[_name] = _n
    _n += _k

NORMS = {n: i for i, n in enumerate(
    ["ab", "mem", "xa0", "f0", "c", "lnmean", "ln", "xa1", "f1", "final", "mix", "moe", "out"])}
PAIRS = {n: i for i, n in enumerate(["abin", "q0", "f0", "pw1", "q1", "f1", "win", "moe"])}
ACCS = {n: i for i, n in enumerate(["about", "wo0", "f0", "pw2", "wo1", "f1", "brd", "brs", "wout", "moe"])}

KB = 1024
MAP = [("raw", 48), ("wh", 16), ("wl", 16), ("x", 8), ("ah", 8), ("al", 8), ("mh", 8), ("ml", 8),
       ("yh", 12), ("yl", 12), ("arena", 46), ("konst", 6.5), ("cols", 3.25), ("tmp", 7), ("memr", 1)]
OFF, _o = {}, 0
for _name, _k in MAP:
    OFF[_name] = _o
    _o += int(_k * KB)


def glu_slab(base, J, kind, j):
    if kind == "d":
        return base + (6 + 3 * j if j <= J - 3 else 3 * J - (J - j))
    g = 2 * j if j < 2 else 4 + 3 * (j - 2)
    return base + g + (kind == "u")


class At:

    def __init__(self, base, step=0, i=None):
        self.base, self.step, self.i = base, step, i

    def __add__(self, k):
        return At(self.base + k, self.step, self.i)

    def of(self, f):
        a = f(self.base)
        if self.i is None:
            return a
        return self.i * (f(self.base + self.step) - a) + a


class Program:

    def __init__(self, eng, chain):
        self.eng, self.chain, self.count, self.last = eng, chain, {}, None

    def done(self, ins, sem=None):
        sem = self.chain if sem is None else sem
        if self.last is not None:
            self.before = (self.last, self.count[self.last.name])
        ins.then_inc(sem, 1)
        base, k = self.count.get(sem.name, (None, 0))
        self.count[sem.name] = (base, k + 1)
        self.last = sem

    def fence(self, back=0):
        if self.last is not None:
            sem, (base, k) = self.before if back else (self.last, self.count[self.last.name])
            self.eng.wait_ge(sem, k if base is None else base + k)

    @contextmanager
    def loop(self, trips, raised, last):
        self.fence()
        before = {s.name: self.count[s.name][1] for s in raised}
        with self.eng.Fori(0, trips) as i:
            for s, k in raised.items():
                self.count[s.name] = (i * k + before[s.name], 0)
            self.last = last
            yield i
            for s, k in raised.items():
                assert self.count[s.name][1] == k, (s.name, self.count[s.name][1], k)
        for s, k in raised.items():
            self.count[s.name] = (None, before[s.name] + k * trips)
        self.last = last


def program(nc, stream, cols_in, konst_in, masks_in, x_in, mem_in, router_in, out):
    ctx = ExitStack()
    with ctx:
        first_free = (nc.sbuf_base + 63) // 64 * 64

        def sb(name, where, at_kb, shape, dt=F32):
            return nc.alloc_sbuf_tensor_at(name, shape, dt, offset=first_free + OFF[where] + int(at_kb * KB))

        sems = {}

        def S(name):
            if name not in sems:
                sems[name] = ctx.enter_context(nc.semaphore(name))
            return sems[name]

        raw = sb("raw", "raw", 0, [P, RAW, SLAB])
        wh = sb("wh", "wh", 0, [P, SPLIT, SLAB], F32R)
        wl = sb("wl", "wl", 0, [P, SPLIT, SLAB], F32R)
        x = sb("x_res", "x", 0, [P, KC, T])
        ah = sb("ah", "ah", 0, [P, KC, T], F32R)
        al = sb("al", "al", 0, [P, KC, T], F32R)
        mh = sb("mh", "mh", 0, [P, KC, T], F32R)
        ml = sb("ml", "ml", 0, [P, KC, T], F32R)
        yh = sb("yh", "yh", 0, [P, 12, T], F32R)
        yl = sb("yl", "yl", 0, [P, 12, T], F32R)
        mem = sb("mem_t", "yh", 4, [P, KC, T])
        cols = sb("cols", "cols", 0, [P, NCOL])
        ident = sb("ident", "konst", 0, [P, P])
        inv = sb("inv_count", "konst", 0.5, [P, 4, T])
        masks = sb("masks", "konst", 0.5, [P, 4, 3 * P])
        q_t = sb("q_t", "arena", 0, [P, KC, T])
        sq = sb("sq", "arena", 0, [P, KC, T])
        k_t = sb("k_t", "arena", 8, [P, KC, T])
        v_m = sb("v_m", "arena", 16, [P, TT, D])
        z = sb("z", "arena", 24, [P, 20, T])
        xr = sb("xr", "ah", 0, [P, KC, T])
        a_t = sb("a_t", "al", 0, [P, KC, T])
        pt = sb("pt", "arena", 24, [P, 2, TT, T])
        prob = sb("prob", "arena", 28, [P, 2, TT, T])
        hpad = sb("hpad", "arena", 24, [P, KC, T + CONV_C - 1])
        cv = sb("cv", "arena", 34, [P, KC, T])
        gpad = sb("gpad", "arena", 24, [P, 2, T + 2])
        cf = sb("cf", "arena", 27, [P, 2, T])
        uf = sb("uf", "arena", 29, [P, 2, T])
        hid = sb("hid", "arena", 31, [P, 2, T])
        q2 = sb("q2", "arena", 0, [P, 20, T])
        k2 = sb("k2", "arena", 20, [P, 13, T])
        v2 = sb("v2", "arena", 33, [P, TT, 1664])
        gt = sb("gt", "mh", 0, [P, 16, T])
        sc = sb("sc", "ah", 0, [P, 2, 9 * P])
        pt2 = sb("pt2", "ah", 9, [P, 3, 3 * P])
        gates_b = sb("gates_b", "arena", 0, [P, NE, T])
        silu = sb("silu", "arena", 33, [P, 2, T])
        hidm = sb("hidm", "arena", 35, [P, 2, T])
        hf = sb("hf", "arena", 37, [P, KC, T])
        rw = sb("router_w", "konst", 0.5, [P, KC, 36])
        gate_rows = sb("gate_rows", "konst", 2, [NE, T])
        gate_row = sb("gate_row", "konst", 3, [NE, 2, T])
        lg = sb("logits", "konst", 5, [P, TT, 36])
        rt = sb("router_tmp", "konst", 5.5, [P, 96])
        ones = sb("ones", "tmp", 0, [P, P])
        t = [sb(f"t{n}", "tmp", 0.5 + n, [P, T]) for n in range(5)]
        diag = sb("diag", "tmp", 4.5, [P, TT, P])
        rstd_b = sb("rstd_b", "tmp", 5.5, [P, T])
        sm = sb("small", "tmp", 6.5, [P, 128])
        ms, rcol, mhalf = sm[:, 0:2], sm[:, 2:4], sm[:, 4:6]
        nmax, den, rec, esink = sm[:, 6:8], sm[:, 8:10], sm[:, 10:12], sm[:, 12:14]
        sp8, n4sp, p4sp, hbx, hba, hbc = (sm[:, 16 + 8 * n:24 + 8 * n] for n in range(6))
        nsink = sm[:, 64:80]
        lam_a, lam_e, lam_z, lam_q = (sm[:, 80 + 8 * n:88 + 8 * n] for n in range(4))

        mem_rstd = sb("mem_rstd", "memr", 0, [P, T])

        pw = [ctx.enter_context(nc.psum_tensor(f"pw{n}", [P, 512], F32)) for n in range(4)]
        acc = [ctx.enter_context(nc.psum_tensor(f"acc{n}", [P, 512], F32)) for n in range(4)]

        def acc_of(n):
            return acc[n // 2][:, (n % 2) * T:(n % 2) * T + T]

        def col(name, n=0, step=0, i=None):
            if i is None:
                return cols[:, C0[name] + n:C0[name] + n + 1]
            return cols[:, bass.ds(i * step + (C0[name] + n), 1)]

        raw_in = [S(f"raw_in{n}") for n in range(RAW)]
        w_hi, w_lo_v, w_lo_p = S("w_hi"), S("w_lo_vector"), S("w_lo_pool")
        slab_done, mm_done = S("slab_done"), S("products_done")
        empty_v, empty_a = S("bank_emptied_vector"), S("bank_emptied_scalar")
        acc_full, acc_out = S("sum_full"), S("sum_taken")
        sq_ready, stat_full, ms_ready = S("squares"), S("sums_full"), S("mean_square")
        rstd_ready, diag_ready, bc_full = S("rstd_column"), S("diagonal"), S("spread_full")
        rstd_b_ready = S("rstd_spread")
        pair_hi, pair_lo = S("a_hi"), S("a_lo")
        block = ctx.enter_context(nc.Block())

        def wait_split(eng, s):
            if s.base % 2 == 0:
                eng.wait_ge(w_lo_v, s.of(lambda n: n // 2 + 1))
            else:
                eng.wait_ge(w_lo_p, s.of(lambda n: (n + 1) // 2))

        def wait_slab(eng, s):
            eng.wait_ge(slab_done, s.of(lambda n: n + 1))

        def wait_emptied(eng, u):
            eng.wait_ge(empty_v if USES[u] == "v" else empty_a, emptied(u))

        def wait_acc(eng, phase, n):
            n |= 1
            if n < KC - 1:
                eng.wait_ge(acc_full, (KC - 1) * ACCS[phase] + n + 1)
            else:
                wait_slab(eng, At(S0[phase] + dict(PHASES)[phase] - 1))

        def wait_new_x(eng, phase, c):
            eng.wait_ge(acc_out, KC * ACCS[phase] + c + 1)

        def glu_steps(J):
            trips = (J - 6) // 4
            return trips, 4 + 4 * trips

        @block.sync
        def _(sp):
            def load(s):
                b = s.base
                if b >= RAW:
                    wait_split(sp, s + -RAW)
                src = stream[b] if s.i is None else \
                    stream[bass.ds(s.i * s.step + b, 1), :, :].rearrange("a p n -> (a p) n")
                sp.dma_start(raw[:, b % RAW, :], src).then_inc(raw_in[b % RAW], 16)

            for s in range(2 * RAW):
                load(At(s))
            trips = NSLAB // RAW - 2
            with sp.Fori(0, trips) as i:
                for j in range(RAW):
                    load(At(2 * RAW + j, RAW, i))
            for s in range(RAW * (trips + 2), NSLAB):
                load(At(s))
            sp.wait_ge(S("x_final"), KC)
            sp.dma_start(out, x[:]).then_inc(S("out_done"), 16)
            sp.wait_ge(S("out_done"), 16)

        @block.scalar
        def _(act):
            A = Program(act, S("scalar_chain"))

            def split(s):
                if s.base >= NSLAB:
                    return
                act.wait_ge(raw_in[s.base % RAW], s.of(lambda n: 16 * (n // RAW + 1)))
                if s.base >= SPLIT:
                    wait_slab(act, s + -SPLIT)
                A.done(act.activation(wh[:, s.base % SPLIT, :], raw[:, s.base % RAW, :], ACT.Copy), w_hi)

            def squares(src, ready, gain=None, name=None):
                for c in range(KC):
                    ready(c)
                    A.done(act.activation(sq[:, c, :], src[:, c, :], ACT.Square), sq_ready)
                    if gain is not None:
                        A.done(act.activation(ah[:, c, :], src[:, c, :], ACT.Copy, scale=col(gain, c)), pair_hi)

            act.dma_start(x[:], x_in).then_inc(S("x_in"), 16)
            act.dma_start(cols[:], cols_in).then_inc(S("const_in"), 16)
            act.dma_start(ident[:], konst_in[:, 0:P]).then_inc(S("const_in"), 16)
            act.dma_start(inv[:], konst_in[:, P:P + 4 * T].rearrange("p (g t) -> p g t", g=4)) \
                .then_inc(S("const_in"), 16)
            act.dma_start(mem[:], mem_in).then_inc(S("mem_in"), 16)
            act.wait_ge(S("const_in"), 48)
            act.wait_ge(S("x_in"), 16)
            squares(x, lambda c: None, "ab_norm")
            for s in range(AHEAD):
                split(At(s))
            act.wait_ge(S("mem_in"), 16)
            act.wait_ge(stat_full, 1)
            squares(mem, lambda c: None)
            A.done(act.activation(lam_a, cols[:, C0["a_lambda"]:C0["a_lambda"] + 8], ACT.Abs), S("decay_abs"))
            A.fence()
            A.done(act.activation(lam_e, lam_a, ACT.Exp, scale=-1.0), S("decay_exp"))

            def mem_pair(l):
                for c in range(KC):
                    act.wait_ge(S("mem_normed"), KC * l + c + 1)
                    A.done(act.activation(mh[:, c, :], mem[:, c, :], ACT.Copy, scale=col(f"mem_norm{l}", c)),
                           S("m_hi"))

            for n in range(20):
                split(At(S0["abin"] + n + AHEAD))
                if n == 9:
                    mem_pair(0)
                if 10 <= n < 18:
                    wait_emptied(act, USE0["abin"] + n - 10)
                    A.done(act.activation(z[:, n - 10, :], z[:, n - 10, :], ACT.Gelu_apprx_tanh), S("gate_gelu"))
            for n in range(8):
                split(At(S0["k0"] + n + AHEAD))
                act.wait_ge(S("xr_ready"), n + 1)
                A.done(act.activation(yh[:, n, :], xr[:, n, :], ACT.Copy), S("xr_hi"))
                if n >= 4:
                    act.wait_ge(S("pooled"), n - 3)
                    A.done(act.activation(yh[:, 4 + n, :], z[:, 12 + n, :], ACT.Copy), S("pooled_hi"))
            act.wait_ge(S("decay"), 1)
            for n in range(4):
                split(At(S0["gates"] + n + AHEAD))
                for h in (2 * n, 2 * n + 1):
                    u = USE0["gates"] + 3 * n + h % 2
                    act.wait_ge(S("gate_products"), h + 1)
                    if h >= 2:
                        act.wait_ge(S("root_in"), h - 1)
                    A.fence()
                    A.done(act.activation(t[h % 2][:], pw[u % 4][:, 0:T], ACT.Tanh, bias=hbx[:, h:h + 1], scale=0.5))
                    A.done(act.activation(t[2 + h % 2][:], pw[u % 4][:, T:2 * T], ACT.Tanh, bias=hba[:, h:h + 1],
                                          scale=0.5), empty_a)
                    A.fence()
                    A.done(act.activation(a_t[:, h, :], t[2 + h % 2][:], ACT.Exp, bias=n4sp[:, h:h + 1],
                                          scale=n4sp[:, h:h + 1]))
                    A.done(act.activation(z[:, 8 + h, :], t[2 + h % 2][:], ACT.Tanh, bias=p4sp[:, h:h + 1],
                                          scale=p4sp[:, h:h + 1]), S("gates_through"))
                wait_emptied(act, USE0["gates"] + 3 * n + 2)
                A.done(act.activation(yh[:, 8 + n, :], z[:, 16 + n, :], ACT.Copy), S("yb_hi"))
            act.wait_ge(S("root_in"), 8)
            A.done(act.activation(z[:, 8:16, :], z[:, 8:16, :], ACT.Sqrt, scale=0.25), S("root"))
            for n in range(8):
                split(At(S0["v0"] + n + AHEAD))
                act.wait_ge(S("ya_ready"), n + 1)
                A.done(act.activation(yh[:, n, :], xr[:, n, :], ACT.Copy), S("ya_hi"))
            act.dma_start(masks[:], masks_in).then_inc(S("masks_in"), 16)

            def row_splits(phase):
                for n in range(dict(PHASES)[phase]):
                    split(At(S0[phase] + n + AHEAD))

            def cross(l):
                name, n_u = f"x{l}", USE0[f"x{l}"]
                for h in range(XH + 1):
                    if h < XH:
                        for qt in range(TT):
                            r, b = 2 * h + qt, pw[(n_u + x_score(h) + qt) % 4]
                            act.wait_ge(S(name + "_max"), r + 1)
                            A.done(act.activation(prob[:, h % 2, qt, :], b[:, 0:T], ACT.Exp,
                                                  bias=nmax[:, qt:qt + 1], accum_out=den[:, qt:qt + 1]), empty_a)
                    if h >= 1:
                        for qt in range(TT):
                            k = x_turn(h - 1) + qt
                            act.wait_ge(mm_done, MM0[name] + k + 1)
                            A.done(act.activation(pt[:, (h - 1) % 2, :, qt * P:qt * P + P],
                                                  pw[(n_u + k) % 4][:, 0:T].rearrange("p (a q) -> p a q", a=TT),
                                                  ACT.Copy), empty_a)
                        k = x_turn(h - 1) + 2
                        act.wait_ge(mm_done, MM0[name] + k + 1)
                        A.done(act.activation(yh[:, 2 * h - 2:2 * h, :],
                                              pw[(n_u + k) % 4][:, :].rearrange("p (a q) -> p a q", a=2),
                                              ACT.Copy), S(name + "_hi"))

            def glu(name, J):
                base, moe = S0[name], name == "moe"

                def step(j, i=None):
                    def slab(kind):
                        return At(glu_slab(base, J, kind, j), 12 if i is not None else 0, i)
                    jj = At(j, 4 if i is not None else 0, i)
                    split(slab("g") + AHEAD)
                    if moe:
                        wait_slab(act, slab("g"))
                        if j >= 2:
                            act.wait_ge(empty_v, (jj + -1).of(lambda n: emptied(USE0[name] - 1, "v") + n))
                        A.done(act.activation(silu[:, j % 2, :], pw[(USE0[name] + 2 * j) % 4][:, 0:T], ACT.Silu),
                               empty_a)
                    split(slab("u") + AHEAD)
                    if not moe:
                        act.wait_ge(S(name + "_conv"), (jj + 1).of(lambda n: n))
                        A.done(act.activation(cf[:, j % 2, :], cf[:, j % 2, :], ACT.Gelu_apprx_tanh),
                               S(name + "_act"))
                    if j >= 2:
                        split(At(slab("u").base + 1 + AHEAD, 12 if i is not None else 0, i))
                    act.wait_ge(S(name + "_hidden"), (jj + 1).of(lambda n: n))
                    src = (hidm if moe else hid)
                    A.done(act.activation(yh[:, j % 4, :], src[:, j % 2, :], ACT.Copy), S(name + "_hid_hi"))

                trips, rest = glu_steps(J)
                for j in range(4):
                    step(j)
                raised = {w_hi: 12, S(name + "_hid_hi"): 4}
                raised[empty_a if moe else S(name + "_act")] = 4
                with A.loop(trips, raised, S(name + "_hid_hi")) as i:
                    for j in range(4, 8):
                        step(j, i)
                for j in range(rest, J):
                    step(j)
                for n in range(2):
                    split(At(base + 3 * J - 2 + n + AHEAD))

            row_splits("about")
            squares(x, lambda c: wait_new_x(act, "about", c), "xa_norm0")
            row_splits("q0")
            cross(0)
            row_splits("wo0")
            squares(x, lambda c: wait_new_x(act, "wo0", c), "f_norm0")
            act.dma_start(mem[:], mem_in).then_inc(S("mem_again"), 16)
            glu("f0", FJ)
            squares(x, lambda c: wait_new_x(act, "f0", c), "c_norm")
            def glu_tanh(c):
                wait_emptied(act, USE0["pw1"] + 2 * c + 1)
                tb = t[2 * (c % 2) + 1][:]
                A.done(act.activation(tb, tb, ACT.Tanh, bias=hbc[:, c:c + 1], scale=0.5), S("glu_tanh"))

            for n in range(16):
                split(At(S0["pw1"] + n + AHEAD))
                if n % 2 == 0 and n >= 2:
                    glu_tanh(n // 2 - 1)
                if n == 10:
                    mem_pair(1)
            glu_tanh(7)
            row_splits("k1")
            row_splits("v1")
            squares(cv, lambda c: act.wait_ge(S("ln_centred"), c + 1))
            for c in range(KC):
                act.wait_ge(S("ln_scaled"), c + 1)
                A.done(act.activation(cv[:, c, :], cv[:, c, :], ACT.Silu, bias=col("c_ln_b", c),
                                      scale=col("c_ln_g", c)), S("ln_silu"))
                A.fence()
                A.done(act.activation(yh[:, c, :], cv[:, c, :], ACT.Copy), S("ln_hi"))
            row_splits("pw2")
            squares(x, lambda c: wait_new_x(act, "pw2", c), "xa_norm1")
            row_splits("q1")
            cross(1)
            row_splits("wo1")
            squares(x, lambda c: wait_new_x(act, "wo1", c), "f_norm1")
            glu("f1", FJ)
            squares(x, lambda c: wait_new_x(act, "f1", c))
            squares(x, lambda c: act.wait_ge(S("x_normed"), c + 1), "g_mix")
            for n in range(62):
                split(At(S0["win"] + n + AHEAD))
                if n >= 46:
                    wait_emptied(act, USE0["win"] + n - 46 + 41)
                    A.done(act.activation(gt[:, n - 46, :], gt[:, n - 46, :], ACT.Tanh, scale=0.5), S("mix_gates"))
            for m in range(len(HEADS2) + 1):
                if m < len(HEADS2):
                    kind, h = HEADS2[m]
                    for qt in range(TT):
                        at, n = (0, P) if qt == 0 else (3 * P, 2 * P)
                        act.wait_ge(S("attn2_max"), 2 * m + qt + 1)
                        s_ap = sc[:, m % 2, at:at + n * groups(kind)]
                        A.fence()
                        if kind == "s":
                            A.done(act.activation(esink[:, qt:qt + 1], col("sinks", h), ACT.Exp,
                                                  bias=nmax[:, qt:qt + 1]))
                        A.done(act.activation(s_ap, s_ap, ACT.Exp, bias=nmax[:, qt:qt + 1],
                                              accum_out=den[:, qt:qt + 1]), S("attn2_exp"))
                if m >= 1:
                    kind, h = HEADS2[m - 1]
                    for g in range(groups(kind)):
                        k = a_turn(m - 1) + g
                        act.wait_ge(mm_done, MM0["attn2"] + k + 1)
                        A.done(act.activation(pt2[:, g, :], pw[(USE0["attn2"] + k) % 4][:, 0:3 * P], ACT.Copy),
                               empty_a)
                    k = a_turn(m - 1) + groups(kind)
                    c, half = mixed_at(kind, h)
                    act.wait_ge(mm_done, MM0["attn2"] + k + 1)
                    A.done(act.activation(yh[half:half + 64, c, :], pw[(USE0["attn2"] + k) % 4][half:half + 64, 0:T],
                                          ACT.Copy), S("attn2_hi"))
            act.dma_start(rw[:], router_in).then_inc(S("router_in"), 16)
            row_splits("brd")
            row_splits("brs")
            for c in range(KC):
                act.wait_ge(S("mixed"), c + 1)
                A.done(act.activation(yh[:, c, :], gt[:, c, :], ACT.Copy, scale=0.5), S("mixed_hi"))
            row_splits("wout")
            squares(x, lambda c: wait_new_x(act, "wout", c))
            for c in range(KC):
                act.wait_ge(S("h_ready"), c + 1)
                A.done(act.activation(ah[:, c, :], hf[:, c, :], ACT.Copy), pair_hi)
            for q in range(TT):
                act.wait_ge(S("group_max"), q + 1)
                A.fence()
                A.done(act.activation(rt[:, 4:8], lg[:, q, 0:4], ACT.Exp, bias=rt[:, 0:1], accum_out=rt[:, 1:2]),
                       S("group_exp"))
                act.wait_ge(S("expert_gap"), q + 1)
                A.done(act.activation(rt[:, 2:3], rt[:, 3:4], ACT.Exp), S("expert_exp"))
            for e in range(NE):
                act.wait_ge(mm_done, MM0["gb"] + e + 1)
                A.done(act.activation(gates_b[:, e, :], pw[(USE0["gb"] + e) % 4][:, 0:T], ACT.Copy), empty_a)
            glu("moe", MJ)
            squares(x, lambda c: wait_new_x(act, "moe", c))

        @block.gpsimd
        def _(pool):
            G = Program(pool, S("pool_chain"))

            def split(s):
                if s.base >= NSLAB or s.base % 2 == 0:
                    return
                pool.wait_ge(w_hi, s.of(lambda n: n + 1))
                G.done(pool.tensor_tensor(wl[:, s.base % SPLIT, :], raw[:, s.base % RAW, :],
                                          wh[:, s.base % SPLIT, :].bitcast(F32), ALU.subtract), w_lo_p)

            def splits(s, n):
                for k in range(n):
                    split(At(s + k + AHEAD))

            def rstd(name, mean=False):
                pool.wait_ge(ms_ready, NORMS[name] + 1)
                G.fence()
                if mean:
                    G.done(pool.tensor_copy(rcol, ms), rstd_ready)
                else:
                    G.done(pool.tensor_tensor(rcol, ms, mhalf, ALU.pow), rstd_ready)

            pool.wait_ge(S("constants"), 1)
            rstd("ab")
            for s in range(AHEAD):
                split(At(s))
            for n in range(20):
                split(At(S0["abin"] + n + AHEAD))
                if n == 4:
                    rstd("mem")
            for n in range(8):
                split(At(S0["k0"] + n + AHEAD))
                if n % 2 == 0:
                    g = n // 2
                    wait_emptied(pool, USE0["abin"] + 16 + g)
                    src = z[:, 16 + g, :]
                    for j in range(g + 1):
                        d, dst = 1 << j, t[2 + j % 2][:]
                        G.fence()
                        G.done(pool.tensor_copy(dst[:, 0:d], src[:, 0:d]))
                        G.done(pool.tensor_tensor(dst[:, d:T], src[:, d:T], src[:, 0:T - d], ALU.add))
                        src = dst
                    G.fence()
                    G.done(pool.tensor_tensor(src, src, inv[:, g, :], ALU.mult))
                    G.fence()
                    G.done(pool.tensor_tensor(z[:, 16 + g, :], src, z[:, 16 + g, :], ALU.subtract), S("pooled"))
            for n in range(4):
                split(At(S0["gates"] + n + AHEAD))
                pool.wait_ge(S("pooled_hi"), n + 1)
                G.done(pool.tensor_tensor(yl[:, 8 + n, :], z[:, 16 + n, :], yh[:, 8 + n, :].bitcast(F32),
                                          ALU.subtract), S("pooled_lo"))
            splits(S0["v0"], 8)
            splits(S0["about"], 12)
            rstd("xa0")
            splits(S0["q0"], 8)
            splits(S0["wo0"], 8)
            rstd("f0")

            def glu(name, J):
                base = S0[name]

                def step(j, i=None):
                    st = 12 if i is not None else 0
                    g = At(glu_slab(base, J, "g", j), st, i)
                    jj = At(j, 4 if i is not None else 0, i)
                    split(g + AHEAD)
                    split(g + (1 + AHEAD))
                    if j >= 2:
                        split(g + (2 + AHEAD))
                    pool.wait_ge(S(name + "_hid_hi"), (jj + 1).of(lambda n: n))
                    src = hidm if name == "moe" else hid
                    G.done(pool.tensor_tensor(yl[:, j % 4, :], src[:, j % 2, :], yh[:, j % 4, :].bitcast(F32),
                                              ALU.subtract), S(name + "_hid_lo"))

                trips, rest = glu_steps(J)
                for j in range(4):
                    step(j)
                with G.loop(trips, {w_lo_p: 6, S(name + "_hid_lo"): 4}, S(name + "_hid_lo")) as i:
                    for j in range(4, 8):
                        step(j, i)
                for j in range(rest, J):
                    step(j)
                splits(base + 3 * J - 2, 2)

            glu("f0", FJ)
            rstd("c")
            splits(S0["pw1"], 32)
            rstd("lnmean", mean=True)
            rstd("ln")
            splits(S0["pw2"], 8)
            rstd("xa1")
            splits(S0["q1"], 16)
            rstd("f1")
            glu("f1", FJ)
            rstd("final")
            rstd("mix")
            splits(S0["win"], 62 + 20)
            rstd("moe")
            glu("moe", MJ)
            rstd("out")

        @block.vector
        def _(dve):
            V = Program(dve, S("vector_chain"))

            def split(s):
                if s.base >= NSLAB or s.base % 2 == 1:
                    return
                dve.wait_ge(w_hi, s.of(lambda n: n + 1))
                V.done(dve.tensor_tensor(wl[:, s.base % SPLIT, :], raw[:, s.base % RAW, :],
                                         wh[:, s.base % SPLIT, :].bitcast(F32), ALU.subtract), w_lo_v)

            def splits(s, n):
                for k in range(n):
                    split(At(s + k + AHEAD))

            def norm_mean(name, eps=EPS):
                dve.wait_ge(stat_full, NORMS[name] + 1)
                V.fence()
                V.done(dve.tensor_scalar(ms, acc[0][:, 0:2], 1.0 / D, eps, ALU.mult, ALU.add), ms_ready)

            def norm_spread(name, dst):
                dve.wait_ge(rstd_ready, NORMS[name] + 1)
                V.fence()
                for q in range(TT):
                    V.done(dve.tensor_scalar(diag[:, q, :], ident[:], rcol[:, q:q + 1], None, ALU.mult), diag_ready)
                dve.wait_ge(bc_full, NORMS[name] + 1)
                V.fence()
                V.done(dve.tensor_copy(dst, acc[0][:, T:2 * T]), rstd_b_ready)
                V.fence()

            def pair_lo_parts(pair, gain):
                for c in range(KC):
                    dve.wait_ge(pair_hi, KC * PAIRS[pair] + c + 1)
                    V.done(dve.scalar_tensor_tensor(al[:, c, :], x[:, c, :], col(gain, c),
                                                    ah[:, c, :].bitcast(F32), ALU.mult, ALU.subtract), pair_lo)

            def take_sums(phase, bias=None):
                for c in range(KC):
                    wait_acc(dve, phase, c)
                    V.fence() if c == 0 else None
                    if bias is None:
                        ins = dve.tensor_tensor(x[:, c, :], acc_of(c), x[:, c, :], ALU.add)
                    else:
                        ins = dve.scalar_tensor_tensor(x[:, c, :], acc_of(c), col(bias, c), x[:, c, :],
                                                       ALU.add, ALU.add)
                    V.done(ins, acc_out)

            def col_out(name, n, dst, scale=None, by=None, slab=None):
                u = USE0[name] + n
                wait_slab(dve, At(S0[name] + (n if slab is None else slab)))
                b = pw[u % 4][:, 0:T]
                if by is None:
                    ins = dve.tensor_copy(dst, b)
                elif scale is None:
                    ins = dve.tensor_tensor(dst, b, by, ALU.mult)
                else:
                    ins = dve.scalar_tensor_tensor(dst, b, scale, by, ALU.mult, ALU.mult)
                V.done(ins, empty_v)

            dve.memset(ones[:], 1.0).then_inc(S("ones"), 1)
            V.done(dve.memset(mhalf, -0.5), S("constants"))
            dve.wait_ge(S("const_in"), 48)
            dve.wait_ge(S("x_in"), 16)
            pair_lo_parts("abin", "ab_norm")
            for s in range(AHEAD):
                split(At(s))
            norm_mean("ab")
            dve.wait_ge(S("decay_exp"), 1)
            lam = cols[:, C0["a_lambda"]:C0["a_lambda"] + 8]
            V.done(dve.tensor_scalar(lam_z, lam_e, 2.0, None, ALU.add))
            V.fence()
            V.done(dve.reciprocal(lam_z, lam_z))
            V.fence()
            V.done(dve.tensor_tensor(lam_z, lam_z, lam_e, ALU.mult))
            V.fence()
            V.done(dve.tensor_tensor(lam_q, lam_z, lam_z, ALU.mult))
            V.done(dve.memset(sp8, 1.0 / 19))
            for k in range(8, -1, -1):
                V.fence()
                V.done(dve.tensor_tensor(sp8, sp8, lam_q, ALU.mult))
                V.fence()
                V.done(dve.tensor_scalar(sp8, sp8, 1.0 / (2 * k + 1), None, ALU.add))
            V.fence()
            V.done(dve.scalar_tensor_tensor(sp8, sp8, 2.0, lam_z, ALU.mult, ALU.mult))
            V.done(dve.tensor_scalar(lam_q, lam, -1.0, 0.0, ALU.mult, ALU.max))
            V.fence()
            V.done(dve.tensor_tensor(sp8, sp8, lam_q, ALU.add))
            V.fence()
            V.done(dve.tensor_scalar(n4sp, sp8, -4.0, None, ALU.mult))
            V.done(dve.tensor_scalar(p4sp, sp8, 4.0, None, ALU.mult))
            V.done(dve.tensor_scalar(hbx, cols[:, C0["a_gate_x_b"]:C0["a_gate_x_b"] + 8], 0.5, None, ALU.mult))
            V.done(dve.tensor_scalar(hba, cols[:, C0["a_gate_a_b"]:C0["a_gate_a_b"] + 8], 0.5, None, ALU.mult))
            V.done(dve.tensor_scalar(hbc, cols[:, C0["c_b_pw1"] + 8:C0["c_b_pw1"] + 16], 0.5, None, ALU.mult))
            V.done(dve.tensor_scalar(nsink, cols[:, C0["sinks"]:C0["sinks"] + 16], -1.0, None, ALU.mult), S("decay"))
            norm_spread("ab", rstd_b[:])

            def mem_lo(l, c):
                dve.wait_ge(S("m_hi"), KC * l + c + 1)
                V.done(dve.scalar_tensor_tensor(ml[:, c, :], mem[:, c, :], col(f"mem_norm{l}", c),
                                                mh[:, c, :].bitcast(F32), ALU.mult, ALU.subtract), S("m_lo"))

            for n in range(20):
                split(At(S0["abin"] + n + AHEAD))
                if n == 4:
                    norm_mean("mem")
                if n == 7:
                    norm_spread("mem", mem_rstd[:])
                    V.fence()
                    for c in range(KC):
                        V.done(dve.tensor_tensor(mem[:, c, :], mem[:, c, :], mem_rstd[:], ALU.mult), S("mem_normed"))
                if n >= 11 and n < 19:
                    mem_lo(0, n - 11)
                col_out("abin", n, z[:, n, :], by=rstd_b[:])
            for n in range(8):
                split(At(S0["k0"] + n + AHEAD))
                col_out("k0", n, k_t[:, n, :])
                for k in range(CONV_A):
                    w, lag = col("a_conv_w", n * CONV_A + CONV_A - 1 - k), k
                    V.fence()
                    if k == 0:
                        V.done(dve.tensor_scalar(xr[:, n, :], z[:, 8 + n, :], w, col("a_conv_b", n),
                                                 ALU.mult, ALU.add))
                    else:
                        V.done(dve.scalar_tensor_tensor(xr[:, n, lag:T], z[:, 8 + n, 0:T - lag], w, xr[:, n, lag:T],
                                                        ALU.mult, ALU.add),
                               S("xr_ready") if k == CONV_A - 1 else None)
                dve.wait_ge(S("xr_hi"), n + 1)
                V.done(dve.tensor_tensor(yl[:, n, :], xr[:, n, :], yh[:, n, :].bitcast(F32), ALU.subtract),
                       S("xr_lo"))
            for n in range(4):
                split(At(S0["gates"] + n + AHEAD))
                for h in (2 * n, 2 * n + 1):
                    dve.wait_ge(S("gates_through"), h + 1)
                    V.fence()
                    V.done(dve.tensor_tensor(diag[:].rearrange("p a b -> p (a b)"), a_t[:, h, :], a_t[:, h, :],
                                             ALU.mult))
                    V.fence()
                    V.done(dve.scalar_tensor_tensor(z[:, 8 + h, :], diag[:].rearrange("p a b -> p (a b)"), 1.0,
                                                    z[:, 8 + h, :], ALU.add, ALU.mult))
                    V.done(dve.scalar_tensor_tensor(xr[:, h, :], t[h % 2][:], 1.0, xr[:, h, :], ALU.add, ALU.mult),
                           S("root_in"))
                u = USE0["gates"] + 3 * n + 2
                wait_slab(dve, At(S0["gates"] + n))
                V.done(dve.tensor_scalar(z[:, 16 + n, :], pw[u % 4][:, 0:T], col("b_group_b", n), col("b_scale", n),
                                         ALU.add, ALU.mult), empty_v)
                dve.wait_ge(S("yb_hi"), n + 1)
                V.done(dve.tensor_tensor(yl[:, 8 + n, :], z[:, 16 + n, :], yh[:, 8 + n, :].bitcast(F32),
                                         ALU.subtract), S("yb_lo"))

            def values_out(name, half):
                wait_slab(dve, At(S0[name] + 4 * half + 3))
                for q in range(TT):
                    u = USE0[name] + 2 * half + q
                    V.done(dve.tensor_copy(v_m[:, q, half * 512:half * 512 + 512], pw[u % 4][:, :]), empty_v)

            for n in range(8):
                split(At(S0["v0"] + n + AHEAD))
                dve.wait_ge(S("root"), 1)
                V.fence()
                V.done(dve.tensor_tensor(xr[:, n, :], xr[:, n, :], z[:, 8 + n, :], ALU.mult))
                V.fence()
                V.done(dve.tensor_tensor_scan(z[:, 8 + n, :], a_t[:, n, :], xr[:, n, :], 0.0, ALU.mult, ALU.add))
                V.fence()
                dve.wait_ge(S("gate_gelu"), n + 1)
                V.done(dve.tensor_tensor(xr[:, n, :], z[:, 8 + n, :], z[:, n, :], ALU.mult), S("ya_ready"))
                dve.wait_ge(S("ya_hi"), n + 1)
                V.done(dve.tensor_tensor(yl[:, n, :], xr[:, n, :], yh[:, n, :].bitcast(F32), ALU.subtract),
                       S("ya_lo"))
                if n == 5 or n == 7:
                    values_out("v0", n // 6)
            splits(S0["about"], 12)
            take_sums("about")

            def normed_pair(name, pair, gain):
                pair_lo_parts(pair, gain)
                norm_mean(name)

            def queries(l):
                for n in range(8):
                    split(At(S0[f"q{l}"] + n + AHEAD))
                    if n == 2:
                        norm_spread(f"xa{l}", rstd_b[:])
                        for k in range(3):
                            col_out(f"q{l}", k, q_t[:, k, :], 1.0 / 16, rstd_b[:])
                    elif n > 2:
                        col_out(f"q{l}", n, q_t[:, n, :], 1.0 / 16, rstd_b[:])

            def cross(l):
                name, n_u = f"x{l}", USE0[f"x{l}"]
                for h in range(XH + 1):
                    if h < XH:
                        for qt in range(TT):
                            k = x_score(h) + qt
                            dve.wait_ge(mm_done, MM0[name] + k + 1)
                            V.fence()
                            V.done(dve.tensor_reduce(nmax[:, qt:qt + 1], pw[(n_u + k) % 4][:, 0:T], AX.X, ALU.max,
                                                     negate=True), S(name + "_max"))
                        for qt in range(TT):
                            wait_emptied(dve, n_u + x_score(h) + qt)
                            V.done(dve.reciprocal(rec[:, qt:qt + 1], den[:, qt:qt + 1]))
                            V.fence()
                            V.done(dve.tensor_scalar(prob[:, h % 2, qt, :], prob[:, h % 2, qt, :], rec[:, qt:qt + 1],
                                                     None, ALU.mult), S(name + "_prob"))
                    if h >= 1:
                        k = x_turn(h - 1) + 2
                        dve.wait_ge(S(name + "_hi"), h)
                        V.done(dve.tensor_tensor(yl[:, 2 * h - 2:2 * h, :],
                                                 pw[(n_u + k) % 4][:, :].rearrange("p (a q) -> p a q", a=2),
                                                 yh[:, 2 * h - 2:2 * h, :].bitcast(F32), ALU.subtract), empty_v)

            def glu(name, J):
                base, moe, l = S0[name], name == "moe", name[-1]

                def step(j, i=None):
                    st, st4 = (12, 4) if i is not None else (0, 0)
                    g = At(glu_slab(base, J, "g", j), st, i)
                    jj = At(j, st4, i)
                    u = USE0[name] + 2 * j
                    if j == 1 and not moe:
                        norm_spread(name, rstd_b[:])
                        gate(0, At(0), At(base), None)
                        up(0, At(0), At(base + 1), USE0[name] + 1)
                    split(g + AHEAD)
                    if j >= 1 and not moe:
                        gate(j, jj, g, i)
                    split(g + (1 + AHEAD))
                    if j >= 1 or moe:
                        up(j, jj, g + 1, u + 1)
                    if j >= 2:
                        split(g + (2 + AHEAD))

                def gate(j, jj, g, i):
                    wait_slab(dve, g)
                    V.fence()
                    V.done(dve.tensor_tensor(gpad[:, j % 2, 2:T + 2], pw[(USE0[name] + 2 * j) % 4][:, 0:T],
                                             rstd_b[:], ALU.mult), empty_v)
                    for k in range(CONV_F):
                        w = col(f"f_dw_w{l}", j * CONV_F + CONV_F - 1 - k, 4 * CONV_F, i)
                        V.fence()
                        if k == 0:
                            V.done(dve.tensor_scalar(cf[:, j % 2, :], gpad[:, j % 2, 2:T + 2], w,
                                                     col(f"f_dw_b{l}", j, 4, i), ALU.mult, ALU.add))
                        else:
                            V.done(dve.scalar_tensor_tensor(cf[:, j % 2, :], gpad[:, j % 2, 2 - k:T + 2 - k], w,
                                                            cf[:, j % 2, :], ALU.mult, ALU.add),
                                   S(name + "_conv") if k == CONV_F - 1 else None)

                def up(j, jj, s, u):
                    wait_slab(dve, s)
                    if j >= 2:
                        dve.wait_ge(S(name + "_hid_lo"), (jj + -1).of(lambda n: n))
                    V.fence()
                    if moe:
                        dve.wait_ge(empty_a, (jj + 1).of(lambda n: emptied(USE0[name] - 1, "a") + n))
                        V.done(dve.tensor_tensor(hidm[:, j % 2, :], pw[u % 4][:, 0:T], silu[:, j % 2, :], ALU.mult),
                               empty_v)
                        V.fence()
                        e = gates_b[:, j // 4, :] if jj.i is None else \
                            gates_b[:, bass.ds(jj.i + j // 4, 1), :].rearrange("p a t -> p (a t)")
                        V.done(dve.tensor_tensor(hidm[:, j % 2, :], hidm[:, j % 2, :], e, ALU.mult),
                               S(name + "_hidden"))
                    else:
                        V.done(dve.tensor_tensor(uf[:, j % 2, :], pw[u % 4][:, 0:T], rstd_b[:], ALU.mult), empty_v)
                        V.fence()
                        dve.wait_ge(S(name + "_act"), (jj + 1).of(lambda n: n))
                        V.done(dve.tensor_tensor(hid[:, j % 2, :], cf[:, j % 2, :], uf[:, j % 2, :], ALU.mult),
                               S(name + "_hidden"))

                if not moe:
                    V.fence()
                    V.done(dve.memset(gpad[:, :, 0:2], 0.0))
                trips, rest = glu_steps(J)
                for j in range(4):
                    step(j)
                raised = {w_lo_v: 6, S(name + "_hidden"): 4, empty_v: 4 if moe else 8}
                if not moe:
                    raised[S(name + "_conv")] = 4
                    raised[S("vector_chain")] = 8
                last = w_lo_v if glu_slab(base, J, "u", 7) % 2 == 0 else S(name + "_hidden")
                with V.loop(trips, raised, last) as i:
                    for j in range(4, 8):
                        step(j, i)
                for j in range(rest, J):
                    step(j)
                splits(base + 3 * J - 2, 2)

            normed_pair("xa0", "q0", "xa_norm0")
            queries(0)
            cross(0)
            splits(S0["wo0"], 8)
            take_sums("wo0")
            normed_pair("f0", "f0", "f_norm0")
            glu("f0", FJ)
            take_sums("f0")
            normed_pair("c", "pw1", "c_norm")
            V.fence()
            V.done(dve.memset(hpad[:, :, 0:CONV_C - 1], 0.0))
            taps = KC * CONV_C

            def conv_taps(lo, hi):
                for m in range(lo, hi):
                    c, k = m % 2 + 2 * (m // (2 * CONV_C)), (m // 2) % CONV_C
                    w = col("c_dw_w", c * CONV_C + k)
                    src = hpad[:, c, k:k + T]
                    V.fence(1)
                    if k == 0:
                        V.done(dve.tensor_scalar(cv[:, c, :], src, w, col("c_dw_b", c), ALU.mult, ALU.add))
                    else:
                        V.done(dve.scalar_tensor_tensor(cv[:, c, :], src, w, cv[:, c, :], ALU.mult, ALU.add),
                               S("conv_out") if k == CONV_C - 1 else None)

            done_taps = 0
            for n in range(32):
                s = S0["pw1"] + n
                split(At(s + AHEAD))
                if n == 2:
                    norm_spread("c", rstd_b[:])
                if 2 <= n < 18:
                    for k in ([0, 1, 2] if n == 2 else [n] if n < 16 else []):
                        c, ta, tb = k // 2, t[2 * (k // 2 % 2)][:], t[2 * (k // 2 % 2) + 1][:]
                        V.fence()
                        col_out("pw1", k, tb if k % 2 else ta, by=rstd_b[:])
                        if k % 2:
                            dve.wait_ge(S("glu_tanh"), c + 1)
                            V.done(dve.tensor_scalar(tb, tb, 0.5, 0.5, ALU.mult, ALU.add))
                            V.fence()
                            V.done(dve.scalar_tensor_tensor(hpad[:, c, CONV_C - 1:], ta, col("c_b_pw1", c), tb,
                                                            ALU.add, ALU.mult), S("glu_out"))
                if n == 7:
                    dve.wait_ge(S("mem_again"), 16)
                    V.fence()
                    for c in range(KC):
                        V.done(dve.tensor_tensor(mem[:, c, :], mem[:, c, :], mem_rstd[:], ALU.mult), S("mem_normed"))
                if 11 <= n < 15:
                    mem_lo(1, 2 * (n - 11))
                    mem_lo(1, 2 * (n - 11) + 1)
                if 16 <= n < 24:
                    col_out("k1", n - 16, k_t[:, n - 16, :])
                if n in (27, 31):
                    values_out("v1", (n - 27) // 4)
                upto = min(taps * max(n - 3, 0) // 28, 2 * CONV_C * ((min(n, 15) + 1) // 4))
                conv_taps(done_taps, upto)
                done_taps = upto
            conv_taps(done_taps, taps)
            norm_mean("lnmean", 0.0)
            norm_spread("lnmean", t[0][:])
            V.fence()
            for c in range(KC):
                V.done(dve.tensor_tensor(cv[:, c, :], cv[:, c, :], t[0][:], ALU.subtract), S("ln_centred"))
            norm_mean("ln")
            norm_spread("ln", t[0][:])
            V.fence()
            for c in range(KC):
                V.done(dve.tensor_tensor(cv[:, c, :], cv[:, c, :], t[0][:], ALU.mult), S("ln_scaled"))
            for c in range(KC):
                dve.wait_ge(S("ln_hi"), c + 1)
                V.done(dve.tensor_tensor(yl[:, c, :], cv[:, c, :], yh[:, c, :].bitcast(F32), ALU.subtract),
                       S("ln_lo"))
            splits(S0["pw2"], 8)
            take_sums("pw2", "c_b_pw2")
            normed_pair("xa1", "q1", "xa_norm1")
            queries(1)
            cross(1)
            splits(S0["wo1"], 8)
            take_sums("wo1")
            normed_pair("f1", "f1", "f_norm1")
            glu("f1", FJ)
            take_sums("f1")
            norm_mean("final")
            norm_spread("final", rstd_b[:])
            V.fence()
            for c in range(KC):
                V.done(dve.scalar_tensor_tensor(x[:, c, :], x[:, c, :], col("final_norm", c), rstd_b[:],
                                                ALU.mult, ALU.mult), S("x_normed"))
            normed_pair("mix", "win", "g_mix")
            for n in range(62):
                split(At(S0["win"] + n + AHEAD))
                if n == 2:
                    norm_spread("mix", rstd_b[:])
                for k in ([0, 1, 2] if n == 2 else [n] if n > 2 else []):
                    if k < 12:
                        col_out("win", k, q2[:, k, :], 0.125, rstd_b[:])
                    elif k < 24:
                        col_out("win", k, k2[:, k - 12, :], by=rstd_b[:])
                    elif k < 32:
                        col_out("win", k, q2[:, k - 12, :], 0.125, rstd_b[:])
                    elif k < 44:
                        if k % 4 == 3:
                            b = (k - 32) // 4
                            wait_slab(dve, At(S0["win"] + k))
                            for q in range(TT):
                                u = USE0["win"] + 32 + 2 * b + q
                                V.done(dve.tensor_scalar(v2[:, q, 512 * b:512 * b + 512], pw[u % 4][:, :],
                                                         rcol[:, q:q + 1], None, ALU.mult), empty_v)
                    elif k == 44:
                        col_out("win", 38, k2[:, 12, :], by=rstd_b[:], slab=44)
                    elif k == 45:
                        wait_slab(dve, At(S0["win"] + 45))
                        for q in range(TT):
                            u = USE0["win"] + 39 + q
                            V.done(dve.tensor_scalar(v2[:, q, 1536:1664], pw[u % 4][:, 0:P], rcol[:, q:q + 1],
                                                     None, ALU.mult), empty_v)
                    else:
                        col_out("win", 41 + k - 46, gt[:, k - 46, :], by=rstd_b[:], slab=k)
            dve.wait_ge(S("masks_in"), 16)
            for m in range(len(HEADS2) + 1):
                if m < len(HEADS2):
                    kind, h = HEADS2[m]
                    G_ = groups(kind)
                    for qt in range(TT):
                        at, nk = (0, P) if qt == 0 else (3 * P, 2 * P)
                        for g in range(G_):
                            k = a_score(m) + qt * G_ + g
                            slope = SLOPES_DIL[8 * g + h] if kind == "d" else SLOPES_SWA[h]
                            dve.wait_ge(mm_done, MM0["attn2"] + k + 1)
                            V.done(dve.scalar_tensor_tensor(
                                sc[:, m % 2, at + g * nk:at + g * nk + nk],
                                masks[:, g if kind == "d" else 3, (0 if qt == 0 else P):(P if qt == 0 else 3 * P)],
                                -slope, pw[(USE0["attn2"] + k) % 4][:, 0:nk], ALU.mult, ALU.add), empty_v)
                        V.fence()
                        mx = nmax[:, qt:qt + 1]
                        V.done(dve.tensor_reduce(mx, sc[:, m % 2, at:at + G_ * nk], AX.X, ALU.max, negate=True),
                               S("attn2_max") if kind == "d" else None)
                        if kind == "s":
                            V.fence()
                            V.done(dve.tensor_scalar(mx, mx, nsink[:, h:h + 1], None, ALU.min), S("attn2_max"))
                    for qt in range(TT):
                        at, nk = (0, P) if qt == 0 else (3 * P, 2 * P)
                        dve.wait_ge(S("attn2_exp"), 2 * m + qt + 1)
                        r = rec[:, qt:qt + 1]
                        if kind == "s":
                            V.fence()
                            V.done(dve.tensor_tensor(den[:, qt:qt + 1], den[:, qt:qt + 1], esink[:, qt:qt + 1],
                                                     ALU.add))
                        V.fence()
                        V.done(dve.reciprocal(r, den[:, qt:qt + 1]))
                        V.fence()
                        s_ap = sc[:, m % 2, at:at + G_ * nk]
                        V.done(dve.tensor_scalar(s_ap, s_ap, r, None, ALU.mult), S("attn2_prob"))
                if m >= 1:
                    kind, h = HEADS2[m - 1]
                    k = a_turn(m - 1) + groups(kind)
                    c, half = mixed_at(kind, h)
                    dve.wait_ge(S("attn2_hi"), m)
                    V.done(dve.tensor_tensor(yl[half:half + 64, c, :], pw[(USE0["attn2"] + k) % 4][half:half + 64, 0:T],
                                             yh[half:half + 64, c, :].bitcast(F32), ALU.subtract), empty_v)
            dve.wait_ge(S("mix_gates"), 16)
            for phase, first in (("brd", 0), ("brs", 8)):
                splits(S0[phase], dict(PHASES)[phase])
                for c in range(KC):
                    wait_acc(dve, phase, c)
                    V.done(dve.scalar_tensor_tensor(gt[:, first + c, :], gt[:, first + c, :], 1.0, acc_of(c),
                                                    ALU.add, ALU.mult), acc_out)
            V.fence()
            for c in range(KC):
                V.done(dve.tensor_tensor(gt[:, c, :], gt[:, c, :], gt[:, 8 + c, :], ALU.add), S("mixed"))
            for c in range(KC):
                dve.wait_ge(S("mixed_hi"), c + 1)
                V.done(dve.scalar_tensor_tensor(yl[:, c, :], gt[:, c, :], 0.5, yh[:, c, :].bitcast(F32),
                                                ALU.mult, ALU.subtract), S("mixed_lo"))
            splits(S0["wout"], 8)
            take_sums("wout")
            norm_mean("moe")
            norm_spread("moe", rstd_b[:])
            V.fence()
            for c in range(KC):
                V.done(dve.scalar_tensor_tensor(hf[:, c, :], x[:, c, :], col("g_ffn", c), rstd_b[:],
                                                ALU.mult, ALU.mult), S("h_ready"))
            for c in range(KC):
                dve.wait_ge(pair_hi, KC * PAIRS["moe"] + c + 1)
                V.done(dve.tensor_tensor(al[:, c, :], hf[:, c, :], ah[:, c, :].bitcast(F32), ALU.subtract), pair_lo)
            def first_of(dst, values, top, n, count):
                V.fence()
                V.done(dve.tensor_scalar(dst, values, top, None, ALU.is_equal))
                V.fence()
                V.done(dve.tensor_tensor_scan(count, one_row[:, 0:n], dst, 0.0, ALU.mult, ALU.add))
                V.fence()
                V.done(dve.tensor_scalar(count, count, 1.0, None, ALU.is_equal))
                V.fence()
                V.done(dve.tensor_tensor(dst, dst, count, ALU.mult))

            one_row = ones[:, 0:8]
            dve.wait_ge(S("router_full"), 1)
            for q in range(TT):
                V.done(dve.tensor_tensor(lg[:, q, :], acc[1][:, 64 * q:64 * q + 36],
                                         cols[:, C0["r_bias"]:C0["r_bias"] + 36], ALU.add), S("logits_out"))
            gmx, gsum, e2, gap = rt[:, 0:1], rt[:, 1:2], rt[:, 2:3], rt[:, 3:4]
            gmask, count = rt[:, 8:12], rt[:, 88:96]
            sel, f1, f2, sel2 = rt[:, 16:24], rt[:, 24:32], rt[:, 32:40], rt[:, 40:48]
            m1, m2, w1, gw = rt[:, 12:13], rt[:, 13:14], rt[:, 14:15], rt[:, 15:16]
            w2, top = rt[:, 48:49], rt[:, 49:50]
            gall = rt[:, 56:88]
            for q in range(TT):
                V.fence()
                V.done(dve.tensor_reduce(top, lg[:, q, 0:4], AX.X, ALU.max))
                V.fence()
                V.done(dve.tensor_scalar(gmx, top, -1.0, None, ALU.mult), S("group_max"))
                first_of(gmask, lg[:, q, 0:4], top, 4, count[:, 0:4])
                for g in range(4):
                    V.fence()
                    el = lg[:, q, 4 + 8 * g:12 + 8 * g]
                    if g == 0:
                        V.done(dve.tensor_scalar(sel, el, gmask[:, 0:1], None, ALU.mult))
                    else:
                        V.done(dve.scalar_tensor_tensor(sel, el, gmask[:, g:g + 1], sel, ALU.mult, ALU.add))
                V.fence()
                V.done(dve.tensor_reduce(m1, sel, AX.X, ALU.max))
                first_of(f1, sel, m1, 8, count)
                V.fence()
                V.done(dve.scalar_tensor_tensor(sel2, f1, NEG, sel, ALU.mult, ALU.add))
                V.fence()
                V.done(dve.tensor_reduce(m2, sel2, AX.X, ALU.max))
                first_of(f2, sel2, m2, 8, count)
                V.fence()
                V.done(dve.tensor_tensor(gap, m2, m1, ALU.subtract), S("expert_gap"))
                dve.wait_ge(S("expert_exp"), q + 1)
                V.done(dve.reciprocal(gw, gsum))
                V.done(dve.tensor_scalar(w1, e2, 1.0, None, ALU.add))
                V.fence()
                V.done(dve.reciprocal(w1, w1))
                V.fence()
                V.done(dve.tensor_tensor(w1, w1, gw, ALU.mult))
                V.fence()
                V.done(dve.tensor_tensor(w2, w1, e2, ALU.mult))
                V.fence()
                V.done(dve.tensor_scalar(f1, f1, w1, None, ALU.mult))
                V.fence()
                V.done(dve.scalar_tensor_tensor(f1, f2, w2, f1, ALU.mult, ALU.add))
                if q == 1:
                    dve.wait_ge(S("gates_turned"), 1)
                for g in range(4):
                    V.fence()
                    V.done(dve.tensor_scalar(gall[:, 8 * g:8 * g + 8], f1, gmask[:, g:g + 1], None, ALU.mult),
                           S("gates") if g == 3 else None)
            dve.wait_ge(S("gates_turned"), 2)
            V.done(dve.tensor_copy(gate_rows[:], acc[2][0:NE, 0:T]), S("gate_rows"))
            V.fence()
            for e in range(NE):
                if e >= 2:
                    dve.wait_ge(mm_done, MM0["gb"] + e - 1)
                V.done(dve.tensor_scalar(gate_row[:, e % 2, :], gate_rows[:], ident[0:NE, e:e + 1], None, ALU.mult),
                       S("gate_row"))
            glu("moe", MJ)
            take_sums("moe")
            norm_mean("out")
            norm_spread("out", rstd_b[:])
            V.fence()
            for c in range(KC):
                V.done(dve.scalar_tensor_tensor(x[:, c, :], x[:, c, :], col("g_final", c), rstd_b[:],
                                                ALU.mult, ALU.mult), S("x_final"))

        @block.tensor
        def _(pe):
            def tile3(dst, s, n, hi, lo, start, stop, **kw):
                w = slice(n * P, n * P + P)
                pe.matmul(dst, wh[:, s.base % SPLIT, w], hi, start=start, stop=False, **kw)
                pe.matmul(dst, wl[:, s.base % SPLIT, w], hi, start=False, stop=False, **kw)
                return pe.matmul(dst, wh[:, s.base % SPLIT, w], lo, start=False, stop=stop, **kw)

            def norm_sums(name, src, ready):
                for c in range(KC):
                    ready(min(c + 1, KC - 1) if c == 0 else c)
                    for q in range(TT):
                        last = pe.matmul(acc[0][:, q:q + 1], src[:, c, q * P:q * P + P], ones[:, 0:1],
                                         start=(c == 0 and q == 0), stop=(c == KC - 1), skip_group_check=True)
                last.then_inc(stat_full, 1)

            def sq_sums(name):
                norm_sums(name, sq, lambda c: pe.wait_ge(sq_ready, KC * (NORMS[name] - (NORMS[name] > NORMS["lnmean"]))
                                                         + c + 1))

            def norm_spread(name):
                pe.wait_ge(diag_ready, TT * (NORMS[name] + 1))
                for q in range(TT):
                    last = pe.matmul(acc[0][:, T + q * P:T + q * P + P], ones[:], diag[:, q, :], start=True, stop=True)
                last.then_inc(bc_full, 1)

            def drain(u):
                for who, sem in (("v", empty_v), ("a", empty_a)):
                    if u and emptied(u - 1, who):
                        pe.wait_ge(sem, emptied(u - 1, who))

            def col_slab(s, u, hi, lo, wait_n=None, first_ready=None):
                wait_split(pe, s)
                if wait_n is not None:
                    pe.wait_ge(empty_v, wait_n)
                for k in range(KC):
                    if first_ready is not None:
                        first_ready(k)
                    last = tile3(pw[u % 4][:, 0:T], s, k, hi[:, k, :], lo[:, k, :], k == 0, k == KC - 1)
                last.then_inc(slab_done, 1)

            def col_phase(name, n, hi, lo, ready=None, hook=None, straight=None, s_off=0, u_off=0):
                s0, u0 = S0[name] + s_off, USE0[name] + u_off
                straight = straight or (8 if n == 8 else 4)
                v0 = emptied(u0 - 1, "v") if u0 else 0
                drain(u0)
                for k in range(straight):
                    col_slab(At(s0 + k), u0 + k, hi, lo, v0 + k - 3 if k >= 4 else None, ready if k == 0 else None)
                    if hook:
                        hook(k)
                if n > straight:
                    with pe.Fori(0, (n - straight) // 4) as i:
                        for j in range(straight, straight + 4):
                            col_slab(At(s0 + j, 4, i), u0 + j, hi, lo, i * 4 + (v0 + j - 3))

            def row_slab(s, k, first, last, start_acc=None):
                wait_split(pe, s)
                for n in range(KC):
                    ins = tile3(acc_of(n), s, n, yh[:, k, :], yl[:, k, :], first and n % 2 == 0, last,
                                skip_group_check=True)
                    if last and n < KC - 1:
                        ins.then_inc(acc_full, 1)
                ins.then_inc(slab_done, 1)

            def row_phase(name, order, ready, norm):
                if ACCS[name]:
                    pe.wait_ge(acc_out, KC * ACCS[name])
                if norm is not None:
                    pe.wait_ge(rstd_b_ready, NORMS[norm] + 1)
                for n, k in enumerate(order):
                    ready(k)
                    row_slab(At(S0[name] + n), k, n == 0, n == len(order) - 1)

            def pair_ready(pair):
                return lambda k: pe.wait_ge(pair_lo, KC * PAIRS[pair] + k + 1)

            def values(s0, u0, hi, lo, half):
                for kk in range(4):
                    s = At(s0 + 4 * half + kk)
                    wait_split(pe, s)
                    if kk == 0:
                        for q in range(TT):
                            wait_emptied(pe, u0 + 2 * half + q - 4)
                    for e in range(2):
                        k = 2 * kk + e
                        w = slice(e * 512, e * 512 + 512)
                        for q in range(TT):
                            dst = pw[(u0 + 2 * half + q) % 4][:, :]
                            tk = slice(q * P, q * P + P)
                            slot = s.base % SPLIT
                            pe.matmul(dst, hi[:, k, tk], wh[:, slot, w], start=(k == 0), stop=False)
                            pe.matmul(dst, hi[:, k, tk], wl[:, slot, w], start=False, stop=False)
                            last = pe.matmul(dst, lo[:, k, tk], wh[:, slot, w], start=False, stop=(k == KC - 1))
                    last.then_inc(slab_done, 1)

            def cross(l):
                name, n_u = f"x{l}", USE0[f"x{l}"]
                wait_emptied(pe, n_u - 1)
                for h in range(XH + 1):
                    if h < XH:
                        for qt in range(TT):
                            u = n_u + x_score(h) + qt
                            wait_emptied(pe, u - 4)
                            for c in range(2):
                                last = pe.matmul(pw[u % 4][:, 0:T], q_t[:, 2 * h + c, qt * P:qt * P + P],
                                                 k_t[:, 2 * h + c, :], start=(c == 0), stop=(c == 1))
                            last.then_inc(mm_done, 1)
                    if h >= 1:
                        g = h - 1
                        for qt in range(TT):
                            u = n_u + x_turn(g) + qt
                            wait_emptied(pe, u - 4)
                            pe.wait_ge(S(name + "_prob"), 2 * g + qt + 1)
                            for kt in range(TT):
                                last = pe.transpose(pw[u % 4][:, kt * P:kt * P + P],
                                                    prob[:, g % 2, qt, kt * P:kt * P + P], ident[:])
                            last.then_inc(mm_done, 1)
                        u = n_u + x_turn(g) + 2
                        wait_emptied(pe, u - 4)
                        wait_emptied(pe, u - 1)
                        for dc in range(2):
                            for kt in range(TT):
                                last = pe.matmul(pw[u % 4][:, dc * T:dc * T + T],
                                                 v_m[:, kt, h_cols(g, dc)], pt[:, g % 2, kt, :],
                                                 start=(kt == 0), stop=(kt == TT - 1))
                        last.then_inc(mm_done, 1)

            def h_cols(h, dc):
                return slice(h * 256 + dc * P, h * 256 + dc * P + P)

            def glu(name, J, pair, hook=None):
                base, moe, u0 = S0[name], name == "moe", USE0[name]
                v0, a0 = emptied(u0 - 1, "v"), emptied(u0 - 1, "a")
                drain(u0)

                def bank_free(j, jj, kind):
                    if j < 2:
                        return
                    if moe:
                        pe.wait_ge(empty_a if kind == "g" else empty_v,
                                   (jj + -1).of(lambda n: (a0 if kind == "g" else v0) + n))
                    else:
                        pe.wait_ge(empty_v, (jj + -2).of(lambda n: v0 + 2 * n + (1 if kind == "g" else 2)))

                def row(j, jj, s, last=False):
                    pe.wait_ge(S(name + "_hid_lo"), (jj + 1).of(lambda n: n))
                    row_slab(s, j % 4, j == 0, last)

                def step(j, i=None):
                    st, st4 = (12, 4) if i is not None else (0, 0)
                    g, jj = At(glu_slab(base, J, "g", j), st, i), At(j, st4, i)
                    bank_free(j, jj, "g")
                    col_slab(g, u0 + 2 * j, ah, al, None, pair_ready(pair) if j == 0 else None)
                    bank_free(j, jj, "u")
                    col_slab(g + 1, u0 + 2 * j + 1, ah, al)
                    if j == 0 and hook:
                        hook()
                    if j >= 2:
                        if j == 2:
                            pe.wait_ge(acc_out, KC * ACCS[name])
                            pe.wait_ge(rstd_b_ready, NORMS[name] + 1)
                        row(j - 2, jj + -2, g + 2)

                trips, rest = glu_steps(J)
                for j in range(4):
                    step(j)
                with pe.Fori(0, trips) as i:
                    for j in range(4, 8):
                        step(j, i)
                for j in range(rest, J):
                    step(j)
                for j in (J - 2, J - 1):
                    row(j, At(j), At(glu_slab(base, J, "d", j)), last=(j == J - 1))

            pe.wait_ge(S("ones"), 1)
            sq_sums("ab")

            def abin_hook(k):
                if k == 1:
                    norm_spread("ab")
                if k == 2:
                    sq_sums_mem()
                if k == 6:
                    norm_spread("mem")

            def sq_sums_mem():
                pe.wait_ge(rstd_b_ready, NORMS["ab"] + 1)
                sq_sums("mem")

            col_phase("abin", 20, ah, al, pair_ready("abin"), abin_hook, straight=8)
            col_phase("k0", 8, mh, ml, lambda k: pe.wait_ge(S("m_lo"), k + 1))
            for n in range(4):
                s = At(S0["gates"] + n)
                wait_split(pe, s)
                for e in range(2):
                    h, u = 2 * n + e, USE0["gates"] + 3 * n + e
                    wait_emptied(pe, u - 4)
                    pe.wait_ge(S("xr_lo"), h + 1)
                    for g in range(2):
                        last = tile3(pw[u % 4][:, g * T:g * T + T], s, 2 * e + g, yh[:, h, :], yl[:, h, :],
                                     True, True)
                    last.then_inc(S("gate_products"), 1)
                u = USE0["gates"] + 3 * n + 2
                wait_emptied(pe, u - 4)
                pe.wait_ge(S("pooled_lo"), n + 1)
                tile3(pw[u % 4][:, 0:T], s, 4, yh[:, 8 + n, :], yl[:, 8 + n, :], True, True) \
                    .then_inc(slab_done, 1)
            for half in range(2):
                values(S0["v0"], USE0["v0"], mh, ml, half)
            row_phase("about", [8, 9, 10, 11, 0, 1, 2, 3, 4, 5, 6, 7],
                      lambda k: pe.wait_ge(S("yb_lo"), k - 7) if k >= 8 else pe.wait_ge(S("ya_lo"), k + 1), "mem")

            def spread_hook(name):
                return lambda k=1: norm_spread(name) if k == 1 else None

            def cross_layer(l):
                sq_sums(f"xa{l}")
                col_phase(f"q{l}", 8, ah, al, pair_ready(f"q{l}"), spread_hook(f"xa{l}"))
                cross(l)
                row_phase(f"wo{l}", range(8),
                          lambda k: wait_emptied(pe, USE0[f"x{l}"] + x_turn(k // 2) + 2), f"xa{l}")
                sq_sums(f"f{l}")
                glu(f"f{l}", FJ, f"f{l}", lambda: norm_spread(f"f{l}"))

            cross_layer(0)
            sq_sums("c")
            col_phase("pw1", 16, ah, al, pair_ready("pw1"), spread_hook("c"))
            col_phase("k1", 8, mh, ml, lambda k: pe.wait_ge(S("m_lo"), KC + k + 1))
            for half in range(2):
                values(S0["v1"], USE0["v1"], mh, ml, half)
            pe.wait_ge(rstd_b_ready, NORMS["c"] + 1)
            norm_sums("lnmean", cv, lambda c: pe.wait_ge(S("conv_out"), c + 1))
            norm_spread("lnmean")
            sq_sums("ln")
            norm_spread("ln")
            row_phase("pw2", range(8), lambda k: pe.wait_ge(S("ln_lo"), k + 1), "ln")
            cross_layer(1)
            sq_sums("final")
            norm_spread("final")
            sq_sums("mix")
            col_phase("win", 32, ah, al, pair_ready("win"), spread_hook("mix"))
            for b in range(3):
                values(S0["win"] + 32 + 4 * b, USE0["win"] + 32 + 2 * b, ah, al, 0)
            s, u = At(S0["win"] + 44), USE0["win"] + 38
            wait_emptied(pe, u - 4)
            col_slab(s, u, ah, al)
            s, u = s + 1, u + 1
            wait_split(pe, s)
            for q in range(TT):
                wait_emptied(pe, u + q - 4)
                dst, slot, tk = pw[(u + q) % 4][:, 0:P], s.base % SPLIT, slice(q * P, q * P + P)
                for k in range(KC):
                    w = slice(k * P, k * P + P)
                    pe.matmul(dst, ah[:, k, tk], wh[:, slot, w], start=(k == 0), stop=False)
                    pe.matmul(dst, ah[:, k, tk], wl[:, slot, w], start=False, stop=False)
                    last = pe.matmul(dst, al[:, k, tk], wh[:, slot, w], start=False, stop=(k == KC - 1))
            last.then_inc(slab_done, 1)
            col_phase("win", 16, ah, al, s_off=46, u_off=41)
            n_u = USE0["attn2"]
            for m in range(len(HEADS2) + 1):
                if m < len(HEADS2):
                    kind, h = HEADS2[m]
                    for qt in range(TT):
                        nk = P * (qt + 1)
                        for g in range(groups(kind)):
                            u = n_u + a_score(m) + qt * groups(kind) + g
                            qc, kc, half = heads_at(kind, h, g)
                            wait_emptied(pe, u - 4)
                            pe.matmul(pw[u % 4][:, 0:nk], q2[half:half + 64, qc, qt * P:qt * P + P],
                                      k2[half:half + 64, kc, 0:nk], start=True, stop=True).then_inc(mm_done, 1)
                if m >= 1:
                    kind, h = HEADS2[m - 1]
                    G_ = groups(kind)
                    pe.wait_ge(S("attn2_prob"), 2 * m)
                    for g in range(G_):
                        u = n_u + a_turn(m - 1) + g
                        wait_emptied(pe, u - 4)
                        b, s_ap = pw[u % 4], sc[:, (m - 1) % 2, :]
                        pe.transpose(b[:, 0:P], s_ap[:, g * P:g * P + P], ident[:])
                        for kt in range(2):
                            a = 3 * P + g * 2 * P + kt * P
                            last = pe.transpose(b[:, (1 + kt) * P:(2 + kt) * P], s_ap[:, a:a + P], ident[:])
                        last.then_inc(mm_done, 1)
                    u = n_u + a_turn(m - 1) + G_
                    wait_emptied(pe, u - 4)
                    wait_emptied(pe, u - 1)
                    c, half = mixed_at(kind, h)
                    for g in range(G_):
                        va = 512 * g + 64 * h if kind == "d" else 1536 + 64 * (h // 8)
                        dst = pw[u % 4][half:half + 64, :]
                        pe.matmul(dst[:, 0:T], v2[:, 0, va:va + 64], pt2[:, g, 0:T], start=(g == 0), stop=False,
                                  skip_group_check=True)
                        last = pe.matmul(dst[:, P:T], v2[:, 1, va:va + 64], pt2[:, g, T:3 * P], start=False,
                                         stop=(g == G_ - 1), skip_group_check=True)
                    last.then_inc(mm_done, 1)
            row_phase("brd", range(4), lambda k: wait_emptied(pe, n_u + a_turn(2 * k + 1) + 3), "mix")
            row_phase("brs", range(4, 12), lambda k: wait_emptied(pe, n_u + a_turn(8 + 8 + k - 4) + 1), None)
            row_phase("wout", range(8), lambda k: pe.wait_ge(S("mixed_lo"), k + 1), None)
            sq_sums("moe")
            norm_spread("moe")
            pe.wait_ge(S("router_in"), 16)
            pe.wait_ge(S("h_ready"), KC)
            for q in range(TT):
                for c in range(KC):
                    last = pe.matmul(acc[1][:, 64 * q:64 * q + 36], hf[:, c, q * P:q * P + P], rw[:, c, :],
                                     start=(c == 0), stop=(c == KC - 1))
            last.then_inc(S("router_full"), 1)
            for q in range(TT):
                pe.wait_ge(S("gates"), q + 1)
                pe.transpose(acc[2][0:NE, q * P:q * P + P], rt[:, 56:88], ident[:]).then_inc(S("gates_turned"), 1)
            drain(USE0["gb"])
            for e in range(NE):
                u = USE0["gb"] + e
                if e >= 4:
                    wait_emptied(pe, u - 4)
                pe.wait_ge(S("gate_row"), e + 1)
                pe.matmul(pw[u % 4][:, 0:T], ones[0:NE, :], gate_row[:, e % 2, :], start=True, stop=True) \
                    .then_inc(mm_done, 1)
            glu("moe", MJ, "moe")
            sq_sums("out")
            norm_spread("out")


def x_score(h):
    return 0 if h == 0 else 2 + 5 * (h - 1)


def x_turn(h):
    return 2 + 5 * h + (2 if h < XH - 1 else 0)


def a_score(m):
    n = 0
    for k in range(m):
        n += 2 * groups(HEADS2[k][0]) + (groups(HEADS2[k - 1][0]) + 1 if k >= 1 else 0)
    return n


def a_turn(m):
    return a_score(m + 1) + (2 * groups(HEADS2[m + 1][0]) if m + 1 < len(HEADS2) else 0)


def heads_at(kind, h, g):
    if kind == "d":
        n = 8 * g + h
        return n // 2, n // 2, 64 * (n % 2)
    return 12 + h % 8, 12, 64 * (h // 8)


def mixed_at(kind, h):
    return (h // 2, 64 * (h % 2)) if kind == "d" else (4 + h % 8, 64 * (h // 8))


def _channels(v):
    return np.asarray(v).reshape(-1, P).T


def _col_slabs(w):
    k, n = w.shape
    return w.reshape(k // P, P, n // P, P).transpose(2, 1, 0, 3).reshape(n // P, P, SLAB)


def _row_slabs(w):
    return w.reshape(-1, P, SLAB)


def _value_slabs(w):
    return w.reshape(4, 2, P, -1, 512).transpose(3, 0, 2, 1, 4).reshape(-1, P, SLAB)


def _glu_slabs(g, u, d, J):
    out = np.empty((3 * J, P, SLAB), np.float32)
    for j in range(J):
        out[glu_slab(0, J, "g", j)] = g[j]
        out[glu_slab(0, J, "u", j)] = u[j]
        out[glu_slab(0, J, "d", j)] = d[j]
    return out


def _taps(w):
    k = w.shape[0]
    return w.reshape(k, -1, P).transpose(2, 1, 0).reshape(P, -1)


def _layout(i):
    a = {k: np.asarray(v) for k, v in i.items()}
    w_in = a["ab_w_in"][0]
    gates = np.zeros((4, P, SLAB), np.float32)
    for n in range(4):
        for e in range(2):
            gates[n, :, (2 * e) * P:(2 * e + 1) * P] = a["a_gate_x_w"][0, 2 * n + e]
            gates[n, :, (2 * e + 1) * P:(2 * e + 2) * P] = a["a_gate_a_w"][0, 2 * n + e]
        gates[n, :, 4 * P:5 * P] = a["b_group_w"][0, n]
    pw1 = _col_slabs(a["c_w_pw1"][0])
    pw1 = np.stack([pw1[:8], pw1[8:]], 1).reshape(16, P, SLAB)
    w2 = a["w_in_2"][0]
    at = np.cumsum([0, 1536, 1536, 1536, 1024, 128, 128, 1024, 1024])
    qd, kd, vd, qs, ks, vs, gd, gs = (w2[:, at[n]:at[n + 1]] for n in range(8))
    qs = qs.reshape(D, 2, 8, 64).transpose(0, 2, 1, 3).reshape(D, D)
    win = [_col_slabs(qd), _col_slabs(kd), _col_slabs(qs), _value_slabs(vd), _col_slabs(ks), _col_slabs(vs),
           _col_slabs(gd), _col_slabs(gs)]
    br_swa = a["w_br_swa_2"][0].reshape(2, 8, 64, D).transpose(1, 0, 2, 3).reshape(D, D)
    about = _row_slabs(a["ab_w_out"][0])[[8, 9, 10, 11, 0, 1, 2, 3, 4, 5, 6, 7]]

    def ffn(l):
        up = _col_slabs(a["f_w_up"][l])
        return _glu_slabs(up[:FJ], up[FJ:], _row_slabs(a["f_w_down"][l]), FJ)

    eg = np.concatenate([_col_slabs(a["w_e_gate_2"][0, e]) for e in range(NE)])
    eu = np.concatenate([_col_slabs(a["w_e_up_2"][0, e]) for e in range(NE)])
    parts = [_col_slabs(w_in), _col_slabs(a["xa_wk"][0]), gates, _value_slabs(a["xa_wv"][0]), about,
             _col_slabs(a["xa_wq"][0]), _row_slabs(a["xa_wo"][0]), ffn(0), pw1, _col_slabs(a["xa_wk"][1]),
             _value_slabs(a["xa_wv"][1]), _row_slabs(a["c_w_pw2"][0]), _col_slabs(a["xa_wq"][1]),
             _row_slabs(a["xa_wo"][1]), ffn(1), *win, _row_slabs(a["w_br_dil_2"][0]), _row_slabs(br_swa),
             _row_slabs(a["w_out_2"][0]), _glu_slabs(eg, eu, _row_slabs(a["w_e_down_2"][0]), MJ)]
    stream = np.concatenate(parts)
    assert stream.shape == (NSLAB, P, SLAB), stream.shape
    rows = np.broadcast_to
    cols = {"ab_norm": _channels(a["ab_norm"][0]), "a_conv_w": _taps(a["a_conv_w"][0]),
            "a_conv_b": _channels(a["a_conv_b"][0]), "a_gate_x_b": _channels(a["a_gate_x_b"][0]),
            "a_gate_a_b": _channels(a["a_gate_a_b"][0]), "a_lambda": _channels(a["a_lambda"][0]),
            "b_group_b": _channels(a["b_group_b"][0]), "b_scale": _channels(a["b_scale"][0]),
            "c_norm": _channels(a["c_norm"][0]), "c_b_pw1": _channels(a["c_b_pw1"][0]),
            "c_dw_w": _taps(a["c_dw_w"][0]), "c_dw_b": _channels(a["c_dw_b"][0]),
            "c_ln_g": _channels(a["c_ln_g"][0]), "c_ln_b": _channels(a["c_ln_b"][0]),
            "c_b_pw2": _channels(a["c_b_pw2"][0]),
            "final_norm": _channels(a["final_norm"]), "g_mix": _channels(a["g_mix_2"][0]),
            "g_ffn": _channels(a["g_ffn_2"][0]), "g_final": _channels(a["g_final_2"]),
            "sinks": rows(a["sinks_2"][0], (P, 16)),
            "r_bias": rows(np.concatenate([a["b_group_2"][0], a["b_router_2"][0]]), (P, 36))}
    for l in range(2):
        cols[f"xa_norm{l}"] = _channels(a["xa_norm"][l])
        cols[f"mem_norm{l}"] = _channels(a["xa_mem_norm"][l])
        cols[f"f_norm{l}"] = _channels(a["f_norm"][l])
        cols[f"f_dw_w{l}"] = _taps(a["f_dw_w"][l])
        cols[f"f_dw_b{l}"] = _channels(a["f_dw_b"][l])
    packed = np.concatenate([cols[name] for name, _ in COLS], 1)
    tok = np.arange(T)
    inv = np.stack([1.0 / np.minimum(tok + 1, w) for w in POOLS]).reshape(1, -1)
    konst = np.concatenate([np.eye(P), np.broadcast_to(inv, (P, 4 * T))], 1).astype(np.float32)
    dist = tok[:, None] - tok[None, :]
    kinds = [(dist >= 0) & (dist <= 128), (dist >= 0) & (dist % 4 == 0), (dist >= 0) & (dist % 16 == 0),
             (dist >= 0) & (dist <= 127)]
    masks = np.empty((P, 4, 3 * P), np.float32)
    for n, ok in enumerate(kinds):
        m = np.where(ok, dist, -NEG)
        masks[:, n, :P] = m[:P, :P]
        masks[:, n, P:] = m[P:, :]
    def turned(v):
        return np.ascontiguousarray(np.asarray(v)[0].T.reshape(KC, P, T).transpose(1, 0, 2))

    router = np.concatenate([a["w_group_2"][0], a["w_router_2"][0]], 1).reshape(KC, P, 36).transpose(1, 0, 2)
    return {"stream": stream, "cols": packed, "konst": konst, "masks": masks, "x": turned(a["x"]),
            "mem": turned(a["mem"]), "router": router}


def kernel(**inputs):
    import concourse.bacc as bacc
    from concourse.bass_utils import run_bass_kernel_spmd

    nc = bacc.Bacc("TRN2", target_bir_lowering=False, num_devices=1)
    arrays, args = {}, []
    for name, a in _layout(inputs).items():
        arrays[f"in_{name}"] = np.ascontiguousarray(a)
        args.append(nc.dram_tensor(f"in_{name}", a.shape, F32, kind="ExternalInput").ap())
    args.append(nc.dram_tensor("out", (P, KC, T), F32, kind="ExternalOutput").ap())
    program(nc, *args)
    got = run_bass_kernel_spmd(nc, [arrays], core_ids=[0]).results[0]["out"]
    return got.transpose(1, 0, 2).reshape(D, T).T[None]
```

```python
from contextlib import ExitStack, contextmanager

import numpy as np

import concourse.bass as bass
from concourse import mybir

F32 = mybir.dt.float32
F32R = mybir.dt.float32r
ACT = mybir.ActivationFunctionType
ALU = mybir.AluOpType
AX = mybir.AxisListType

P = 128
T = 256
TT = T // P
D = 1024
KC = D // P
SLAB = 1024
EPS = 1e-6
NEG = -1e30
FF = 3 * D
FJ = FF // P
NE = 32
DE = 512
CAP = 64
PAIRS_E = NE // 2
EXPERT = 12
CONV_A, CONV_C, CONV_F = 4, 31, 3
XH = 4
POOLS = (2, 4, 8, 16)
RAW = 12
SPLIT = 4
AHEAD = 3
SLOPES_DIL = [2.0 ** (-8.0 * (h + 1) / 24) for h in range(24)]
SLOPES_SWA = [2.0 ** (-8.0 * (h + 1) / 16) for h in range(16)]

PHASES = [("abin", 20), ("k0", 8), ("gates", 4), ("v0", 8), ("about", 12), ("q0", 8), ("wo0", 8),
          ("f0", 3 * FJ), ("pw1", 16), ("k1", 8), ("v1", 8), ("pw2", 8), ("q1", 8), ("wo1", 8),
          ("f1", 3 * FJ), ("win", 62), ("brd", 4), ("brs", 8), ("wout", 8), ("moe", EXPERT * NE)]
S0, _n = {}, 0
for _name, _k in PHASES:
    S0[_name] = _n
    _n += _k
NSLAB = _n

COLS = [("ab_norm", 8), ("a_conv_w", 8 * CONV_A), ("a_conv_b", 8), ("a_gate_x_b", 8), ("a_gate_a_b", 8),
        ("a_lambda", 8), ("b_group_b", 4), ("b_scale", 4), ("c_norm", 8), ("c_b_pw1", 16),
        ("c_dw_w", 8 * CONV_C), ("c_dw_b", 8), ("c_ln_g", 8), ("c_ln_b", 8), ("c_b_pw2", 8),
        ("xa_norm0", 8), ("xa_norm1", 8), ("mem_norm0", 8), ("mem_norm1", 8), ("f_norm0", 8), ("f_norm1", 8),
        ("f_dw_w0", FJ * CONV_F), ("f_dw_w1", FJ * CONV_F), ("f_dw_b0", FJ), ("f_dw_b1", FJ),
        ("final_norm", 8), ("g_mix", 8), ("g_ffn", 8), ("g_final", 8), ("sinks", 16), ("r_bias", 36)]
C0, _n = {}, 0
for _name, _k in COLS:
    C0[_name] = _n
    _n += _k
NCOL = _n

USES, USE0 = [], {}


def _uses(name, who):
    USE0[name] = len(USES)
    USES.extend(who)


def _attn_uses(n):
    out = []
    for h in range(n + 1):
        if h < n:
            out += ["a", "a"]
        if h >= 1:
            out += ["a", "a", "v"]
    return out


HEADS2 = [("d", h) for h in range(8)] + [("s", h) for h in range(16)]


def groups(kind):
    return 3 if kind == "d" else 1


def _attn2_uses():
    out = []
    for n in range(len(HEADS2) + 1):
        if n < len(HEADS2):
            out += ["v"] * (2 * groups(HEADS2[n][0]))
        if n >= 1:
            out += ["a"] * groups(HEADS2[n - 1][0]) + ["v"]
    return out


_uses("abin", "v" * 20)
_uses("k0", "v" * 8)
_uses("gates", "aav" * 4)
_uses("v0", "v" * 4)
_uses("q0", "v" * 8)
_uses("x0", _attn_uses(XH))
_uses("f0", "vv" * FJ)
_uses("pw1", "v" * 16)
_uses("k1", "v" * 8)
_uses("v1", "v" * 4)
_uses("q1", "v" * 8)
_uses("x1", _attn_uses(XH))
_uses("f1", "vv" * FJ)
_uses("win", "v" * (32 + 6 + 3 + 16))
_uses("attn2", _attn2_uses())


def emptied(u, who=None):
    who = who or USES[u]
    return sum(1 for w in USES[:u + 1] if w == who)


MM0 = {}
_n = 0
for _name, _k in (("x0", len(_attn_uses(XH))), ("x1", len(_attn_uses(XH))), ("attn2", len(_attn2_uses()))):
    MM0[_name] = _n
    _n += _k

NORMS = {n: i for i, n in enumerate(
    ["ab", "mem", "xa0", "f0", "c", "lnmean", "ln", "xa1", "f1", "final", "mix", "moe", "out"])}
PAIRS = {n: i for i, n in enumerate(["abin", "q0", "f0", "pw1", "q1", "f1", "win", "moe"])}
ACCS = {n: i for i, n in enumerate(["about", "wo0", "f0", "pw2", "wo1", "f1", "brd", "brs", "wout", "moe"])}

KB = 1024
MAP = [("raw", 48), ("wh", 16), ("wl", 16), ("x", 8), ("ah", 8), ("al", 8), ("mh", 8), ("ml", 8),
       ("yh", 12), ("yl", 12), ("arena", 46), ("konst", 6.5), ("cols", 3.25), ("tmp", 7), ("memr", 1)]
OFF, _o = {}, 0
for _name, _k in MAP:
    OFF[_name] = _o
    _o += int(_k * KB)


def glu_slab(base, J, kind, j):
    if kind == "d":
        return base + (6 + 3 * j if j <= J - 3 else 3 * J - (J - j))
    g = 2 * j if j < 2 else 4 + 3 * (j - 2)
    return base + g + (kind == "u")


class At:

    def __init__(self, base, step=0, i=None):
        self.base, self.step, self.i = base, step, i

    def __add__(self, k):
        return At(self.base + k, self.step, self.i)

    def of(self, f):
        a = f(self.base)
        if self.i is None:
            return a
        return self.i * (f(self.base + self.step) - a) + a


class Program:

    def __init__(self, eng, chain):
        self.eng, self.chain, self.count, self.last = eng, chain, {}, None

    def done(self, ins, sem=None):
        sem = self.chain if sem is None else sem
        if self.last is not None:
            self.before = (self.last, self.count[self.last.name])
        ins.then_inc(sem, 1)
        base, k = self.count.get(sem.name, (None, 0))
        self.count[sem.name] = (base, k + 1)
        self.last = sem

    def fence(self, back=0):
        if self.last is not None:
            sem, (base, k) = self.before if back else (self.last, self.count[self.last.name])
            self.eng.wait_ge(sem, k if base is None else base + k)

    @contextmanager
    def loop(self, trips, raised, last):
        self.fence()
        before = {s.name: self.count.get(s.name, (None, 0))[1] for s in raised}
        with self.eng.Fori(0, trips) as i:
            for s, k in raised.items():
                self.count[s.name] = (i * k + before[s.name], 0)
            self.last = last
            yield i
            for s, k in raised.items():
                assert self.count[s.name][1] == k, (s.name, self.count[s.name][1], k)
        for s, k in raised.items():
            self.count[s.name] = (None, before[s.name] + k * trips)
        self.last = last


def program(nc, stream, cols_in, konst_in, masks_in, x_in, mem_in, router_in, out):
    ctx = ExitStack()
    with ctx:
        first_free = (nc.sbuf_base + 63) // 64 * 64

        def sb(name, where, at_kb, shape, dt=F32):
            return nc.alloc_sbuf_tensor_at(name, shape, dt, offset=first_free + OFF[where] + int(at_kb * KB))

        sems = {}

        def S(name):
            if name not in sems:
                sems[name] = ctx.enter_context(nc.semaphore(name))
            return sems[name]

        raw = sb("raw", "raw", 0, [P, RAW, SLAB])
        wh = sb("wh", "wh", 0, [P, SPLIT, SLAB], F32R)
        wl = sb("wl", "wl", 0, [P, SPLIT, SLAB], F32R)
        x = sb("x_res", "x", 0, [P, KC, T])
        ah = sb("ah", "ah", 0, [P, KC, T], F32R)
        al = sb("al", "al", 0, [P, KC, T], F32R)
        mh = sb("mh", "mh", 0, [P, KC, T], F32R)
        ml = sb("ml", "ml", 0, [P, KC, T], F32R)
        yh = sb("yh", "yh", 0, [P, 12, T], F32R)
        yl = sb("yl", "yl", 0, [P, 12, T], F32R)
        mem = sb("mem_t", "yh", 4, [P, KC, T])
        cols = sb("cols", "cols", 0, [P, NCOL])
        ident = sb("ident", "konst", 0, [P, P])
        inv = sb("inv_count", "konst", 0.5, [P, 4, T])
        masks = sb("masks", "konst", 0.5, [P, 4, 3 * P])
        q_t = sb("q_t", "arena", 0, [P, KC, T])
        sq = sb("sq", "arena", 0, [P, KC, T])
        k_t = sb("k_t", "arena", 8, [P, KC, T])
        v_m = sb("v_m", "arena", 16, [P, TT, D])
        z = sb("z", "arena", 24, [P, 20, T])
        xr = sb("xr", "ah", 0, [P, KC, T])
        a_t = sb("a_t", "al", 0, [P, KC, T])
        pt = sb("pt", "arena", 24, [P, 2, TT, T])
        prob = sb("prob", "arena", 28, [P, 2, TT, T])
        hpad = sb("hpad", "arena", 24, [P, KC, T + CONV_C - 1])
        cv = sb("cv", "arena", 34, [P, KC, T])
        gpad = sb("gpad", "arena", 24, [P, 2, T + 2])
        cf = sb("cf", "arena", 27, [P, 2, T])
        uf = sb("uf", "arena", 29, [P, 2, T])
        hid = sb("hid", "arena", 31, [P, 2, T])
        q2 = sb("q2", "arena", 0, [P, 20, T])
        k2 = sb("k2", "arena", 20, [P, 13, T])
        v2 = sb("v2", "arena", 33, [P, TT, 1664])
        gt = sb("gt", "mh", 0, [P, 16, T])
        sc = sb("sc", "ah", 0, [P, 2, 9 * P])
        pt2 = sb("pt2", "ah", 9, [P, 3, 3 * P])
        hf = sb("hf", "arena", 37, [P, KC, T])
        htok_hi = sb("h_by_token_hi", "arena", 0, [P, TT, D], F32R)
        htok_lo = sb("h_by_token_lo", "arena", 8, [P, TT, D], F32R)
        onehot = sb("onehot", "arena", 16, [P, 2, TT, 4 * CAP], F32R)
        silu = sb("silu", "arena", 20, [P, DE])
        hide = sb("hidden_e", "arena", 22, [P, DE])
        ht_hi = sb("hidden_turned_hi", "arena", 24, [P, DE // P, 3 * CAP], F32R)
        ht_lo = sb("hidden_turned_lo", "arena", 27, [P, DE // P, 3 * CAP], F32R)
        back = sb("slots_to_tokens", "arena", 30, [P, 2, T], F32R)
        xg_hi = sb("gathered_hi", "ah", 0, [P, 2, 2 * KC, 3 * CAP], F32R)
        xg_lo = sb("gathered_lo", "ah", 24, [P, 2, 2 * KC, 3 * CAP], F32R)
        ye_hi = sb("expert_out_hi", "yl", 4, [P, D], F32R)
        ye_lo = sb("expert_out_lo", "yl", 8, [P, D], F32R)
        dense_silu = sb("dense_silu", "arena", 0, [P, TT, DE])
        dense_hid = sb("dense_hidden", "arena", 4, [P, TT, DE])
        dense_turned = sb("dense_turned", "arena", 8, [P, DE // P, T])
        zeros = sb("zeros", "arena", 45, [P, T], F32R)
        rk = sb("router_konst", "konst", 0.5, [P, KC * 36 + P + CAP])
        rw = rk[:, 0:KC * 36].rearrange("p (k n) -> p k n", k=KC)
        until = rk[:, KC * 36:KC * 36 + P]
        slot_no = rk[:, KC * 36 + P:KC * 36 + P + CAP]
        place = sb("place", "konst", 2.5, [P, TT, NE])
        gates = sb("gates", "konst", 2.75, [P, TT, NE])
        chosen = sb("chosen", "konst", 3, [P, TT, NE])
        slot_gate = sb("slot_gate", "konst", 3.25, [P, 2])
        most = sb("most", "konst", 3.375, [P, 1])
        overflow = sb("overflow", "konst", 3.5, [P, 1], mybir.dt.int32)
        lg = sb("logits", "konst", 5, [P, TT, 36])
        rt = sb("router_tmp", "konst", 5.5, [P, 96])
        ones = sb("ones", "tmp", 0, [P, P])
        t = [sb(f"t{n}", "tmp", 0.5 + n, [P, T]) for n in range(5)]
        diag = sb("diag", "tmp", 4.5, [P, TT, P])
        rstd_b = sb("rstd_b", "tmp", 5.5, [P, T])
        sm = sb("small", "tmp", 6.5, [P, 128])
        ms, rcol, mhalf = sm[:, 0:2], sm[:, 2:4], sm[:, 4:6]
        nmax, den, rec, esink = sm[:, 6:8], sm[:, 8:10], sm[:, 10:12], sm[:, 12:14]
        sp8, n4sp, p4sp, hbx, hba, hbc = (sm[:, 16 + 8 * n:24 + 8 * n] for n in range(6))
        nsink = sm[:, 64:80]
        lam_a, lam_e, lam_z, lam_q = (sm[:, 80 + 8 * n:88 + 8 * n] for n in range(4))

        mem_rstd = sb("mem_rstd", "memr", 0, [P, T])

        pw = [ctx.enter_context(nc.psum_tensor(f"pw{n}", [P, 512], F32)) for n in range(4)]
        acc = [ctx.enter_context(nc.psum_tensor(f"acc{n}", [P, 512], F32)) for n in range(4)]

        def acc_of(n):
            return acc[n // 2][:, (n % 2) * T:(n % 2) * T + T]

        def col(name, n=0, step=0, i=None):
            if i is None:
                return cols[:, C0[name] + n:C0[name] + n + 1]
            return cols[:, bass.ds(i * step + (C0[name] + n), 1)]

        raw_in = [S(f"raw_in{n}") for n in range(RAW)]
        w_hi, w_lo_v, w_lo_p = S("w_hi"), S("w_lo_vector"), S("w_lo_pool")
        slab_done, mm_done = S("slab_done"), S("products_done")
        empty_v, empty_a = S("bank_emptied_vector"), S("bank_emptied_scalar")
        acc_full, acc_out = S("sum_full"), S("sum_taken")
        sq_ready, stat_full, ms_ready = S("squares"), S("sums_full"), S("mean_square")
        rstd_ready, diag_ready, bc_full = S("rstd_column"), S("diagonal"), S("spread_full")
        rstd_b_ready = S("rstd_spread")
        pair_hi, pair_lo = S("a_hi"), S("a_lo")
        block = ctx.enter_context(nc.Block())

        def wait_split(eng, s):
            if s.base % 2 == 0:
                eng.wait_ge(w_lo_v, s.of(lambda n: n // 2 + 1))
            else:
                eng.wait_ge(w_lo_p, s.of(lambda n: (n + 1) // 2))

        def wait_slab(eng, s):
            eng.wait_ge(slab_done, s.of(lambda n: n + 1))

        def wait_emptied(eng, u):
            eng.wait_ge(empty_v if USES[u] == "v" else empty_a, emptied(u))

        def wait_acc(eng, phase, n):
            n |= 1
            if n < KC - 1:
                eng.wait_ge(acc_full, (KC - 1) * ACCS[phase] + n + 1)
            else:
                wait_slab(eng, At(S0[phase] + dict(PHASES)[phase] - 1))

        def wait_new_x(eng, phase, c):
            eng.wait_ge(acc_out, KC * ACCS[phase] + c + 1)

        def gather_bank(j):
            return j if j < 4 else 3 - j % 2

        def both_of_pairs(tile):
            return tile.rearrange("p n (t s) -> p n t s", t=3)[:, :, 0:3:2, :]

        def gu_slab(p):
            return S0["moe"] + (24 * p - 8 if p else 0)

        def moe_schedule(prog, raised, last, period):
            period(0, None)
            period(1, None)
            with prog.loop(3, raised, last) as i:
                for p in range(2, 6):
                    period(p, i)
            period(14, None)
            period(15, None)

        def per_trip(p, i):
            return At(p, 4 if i is not None else 0, i)

        def glu_steps(J):
            trips = (J - 6) // 4
            return trips, 4 + 4 * trips

        @block.sync
        def _(sp):
            def load(s, d=None):
                b, d = s.base, d or s
                if b >= RAW:
                    wait_split(sp, s + -RAW)
                src = stream[d.base] if d.i is None else \
                    stream[bass.ds(d.i * d.step + d.base, 1), :, :].rearrange("a p n -> (a p) n")
                sp.dma_start(raw[:, b % RAW, :], src).then_inc(raw_in[b % RAW], 16)

            for s in range(2 * RAW):
                load(At(s))
            trips = S0["moe"] // RAW - 2
            with sp.Fori(0, trips) as i:
                for j in range(RAW):
                    load(At(2 * RAW + j, RAW, i))
            for s in range(RAW * (trips + 2), S0["moe"]):
                load(At(s))

            def inputs_at(p):
                return [S0["moe"] + EXPERT * (2 * p + e) + k for e in range(2) for k in range(8)]

            def outputs_at(p):
                return [S0["moe"] + EXPERT * (2 * p + e) + 8 + k for e in range(2) for k in range(4)]

            for n, d in enumerate(inputs_at(0)):
                load(At(S0["moe"] + n), At(d))
            with sp.Fori(0, PAIRS_E - 1) as i:
                for n, d in enumerate(inputs_at(1) + outputs_at(0)):
                    load(At(S0["moe"] + 16 + n, 24, i), At(d, 24, i))
            for n, d in enumerate(outputs_at(PAIRS_E - 1)):
                load(At(NSLAB - 8 + n), At(d))

            sp.wait_ge(S("overflow_known"), 1)
            over = sp.value_load(overflow[0:1, 0:1], min_val=0, max_val=1)
            with sp.If(over > 0):
                for s in range(NSLAB - 2, NSLAB):
                    wait_split(sp, At(s))
                with sp.Fori(0, NE) as i:
                    sp.wait_ge(S("dense_down"), i + 1)
                    for j in range(EXPERT):
                        sp.dma_start(raw[:, j, :], stream[bass.ds(i * EXPERT + (S0["moe"] + j), 1), :, :]
                                     .rearrange("a p n -> (a p) n")).then_inc(S("dense_in"), 16)
            sp.wait_ge(S("x_final"), KC)
            sp.dma_start(out, x[:]).then_inc(S("out_done"), 16)
            sp.wait_ge(S("out_done"), 16)

        @block.scalar
        def _(act):
            A = Program(act, S("scalar_chain"))

            def split(s):
                if s.base >= NSLAB:
                    return
                act.wait_ge(raw_in[s.base % RAW], s.of(lambda n: 16 * (n // RAW + 1)))
                if s.base >= SPLIT:
                    wait_slab(act, s + -SPLIT)
                A.done(act.activation(wh[:, s.base % SPLIT, :], raw[:, s.base % RAW, :], ACT.Copy), w_hi)

            def squares(src, ready, gain=None, name=None):
                for c in range(KC):
                    ready(c)
                    A.done(act.activation(sq[:, c, :], src[:, c, :], ACT.Square), sq_ready)
                    if gain is not None:
                        A.done(act.activation(ah[:, c, :], src[:, c, :], ACT.Copy, scale=col(gain, c)), pair_hi)

            act.dma_start(x[:], x_in).then_inc(S("x_in"), 16)
            act.dma_start(cols[:], cols_in).then_inc(S("const_in"), 16)
            act.dma_start(ident[:], konst_in[:, 0:P]).then_inc(S("const_in"), 16)
            act.dma_start(inv[:], konst_in[:, P:P + 4 * T].rearrange("p (g t) -> p g t", g=4)) \
                .then_inc(S("const_in"), 16)
            act.dma_start(mem[:], mem_in).then_inc(S("mem_in"), 16)
            act.wait_ge(S("const_in"), 48)
            act.wait_ge(S("x_in"), 16)
            squares(x, lambda c: None, "ab_norm")
            for s in range(AHEAD):
                split(At(s))
            act.wait_ge(S("mem_in"), 16)
            act.wait_ge(stat_full, 1)
            squares(mem, lambda c: None)
            A.done(act.activation(lam_a, cols[:, C0["a_lambda"]:C0["a_lambda"] + 8], ACT.Abs), S("decay_abs"))
            A.fence()
            A.done(act.activation(lam_e, lam_a, ACT.Exp, scale=-1.0), S("decay_exp"))

            def mem_pair(l):
                for c in range(KC):
                    act.wait_ge(S("mem_normed"), KC * l + c + 1)
                    A.done(act.activation(mh[:, c, :], mem[:, c, :], ACT.Copy, scale=col(f"mem_norm{l}", c)),
                           S("m_hi"))

            for n in range(20):
                split(At(S0["abin"] + n + AHEAD))
                if n == 9:
                    mem_pair(0)
                if 10 <= n < 18:
                    wait_emptied(act, USE0["abin"] + n - 10)
                    A.done(act.activation(z[:, n - 10, :], z[:, n - 10, :], ACT.Gelu_apprx_tanh), S("gate_gelu"))
            for n in range(8):
                split(At(S0["k0"] + n + AHEAD))
                act.wait_ge(S("xr_ready"), n + 1)
                A.done(act.activation(yh[:, n, :], xr[:, n, :], ACT.Copy), S("xr_hi"))
                if n >= 4:
                    act.wait_ge(S("pooled"), n - 3)
                    A.done(act.activation(yh[:, 4 + n, :], z[:, 12 + n, :], ACT.Copy), S("pooled_hi"))
            act.wait_ge(S("decay"), 1)
            for n in range(4):
                split(At(S0["gates"] + n + AHEAD))
                for h in (2 * n, 2 * n + 1):
                    u = USE0["gates"] + 3 * n + h % 2
                    act.wait_ge(S("gate_products"), h + 1)
                    if h >= 2:
                        act.wait_ge(S("root_in"), h - 1)
                    A.fence()
                    A.done(act.activation(t[h % 2][:], pw[u % 4][:, 0:T], ACT.Tanh, bias=hbx[:, h:h + 1], scale=0.5))
                    A.done(act.activation(t[2 + h % 2][:], pw[u % 4][:, T:2 * T], ACT.Tanh, bias=hba[:, h:h + 1],
                                          scale=0.5), empty_a)
                    A.fence()
                    A.done(act.activation(a_t[:, h, :], t[2 + h % 2][:], ACT.Exp, bias=n4sp[:, h:h + 1],
                                          scale=n4sp[:, h:h + 1]))
                    A.done(act.activation(z[:, 8 + h, :], t[2 + h % 2][:], ACT.Tanh, bias=p4sp[:, h:h + 1],
                                          scale=p4sp[:, h:h + 1]), S("gates_through"))
                wait_emptied(act, USE0["gates"] + 3 * n + 2)
                A.done(act.activation(yh[:, 8 + n, :], z[:, 16 + n, :], ACT.Copy), S("yb_hi"))
            act.wait_ge(S("root_in"), 8)
            A.done(act.activation(z[:, 8:16, :], z[:, 8:16, :], ACT.Sqrt, scale=0.25), S("root"))
            for n in range(8):
                split(At(S0["v0"] + n + AHEAD))
                act.wait_ge(S("ya_ready"), n + 1)
                A.done(act.activation(yh[:, n, :], xr[:, n, :], ACT.Copy), S("ya_hi"))
            act.dma_start(masks[:], masks_in).then_inc(S("masks_in"), 16)

            def row_splits(phase):
                for n in range(dict(PHASES)[phase]):
                    split(At(S0[phase] + n + AHEAD))

            def cross(l):
                name, n_u = f"x{l}", USE0[f"x{l}"]
                for h in range(XH + 1):
                    if h < XH:
                        for qt in range(TT):
                            r, b = 2 * h + qt, pw[(n_u + x_score(h) + qt) % 4]
                            act.wait_ge(S(name + "_max"), r + 1)
                            A.done(act.activation(prob[:, h % 2, qt, :], b[:, 0:T], ACT.Exp,
                                                  bias=nmax[:, qt:qt + 1], accum_out=den[:, qt:qt + 1]), empty_a)
                    if h >= 1:
                        for qt in range(TT):
                            k = x_turn(h - 1) + qt
                            act.wait_ge(mm_done, MM0[name] + k + 1)
                            A.done(act.activation(pt[:, (h - 1) % 2, :, qt * P:qt * P + P],
                                                  pw[(n_u + k) % 4][:, 0:T].rearrange("p (a q) -> p a q", a=TT),
                                                  ACT.Copy), empty_a)
                        k = x_turn(h - 1) + 2
                        act.wait_ge(mm_done, MM0[name] + k + 1)
                        A.done(act.activation(yh[:, 2 * h - 2:2 * h, :],
                                              pw[(n_u + k) % 4][:, :].rearrange("p (a q) -> p a q", a=2),
                                              ACT.Copy), S(name + "_hi"))

            def glu(name, J):
                base = S0[name]

                def step(j, i=None):
                    def slab(kind):
                        return At(glu_slab(base, J, kind, j), 12 if i is not None else 0, i)
                    jj = At(j, 4 if i is not None else 0, i)
                    split(slab("g") + AHEAD)
                    split(slab("u") + AHEAD)
                    act.wait_ge(S(name + "_conv"), (jj + 1).of(lambda n: n))
                    A.done(act.activation(cf[:, j % 2, :], cf[:, j % 2, :], ACT.Gelu_apprx_tanh), S(name + "_act"))
                    if j >= 2:
                        split(At(slab("u").base + 1 + AHEAD, 12 if i is not None else 0, i))
                    act.wait_ge(S(name + "_hidden"), (jj + 1).of(lambda n: n))
                    A.done(act.activation(yh[:, j % 4, :], hid[:, j % 2, :], ACT.Copy), S(name + "_hid_hi"))

                trips, rest = glu_steps(J)
                for j in range(4):
                    step(j)
                raised = {w_hi: 12, S(name + "_hid_hi"): 4, S(name + "_act"): 4}
                with A.loop(trips, raised, S(name + "_hid_hi")) as i:
                    for j in range(4, 8):
                        step(j, i)
                for j in range(rest, J):
                    step(j)
                for n in range(2):
                    split(At(base + 3 * J - 2 + n + AHEAD))

            row_splits("about")
            squares(x, lambda c: wait_new_x(act, "about", c), "xa_norm0")
            row_splits("q0")
            cross(0)
            row_splits("wo0")
            squares(x, lambda c: wait_new_x(act, "wo0", c), "f_norm0")
            act.dma_start(mem[:], mem_in).then_inc(S("mem_again"), 16)
            glu("f0", FJ)
            squares(x, lambda c: wait_new_x(act, "f0", c), "c_norm")
            def glu_tanh(c):
                wait_emptied(act, USE0["pw1"] + 2 * c + 1)
                tb = t[2 * (c % 2) + 1][:]
                A.done(act.activation(tb, tb, ACT.Tanh, bias=hbc[:, c:c + 1], scale=0.5), S("glu_tanh"))

            for n in range(16):
                split(At(S0["pw1"] + n + AHEAD))
                if n % 2 == 0 and n >= 2:
                    glu_tanh(n // 2 - 1)
                if n == 10:
                    mem_pair(1)
            glu_tanh(7)
            row_splits("k1")
            row_splits("v1")
            squares(cv, lambda c: act.wait_ge(S("ln_centred"), c + 1))
            for c in range(KC):
                act.wait_ge(S("ln_scaled"), c + 1)
                A.done(act.activation(cv[:, c, :], cv[:, c, :], ACT.Silu, bias=col("c_ln_b", c),
                                      scale=col("c_ln_g", c)), S("ln_silu"))
                A.fence()
                A.done(act.activation(yh[:, c, :], cv[:, c, :], ACT.Copy), S("ln_hi"))
            row_splits("pw2")
            squares(x, lambda c: wait_new_x(act, "pw2", c), "xa_norm1")
            row_splits("q1")
            cross(1)
            row_splits("wo1")
            squares(x, lambda c: wait_new_x(act, "wo1", c), "f_norm1")
            glu("f1", FJ)
            squares(x, lambda c: wait_new_x(act, "f1", c))
            squares(x, lambda c: act.wait_ge(S("x_normed"), c + 1), "g_mix")
            for n in range(62):
                split(At(S0["win"] + n + AHEAD))
                if n >= 46:
                    wait_emptied(act, USE0["win"] + n - 46 + 41)
                    A.done(act.activation(gt[:, n - 46, :], gt[:, n - 46, :], ACT.Tanh, scale=0.5), S("mix_gates"))
            for m in range(len(HEADS2) + 1):
                if m < len(HEADS2):
                    kind, h = HEADS2[m]
                    for qt in range(TT):
                        at, n = (0, P) if qt == 0 else (3 * P, 2 * P)
                        act.wait_ge(S("attn2_max"), 2 * m + qt + 1)
                        s_ap = sc[:, m % 2, at:at + n * groups(kind)]
                        A.fence()
                        if kind == "s":
                            A.done(act.activation(esink[:, qt:qt + 1], col("sinks", h), ACT.Exp,
                                                  bias=nmax[:, qt:qt + 1]))
                        A.done(act.activation(s_ap, s_ap, ACT.Exp, bias=nmax[:, qt:qt + 1],
                                              accum_out=den[:, qt:qt + 1]), S("attn2_exp"))
                if m >= 1:
                    kind, h = HEADS2[m - 1]
                    for g in range(groups(kind)):
                        k = a_turn(m - 1) + g
                        act.wait_ge(mm_done, MM0["attn2"] + k + 1)
                        A.done(act.activation(pt2[:, g, :], pw[(USE0["attn2"] + k) % 4][:, 0:3 * P], ACT.Copy),
                               empty_a)
                    k = a_turn(m - 1) + groups(kind)
                    c, half = mixed_at(kind, h)
                    act.wait_ge(mm_done, MM0["attn2"] + k + 1)
                    A.done(act.activation(yh[half:half + 64, c, :], pw[(USE0["attn2"] + k) % 4][half:half + 64, 0:T],
                                          ACT.Copy), S("attn2_hi"))
            act.dma_start(rk[:], router_in).then_inc(S("router_in"), 16)
            row_splits("brd")
            row_splits("brs")
            for c in range(KC):
                act.wait_ge(S("mixed"), c + 1)
                A.done(act.activation(yh[:, c, :], gt[:, c, :], ACT.Copy, scale=0.5), S("mixed_hi"))
            row_splits("wout")
            squares(x, lambda c: wait_new_x(act, "wout", c))
            for j in range(4):
                act.wait_ge(S("h_turned"), j + 1)
                A.done(act.activation(htok_hi[:, j // 2, 512 * (j % 2):512 * (j % 2) + 512], pw[j][:, :], ACT.Copy),
                       S("h_turned_hi"))
            for q in range(TT):
                act.wait_ge(S("group_max"), q + 1)
                A.fence()
                A.done(act.activation(rt[:, 4:8], lg[:, q, 0:4], ACT.Exp, bias=rt[:, 0:1], accum_out=rt[:, 1:2]),
                       S("group_exp"))
                act.wait_ge(S("expert_gap"), q + 1)
                A.done(act.activation(rt[:, 2:3], rt[:, 3:4], ACT.Exp), S("expert_exp"))

            def gather_hi(j):
                act.wait_ge(S("gathered"), (j + 1).of(lambda n: n))
                c = 4 * (j.base % 4)
                A.done(act.activation(both_of_pairs(xg_hi[:, j.base // 4 % 2, c:c + 4, :]),
                                      pw[gather_bank(j.base)][:, :].rearrange("p (n e s) -> p n e s", n=4, e=2),
                                      ACT.Copy), S("gathered_hi"))

            def y_hi(p, i, h):
                if h == 0:
                    wait_slab(act, At(gu_slab(p + 1) + 23, 96 if i is not None else 0, i) if p + 1 < PAIRS_E
                              else At(NSLAB - 1))
                A.done(act.activation(ye_hi[:, 512 * h:512 * h + 512], pw[2 + h][:, :], ACT.Copy), S("expert_out_hi"))

            def turned_hi(p):
                act.wait_ge(S("hidden_turned"), (p + 1).of(lambda n: n))
                A.done(act.activation(both_of_pairs(ht_hi[:]), pw[2][:, :].rearrange("p (n e s) -> p n e s", n=4, e=2),
                                      ACT.Copy), S("hidden_turned_hi"))

            def back_out(p):
                act.wait_ge(S("slots_turned"), (p + 1).of(lambda n: n))
                A.done(act.activation(back[:, p.base % 2, :], pw[3][:, 0:T], ACT.Copy), S("slots_turned_out"))

            def period(p, i):
                pp = per_trip(p, i)
                for n in range(24 if p else 16):
                    s = At(gu_slab(p) + n, 96 if i is not None else 0, i)
                    split(s + AHEAD)
                    if p >= 2 and n < 2:
                        y_hi(p - 2, i, n)
                    if p >= 1 and n == 4:
                        turned_hi(pp + -1)
                    if p < 14 and n in (8, 10):
                        gather_hi(At(4 + 2 * p + (n == 10), 8 if i is not None else 0, i))
                    if n == 12:
                        back_out(pp)
                    if n == 15:
                        wait_slab(act, s)
                        if p:
                            act.wait_ge(S("hidden_done"), pp.of(lambda n: n))
                        A.done(act.activation(silu[:], pw[0][:, :], ACT.Silu), S("silu"))

            for j in range(4):
                gather_hi(At(j))
            moe_schedule(A, {w_hi: 96, S("expert_out_hi"): 8, S("hidden_turned_hi"): 4, S("gathered_hi"): 8,
                             S("slots_turned_out"): 4, S("silu"): 4}, w_hi, period)
            last = PAIRS_E - 1
            split(At(NSLAB - 8 + AHEAD))
            y_hi(last - 1, None, 0)
            y_hi(last - 1, None, 1)
            turned_hi(At(last))
            for n in range(1, 8):
                split(At(NSLAB - 8 + n + AHEAD))
            y_hi(last, None, 0)
            y_hi(last, None, 1)
            act.wait_ge(S("overflow_known"), 1)
            over = act.value_load(overflow[0:1, 0:1], min_val=0, max_val=1)
            with act.If(over > 0):
                with act.Fori(0, NE) as i:
                    act.wait_ge(S("dense_products"), i + 1)
                    for q in range(TT):
                        act.activation(dense_silu[:, q, :], pw[2 * q][:, :], ACT.Silu).then_inc(S("dense_silu"), 1)
                    act.wait_ge(S("dense_turns"), i + 1)
                    for n in range(2):
                        act.activation(dense_turned[:, 2 * n:2 * n + 2, :],
                                       pw[n][:, :].rearrange("p (c t) -> p c t", c=2), ACT.Copy) \
                            .then_inc(S("dense_turned"), 1)
            squares(x, lambda c: wait_new_x(act, "moe", c))

        @block.gpsimd
        def _(pool):
            G = Program(pool, S("pool_chain"))

            def split(s):
                if s.base >= NSLAB or s.base % 2 == 0:
                    return
                pool.wait_ge(w_hi, s.of(lambda n: n + 1))
                G.done(pool.tensor_tensor(wl[:, s.base % SPLIT, :], raw[:, s.base % RAW, :],
                                          wh[:, s.base % SPLIT, :].bitcast(F32), ALU.subtract), w_lo_p)

            def splits(s, n):
                for k in range(n):
                    split(At(s + k + AHEAD))

            def rstd(name, mean=False):
                pool.wait_ge(ms_ready, NORMS[name] + 1)
                G.fence()
                if mean:
                    G.done(pool.tensor_copy(rcol, ms), rstd_ready)
                else:
                    G.done(pool.tensor_tensor(rcol, ms, mhalf, ALU.pow), rstd_ready)

            pool.wait_ge(S("constants"), 1)
            rstd("ab")
            for s in range(AHEAD):
                split(At(s))
            for n in range(20):
                split(At(S0["abin"] + n + AHEAD))
                if n == 4:
                    rstd("mem")
            for n in range(8):
                split(At(S0["k0"] + n + AHEAD))
                if n % 2 == 0:
                    g = n // 2
                    wait_emptied(pool, USE0["abin"] + 16 + g)
                    src = z[:, 16 + g, :]
                    for j in range(g + 1):
                        d, dst = 1 << j, t[2 + j % 2][:]
                        G.fence()
                        G.done(pool.tensor_copy(dst[:, 0:d], src[:, 0:d]))
                        G.done(pool.tensor_tensor(dst[:, d:T], src[:, d:T], src[:, 0:T - d], ALU.add))
                        src = dst
                    G.fence()
                    G.done(pool.tensor_tensor(src, src, inv[:, g, :], ALU.mult))
                    G.fence()
                    G.done(pool.tensor_tensor(z[:, 16 + g, :], src, z[:, 16 + g, :], ALU.subtract), S("pooled"))
            for n in range(4):
                split(At(S0["gates"] + n + AHEAD))
                pool.wait_ge(S("pooled_hi"), n + 1)
                G.done(pool.tensor_tensor(yl[:, 8 + n, :], z[:, 16 + n, :], yh[:, 8 + n, :].bitcast(F32),
                                          ALU.subtract), S("pooled_lo"))
            splits(S0["v0"], 8)
            splits(S0["about"], 12)
            rstd("xa0")
            splits(S0["q0"], 8)
            splits(S0["wo0"], 8)
            rstd("f0")

            def glu(name, J):
                base = S0[name]

                def step(j, i=None):
                    st = 12 if i is not None else 0
                    g = At(glu_slab(base, J, "g", j), st, i)
                    jj = At(j, 4 if i is not None else 0, i)
                    split(g + AHEAD)
                    split(g + (1 + AHEAD))
                    if j >= 2:
                        split(g + (2 + AHEAD))
                    pool.wait_ge(S(name + "_hid_hi"), (jj + 1).of(lambda n: n))
                    G.done(pool.tensor_tensor(yl[:, j % 4, :], hid[:, j % 2, :], yh[:, j % 4, :].bitcast(F32),
                                              ALU.subtract), S(name + "_hid_lo"))

                trips, rest = glu_steps(J)
                for j in range(4):
                    step(j)
                with G.loop(trips, {w_lo_p: 6, S(name + "_hid_lo"): 4}, S(name + "_hid_lo")) as i:
                    for j in range(4, 8):
                        step(j, i)
                for j in range(rest, J):
                    step(j)
                splits(base + 3 * J - 2, 2)

            glu("f0", FJ)
            rstd("c")
            splits(S0["pw1"], 32)
            rstd("lnmean", mean=True)
            rstd("ln")
            splits(S0["pw2"], 8)
            rstd("xa1")
            splits(S0["q1"], 16)
            rstd("f1")
            glu("f1", FJ)
            rstd("final")
            rstd("mix")
            splits(S0["win"], 62 + 20)
            wait_slab(pool, At(S0["wout"] + 7))
            for tile in (xg_hi, xg_lo):
                G.done(pool.memset(tile[:].rearrange("p a n s -> p (a n) s")[:, :, CAP:2 * CAP].bitcast(F32), 0.0),
                       S("pads"))
            for tile in (ht_hi, ht_lo):
                G.done(pool.memset(tile[:, :, CAP:2 * CAP].bitcast(F32), 0.0), S("pads"))
            rstd("moe")
            moe_schedule(G, {w_lo_p: 48}, w_lo_p, lambda p, i: [
                split(At(gu_slab(p) + n + AHEAD, 96 if i is not None else 0, i)) for n in range(24 if p else 16)])
            splits(NSLAB - 8, 8)
            rstd("out")

        @block.vector
        def _(dve):
            V = Program(dve, S("vector_chain"))

            def split(s):
                if s.base >= NSLAB or s.base % 2 == 1:
                    return
                dve.wait_ge(w_hi, s.of(lambda n: n + 1))
                V.done(dve.tensor_tensor(wl[:, s.base % SPLIT, :], raw[:, s.base % RAW, :],
                                         wh[:, s.base % SPLIT, :].bitcast(F32), ALU.subtract), w_lo_v)

            def splits(s, n):
                for k in range(n):
                    split(At(s + k + AHEAD))

            def norm_mean(name, eps=EPS):
                dve.wait_ge(stat_full, NORMS[name] + 1)
                V.fence()
                V.done(dve.tensor_scalar(ms, acc[0][:, 0:2], 1.0 / D, eps, ALU.mult, ALU.add), ms_ready)

            def norm_spread(name, dst):
                dve.wait_ge(rstd_ready, NORMS[name] + 1)
                V.fence()
                for q in range(TT):
                    V.done(dve.tensor_scalar(diag[:, q, :], ident[:], rcol[:, q:q + 1], None, ALU.mult), diag_ready)
                dve.wait_ge(bc_full, NORMS[name] + 1)
                V.fence()
                V.done(dve.tensor_copy(dst, acc[0][:, T:2 * T]), rstd_b_ready)
                V.fence()

            def pair_lo_parts(pair, gain):
                for c in range(KC):
                    dve.wait_ge(pair_hi, KC * PAIRS[pair] + c + 1)
                    V.done(dve.scalar_tensor_tensor(al[:, c, :], x[:, c, :], col(gain, c),
                                                    ah[:, c, :].bitcast(F32), ALU.mult, ALU.subtract), pair_lo)

            def take_sums(phase, bias=None):
                for c in range(KC):
                    if phase != "moe":
                        wait_acc(dve, phase, c)
                    if c == 0:
                        V.fence()
                    if bias is None:
                        ins = dve.tensor_tensor(x[:, c, :], acc_of(c), x[:, c, :], ALU.add)
                    else:
                        ins = dve.scalar_tensor_tensor(x[:, c, :], acc_of(c), col(bias, c), x[:, c, :],
                                                       ALU.add, ALU.add)
                    V.done(ins, acc_out)

            def col_out(name, n, dst, scale=None, by=None, slab=None):
                u = USE0[name] + n
                wait_slab(dve, At(S0[name] + (n if slab is None else slab)))
                b = pw[u % 4][:, 0:T]
                if by is None:
                    ins = dve.tensor_copy(dst, b)
                elif scale is None:
                    ins = dve.tensor_tensor(dst, b, by, ALU.mult)
                else:
                    ins = dve.scalar_tensor_tensor(dst, b, scale, by, ALU.mult, ALU.mult)
                V.done(ins, empty_v)

            dve.memset(ones[:], 1.0).then_inc(S("ones"), 1)
            V.done(dve.memset(mhalf, -0.5), S("constants"))
            dve.wait_ge(S("const_in"), 48)
            dve.wait_ge(S("x_in"), 16)
            pair_lo_parts("abin", "ab_norm")
            for s in range(AHEAD):
                split(At(s))
            norm_mean("ab")
            dve.wait_ge(S("decay_exp"), 1)
            lam = cols[:, C0["a_lambda"]:C0["a_lambda"] + 8]
            V.done(dve.tensor_scalar(lam_z, lam_e, 2.0, None, ALU.add))
            V.fence()
            V.done(dve.reciprocal(lam_z, lam_z))
            V.fence()
            V.done(dve.tensor_tensor(lam_z, lam_z, lam_e, ALU.mult))
            V.fence()
            V.done(dve.tensor_tensor(lam_q, lam_z, lam_z, ALU.mult))
            V.done(dve.memset(sp8, 1.0 / 19))
            for k in range(8, -1, -1):
                V.fence()
                V.done(dve.tensor_tensor(sp8, sp8, lam_q, ALU.mult))
                V.fence()
                V.done(dve.tensor_scalar(sp8, sp8, 1.0 / (2 * k + 1), None, ALU.add))
            V.fence()
            V.done(dve.scalar_tensor_tensor(sp8, sp8, 2.0, lam_z, ALU.mult, ALU.mult))
            V.done(dve.tensor_scalar(lam_q, lam, -1.0, 0.0, ALU.mult, ALU.max))
            V.fence()
            V.done(dve.tensor_tensor(sp8, sp8, lam_q, ALU.add))
            V.fence()
            V.done(dve.tensor_scalar(n4sp, sp8, -4.0, None, ALU.mult))
            V.done(dve.tensor_scalar(p4sp, sp8, 4.0, None, ALU.mult))
            V.done(dve.tensor_scalar(hbx, cols[:, C0["a_gate_x_b"]:C0["a_gate_x_b"] + 8], 0.5, None, ALU.mult))
            V.done(dve.tensor_scalar(hba, cols[:, C0["a_gate_a_b"]:C0["a_gate_a_b"] + 8], 0.5, None, ALU.mult))
            V.done(dve.tensor_scalar(hbc, cols[:, C0["c_b_pw1"] + 8:C0["c_b_pw1"] + 16], 0.5, None, ALU.mult))
            V.done(dve.tensor_scalar(nsink, cols[:, C0["sinks"]:C0["sinks"] + 16], -1.0, None, ALU.mult), S("decay"))
            norm_spread("ab", rstd_b[:])

            def mem_lo(l, c):
                dve.wait_ge(S("m_hi"), KC * l + c + 1)
                V.done(dve.scalar_tensor_tensor(ml[:, c, :], mem[:, c, :], col(f"mem_norm{l}", c),
                                                mh[:, c, :].bitcast(F32), ALU.mult, ALU.subtract), S("m_lo"))

            for n in range(20):
                split(At(S0["abin"] + n + AHEAD))
                if n == 4:
                    norm_mean("mem")
                if n == 7:
                    norm_spread("mem", mem_rstd[:])
                    V.fence()
                    for c in range(KC):
                        V.done(dve.tensor_tensor(mem[:, c, :], mem[:, c, :], mem_rstd[:], ALU.mult), S("mem_normed"))
                if n >= 11 and n < 19:
                    mem_lo(0, n - 11)
                col_out("abin", n, z[:, n, :], by=rstd_b[:])
            for n in range(8):
                split(At(S0["k0"] + n + AHEAD))
                col_out("k0", n, k_t[:, n, :])
                for k in range(CONV_A):
                    w, lag = col("a_conv_w", n * CONV_A + CONV_A - 1 - k), k
                    V.fence()
                    if k == 0:
                        V.done(dve.tensor_scalar(xr[:, n, :], z[:, 8 + n, :], w, col("a_conv_b", n),
                                                 ALU.mult, ALU.add))
                    else:
                        V.done(dve.scalar_tensor_tensor(xr[:, n, lag:T], z[:, 8 + n, 0:T - lag], w, xr[:, n, lag:T],
                                                        ALU.mult, ALU.add),
                               S("xr_ready") if k == CONV_A - 1 else None)
                dve.wait_ge(S("xr_hi"), n + 1)
                V.done(dve.tensor_tensor(yl[:, n, :], xr[:, n, :], yh[:, n, :].bitcast(F32), ALU.subtract),
                       S("xr_lo"))
            for n in range(4):
                split(At(S0["gates"] + n + AHEAD))
                for h in (2 * n, 2 * n + 1):
                    dve.wait_ge(S("gates_through"), h + 1)
                    V.fence()
                    V.done(dve.tensor_tensor(diag[:].rearrange("p a b -> p (a b)"), a_t[:, h, :], a_t[:, h, :],
                                             ALU.mult))
                    V.fence()
                    V.done(dve.scalar_tensor_tensor(z[:, 8 + h, :], diag[:].rearrange("p a b -> p (a b)"), 1.0,
                                                    z[:, 8 + h, :], ALU.add, ALU.mult))
                    V.done(dve.scalar_tensor_tensor(xr[:, h, :], t[h % 2][:], 1.0, xr[:, h, :], ALU.add, ALU.mult),
                           S("root_in"))
                u = USE0["gates"] + 3 * n + 2
                wait_slab(dve, At(S0["gates"] + n))
                V.done(dve.tensor_scalar(z[:, 16 + n, :], pw[u % 4][:, 0:T], col("b_group_b", n), col("b_scale", n),
                                         ALU.add, ALU.mult), empty_v)
                dve.wait_ge(S("yb_hi"), n + 1)
                V.done(dve.tensor_tensor(yl[:, 8 + n, :], z[:, 16 + n, :], yh[:, 8 + n, :].bitcast(F32),
                                         ALU.subtract), S("yb_lo"))

            def values_out(name, half):
                wait_slab(dve, At(S0[name] + 4 * half + 3))
                for q in range(TT):
                    u = USE0[name] + 2 * half + q
                    V.done(dve.tensor_copy(v_m[:, q, half * 512:half * 512 + 512], pw[u % 4][:, :]), empty_v)

            for n in range(8):
                split(At(S0["v0"] + n + AHEAD))
                dve.wait_ge(S("root"), 1)
                V.fence()
                V.done(dve.tensor_tensor(xr[:, n, :], xr[:, n, :], z[:, 8 + n, :], ALU.mult))
                V.fence()
                V.done(dve.tensor_tensor_scan(z[:, 8 + n, :], a_t[:, n, :], xr[:, n, :], 0.0, ALU.mult, ALU.add))
                V.fence()
                dve.wait_ge(S("gate_gelu"), n + 1)
                V.done(dve.tensor_tensor(xr[:, n, :], z[:, 8 + n, :], z[:, n, :], ALU.mult), S("ya_ready"))
                dve.wait_ge(S("ya_hi"), n + 1)
                V.done(dve.tensor_tensor(yl[:, n, :], xr[:, n, :], yh[:, n, :].bitcast(F32), ALU.subtract),
                       S("ya_lo"))
                if n == 5 or n == 7:
                    values_out("v0", n // 6)
            splits(S0["about"], 12)
            take_sums("about")

            def normed_pair(name, pair, gain):
                pair_lo_parts(pair, gain)
                norm_mean(name)

            def queries(l):
                for n in range(8):
                    split(At(S0[f"q{l}"] + n + AHEAD))
                    if n == 2:
                        norm_spread(f"xa{l}", rstd_b[:])
                        for k in range(3):
                            col_out(f"q{l}", k, q_t[:, k, :], 1.0 / 16, rstd_b[:])
                    elif n > 2:
                        col_out(f"q{l}", n, q_t[:, n, :], 1.0 / 16, rstd_b[:])

            def cross(l):
                name, n_u = f"x{l}", USE0[f"x{l}"]
                for h in range(XH + 1):
                    if h < XH:
                        for qt in range(TT):
                            k = x_score(h) + qt
                            dve.wait_ge(mm_done, MM0[name] + k + 1)
                            V.fence()
                            V.done(dve.tensor_reduce(nmax[:, qt:qt + 1], pw[(n_u + k) % 4][:, 0:T], AX.X, ALU.max,
                                                     negate=True), S(name + "_max"))
                        for qt in range(TT):
                            wait_emptied(dve, n_u + x_score(h) + qt)
                            V.done(dve.reciprocal(rec[:, qt:qt + 1], den[:, qt:qt + 1]))
                            V.fence()
                            V.done(dve.tensor_scalar(prob[:, h % 2, qt, :], prob[:, h % 2, qt, :], rec[:, qt:qt + 1],
                                                     None, ALU.mult), S(name + "_prob"))
                    if h >= 1:
                        k = x_turn(h - 1) + 2
                        dve.wait_ge(S(name + "_hi"), h)
                        V.done(dve.tensor_tensor(yl[:, 2 * h - 2:2 * h, :],
                                                 pw[(n_u + k) % 4][:, :].rearrange("p (a q) -> p a q", a=2),
                                                 yh[:, 2 * h - 2:2 * h, :].bitcast(F32), ALU.subtract), empty_v)

            def glu(name, J):
                base, l = S0[name], name[-1]

                def step(j, i=None):
                    st, st4 = (12, 4) if i is not None else (0, 0)
                    g = At(glu_slab(base, J, "g", j), st, i)
                    jj = At(j, st4, i)
                    u = USE0[name] + 2 * j
                    if j == 1:
                        norm_spread(name, rstd_b[:])
                        gate(0, At(0), At(base), None)
                        up(0, At(0), At(base + 1), USE0[name] + 1)
                    split(g + AHEAD)
                    if j >= 1:
                        gate(j, jj, g, i)
                    split(g + (1 + AHEAD))
                    if j >= 1:
                        up(j, jj, g + 1, u + 1)
                    if j >= 2:
                        split(g + (2 + AHEAD))

                def gate(j, jj, g, i):
                    wait_slab(dve, g)
                    V.fence()
                    V.done(dve.tensor_tensor(gpad[:, j % 2, 2:T + 2], pw[(USE0[name] + 2 * j) % 4][:, 0:T],
                                             rstd_b[:], ALU.mult), empty_v)
                    for k in range(CONV_F):
                        w = col(f"f_dw_w{l}", j * CONV_F + CONV_F - 1 - k, 4 * CONV_F, i)
                        V.fence()
                        if k == 0:
                            V.done(dve.tensor_scalar(cf[:, j % 2, :], gpad[:, j % 2, 2:T + 2], w,
                                                     col(f"f_dw_b{l}", j, 4, i), ALU.mult, ALU.add))
                        else:
                            V.done(dve.scalar_tensor_tensor(cf[:, j % 2, :], gpad[:, j % 2, 2 - k:T + 2 - k], w,
                                                            cf[:, j % 2, :], ALU.mult, ALU.add),
                                   S(name + "_conv") if k == CONV_F - 1 else None)

                def up(j, jj, s, u):
                    wait_slab(dve, s)
                    if j >= 2:
                        dve.wait_ge(S(name + "_hid_lo"), (jj + -1).of(lambda n: n))
                    V.fence()
                    V.done(dve.tensor_tensor(uf[:, j % 2, :], pw[u % 4][:, 0:T], rstd_b[:], ALU.mult), empty_v)
                    V.fence()
                    dve.wait_ge(S(name + "_act"), (jj + 1).of(lambda n: n))
                    V.done(dve.tensor_tensor(hid[:, j % 2, :], cf[:, j % 2, :], uf[:, j % 2, :], ALU.mult),
                           S(name + "_hidden"))

                V.fence()
                V.done(dve.memset(gpad[:, :, 0:2], 0.0))
                trips, rest = glu_steps(J)
                for j in range(4):
                    step(j)
                raised = {w_lo_v: 6, S(name + "_hidden"): 4, empty_v: 8, S(name + "_conv"): 4, S("vector_chain"): 8}
                last = w_lo_v if glu_slab(base, J, "u", 7) % 2 == 0 else S(name + "_hidden")
                with V.loop(trips, raised, last) as i:
                    for j in range(4, 8):
                        step(j, i)
                for j in range(rest, J):
                    step(j)
                splits(base + 3 * J - 2, 2)

            normed_pair("xa0", "q0", "xa_norm0")
            queries(0)
            cross(0)
            splits(S0["wo0"], 8)
            take_sums("wo0")
            normed_pair("f0", "f0", "f_norm0")
            glu("f0", FJ)
            take_sums("f0")
            normed_pair("c", "pw1", "c_norm")
            V.fence()
            V.done(dve.memset(hpad[:, :, 0:CONV_C - 1], 0.0))
            taps = KC * CONV_C

            def conv_taps(lo, hi):
                for m in range(lo, hi):
                    c, k = m % 2 + 2 * (m // (2 * CONV_C)), (m // 2) % CONV_C
                    w = col("c_dw_w", c * CONV_C + k)
                    src = hpad[:, c, k:k + T]
                    V.fence(1)
                    if k == 0:
                        V.done(dve.tensor_scalar(cv[:, c, :], src, w, col("c_dw_b", c), ALU.mult, ALU.add))
                    else:
                        V.done(dve.scalar_tensor_tensor(cv[:, c, :], src, w, cv[:, c, :], ALU.mult, ALU.add),
                               S("conv_out") if k == CONV_C - 1 else None)

            done_taps = 0
            for n in range(32):
                s = S0["pw1"] + n
                split(At(s + AHEAD))
                if n == 2:
                    norm_spread("c", rstd_b[:])
                if 2 <= n < 18:
                    for k in ([0, 1, 2] if n == 2 else [n] if n < 16 else []):
                        c, ta, tb = k // 2, t[2 * (k // 2 % 2)][:], t[2 * (k // 2 % 2) + 1][:]
                        V.fence()
                        col_out("pw1", k, tb if k % 2 else ta, by=rstd_b[:])
                        if k % 2:
                            dve.wait_ge(S("glu_tanh"), c + 1)
                            V.done(dve.tensor_scalar(tb, tb, 0.5, 0.5, ALU.mult, ALU.add))
                            V.fence()
                            V.done(dve.scalar_tensor_tensor(hpad[:, c, CONV_C - 1:], ta, col("c_b_pw1", c), tb,
                                                            ALU.add, ALU.mult), S("glu_out"))
                if n == 7:
                    dve.wait_ge(S("mem_again"), 16)
                    V.fence()
                    for c in range(KC):
                        V.done(dve.tensor_tensor(mem[:, c, :], mem[:, c, :], mem_rstd[:], ALU.mult), S("mem_normed"))
                if 11 <= n < 15:
                    mem_lo(1, 2 * (n - 11))
                    mem_lo(1, 2 * (n - 11) + 1)
                if 16 <= n < 24:
                    col_out("k1", n - 16, k_t[:, n - 16, :])
                if n in (27, 31):
                    values_out("v1", (n - 27) // 4)
                upto = min(taps * max(n - 3, 0) // 28, 2 * CONV_C * ((min(n, 15) + 1) // 4))
                conv_taps(done_taps, upto)
                done_taps = upto
            conv_taps(done_taps, taps)
            norm_mean("lnmean", 0.0)
            norm_spread("lnmean", t[0][:])
            V.fence()
            for c in range(KC):
                V.done(dve.tensor_tensor(cv[:, c, :], cv[:, c, :], t[0][:], ALU.subtract), S("ln_centred"))
            norm_mean("ln")
            norm_spread("ln", t[0][:])
            V.fence()
            for c in range(KC):
                V.done(dve.tensor_tensor(cv[:, c, :], cv[:, c, :], t[0][:], ALU.mult), S("ln_scaled"))
            for c in range(KC):
                dve.wait_ge(S("ln_hi"), c + 1)
                V.done(dve.tensor_tensor(yl[:, c, :], cv[:, c, :], yh[:, c, :].bitcast(F32), ALU.subtract),
                       S("ln_lo"))
            splits(S0["pw2"], 8)
            take_sums("pw2", "c_b_pw2")
            normed_pair("xa1", "q1", "xa_norm1")
            queries(1)
            cross(1)
            splits(S0["wo1"], 8)
            take_sums("wo1")
            normed_pair("f1", "f1", "f_norm1")
            glu("f1", FJ)
            take_sums("f1")
            norm_mean("final")
            norm_spread("final", rstd_b[:])
            V.fence()
            for c in range(KC):
                V.done(dve.scalar_tensor_tensor(x[:, c, :], x[:, c, :], col("final_norm", c), rstd_b[:],
                                                ALU.mult, ALU.mult), S("x_normed"))
            normed_pair("mix", "win", "g_mix")
            for n in range(62):
                split(At(S0["win"] + n + AHEAD))
                if n == 2:
                    norm_spread("mix", rstd_b[:])
                for k in ([0, 1, 2] if n == 2 else [n] if n > 2 else []):
                    if k < 12:
                        col_out("win", k, q2[:, k, :], 0.125, rstd_b[:])
                    elif k < 24:
                        col_out("win", k, k2[:, k - 12, :], by=rstd_b[:])
                    elif k < 32:
                        col_out("win", k, q2[:, k - 12, :], 0.125, rstd_b[:])
                    elif k < 44:
                        if k % 4 == 3:
                            b = (k - 32) // 4
                            wait_slab(dve, At(S0["win"] + k))
                            for q in range(TT):
                                u = USE0["win"] + 32 + 2 * b + q
                                V.done(dve.tensor_scalar(v2[:, q, 512 * b:512 * b + 512], pw[u % 4][:, :],
                                                         rcol[:, q:q + 1], None, ALU.mult), empty_v)
                    elif k == 44:
                        col_out("win", 38, k2[:, 12, :], by=rstd_b[:], slab=44)
                    elif k == 45:
                        wait_slab(dve, At(S0["win"] + 45))
                        for q in range(TT):
                            u = USE0["win"] + 39 + q
                            V.done(dve.tensor_scalar(v2[:, q, 1536:1664], pw[u % 4][:, 0:P], rcol[:, q:q + 1],
                                                     None, ALU.mult), empty_v)
                    else:
                        col_out("win", 41 + k - 46, gt[:, k - 46, :], by=rstd_b[:], slab=k)
            dve.wait_ge(S("masks_in"), 16)
            for m in range(len(HEADS2) + 1):
                if m < len(HEADS2):
                    kind, h = HEADS2[m]
                    G_ = groups(kind)
                    for qt in range(TT):
                        at, nk = (0, P) if qt == 0 else (3 * P, 2 * P)
                        for g in range(G_):
                            k = a_score(m) + qt * G_ + g
                            slope = SLOPES_DIL[8 * g + h] if kind == "d" else SLOPES_SWA[h]
                            dve.wait_ge(mm_done, MM0["attn2"] + k + 1)
                            V.done(dve.scalar_tensor_tensor(
                                sc[:, m % 2, at + g * nk:at + g * nk + nk],
                                masks[:, g if kind == "d" else 3, (0 if qt == 0 else P):(P if qt == 0 else 3 * P)],
                                -slope, pw[(USE0["attn2"] + k) % 4][:, 0:nk], ALU.mult, ALU.add), empty_v)
                        V.fence()
                        mx = nmax[:, qt:qt + 1]
                        V.done(dve.tensor_reduce(mx, sc[:, m % 2, at:at + G_ * nk], AX.X, ALU.max, negate=True),
                               S("attn2_max") if kind == "d" else None)
                        if kind == "s":
                            V.fence()
                            V.done(dve.tensor_scalar(mx, mx, nsink[:, h:h + 1], None, ALU.min), S("attn2_max"))
                    for qt in range(TT):
                        at, nk = (0, P) if qt == 0 else (3 * P, 2 * P)
                        dve.wait_ge(S("attn2_exp"), 2 * m + qt + 1)
                        r = rec[:, qt:qt + 1]
                        if kind == "s":
                            V.fence()
                            V.done(dve.tensor_tensor(den[:, qt:qt + 1], den[:, qt:qt + 1], esink[:, qt:qt + 1],
                                                     ALU.add))
                        V.fence()
                        V.done(dve.reciprocal(r, den[:, qt:qt + 1]))
                        V.fence()
                        s_ap = sc[:, m % 2, at:at + G_ * nk]
                        V.done(dve.tensor_scalar(s_ap, s_ap, r, None, ALU.mult), S("attn2_prob"))
                if m >= 1:
                    kind, h = HEADS2[m - 1]
                    k = a_turn(m - 1) + groups(kind)
                    c, half = mixed_at(kind, h)
                    dve.wait_ge(S("attn2_hi"), m)
                    V.done(dve.tensor_tensor(yl[half:half + 64, c, :], pw[(USE0["attn2"] + k) % 4][half:half + 64, 0:T],
                                             yh[half:half + 64, c, :].bitcast(F32), ALU.subtract), empty_v)
            dve.wait_ge(S("mix_gates"), 16)
            for phase, first in (("brd", 0), ("brs", 8)):
                splits(S0[phase], dict(PHASES)[phase])
                for c in range(KC):
                    wait_acc(dve, phase, c)
                    V.done(dve.scalar_tensor_tensor(gt[:, first + c, :], gt[:, first + c, :], 1.0, acc_of(c),
                                                    ALU.add, ALU.mult), acc_out)
            V.fence()
            for c in range(KC):
                V.done(dve.tensor_tensor(gt[:, c, :], gt[:, c, :], gt[:, 8 + c, :], ALU.add), S("mixed"))
            for c in range(KC):
                dve.wait_ge(S("mixed_hi"), c + 1)
                V.done(dve.scalar_tensor_tensor(yl[:, c, :], gt[:, c, :], 0.5, yh[:, c, :].bitcast(F32),
                                                ALU.mult, ALU.subtract), S("mixed_lo"))
            splits(S0["wout"], 8)
            take_sums("wout")
            norm_mean("moe")
            norm_spread("moe", rstd_b[:])
            V.fence()
            for c in range(KC):
                V.done(dve.scalar_tensor_tensor(hf[:, c, :], x[:, c, :], col("g_ffn", c), rstd_b[:],
                                                ALU.mult, ALU.mult), S("h_ready"))
            def first_of(dst, values, top, n, count):
                V.fence()
                V.done(dve.tensor_scalar(dst, values, top, None, ALU.is_equal))
                V.fence()
                V.done(dve.tensor_tensor_scan(count, one_row[:, 0:n], dst, 0.0, ALU.mult, ALU.add))
                V.fence()
                V.done(dve.tensor_scalar(count, count, 1.0, None, ALU.is_equal))
                V.fence()
                V.done(dve.tensor_tensor(dst, dst, count, ALU.mult))

            one_row = ones[:, 0:8]
            dve.wait_ge(S("router_full"), 1)
            for q in range(TT):
                V.done(dve.tensor_tensor(lg[:, q, :], acc[1][:, 64 * q:64 * q + 36],
                                         cols[:, C0["r_bias"]:C0["r_bias"] + 36], ALU.add), S("logits_out"))
            gmx, gsum, e2, gap = rt[:, 0:1], rt[:, 1:2], rt[:, 2:3], rt[:, 3:4]
            gmask, count = rt[:, 8:12], rt[:, 88:96]
            sel, f1, f2, sel2 = rt[:, 16:24], rt[:, 24:32], rt[:, 32:40], rt[:, 40:48]
            m1, m2, w1, gw = rt[:, 12:13], rt[:, 13:14], rt[:, 14:15], rt[:, 15:16]
            w2, top = rt[:, 48:49], rt[:, 49:50]

            def h_by_token_lo(j):
                dve.wait_ge(S("h_turned_hi"), j + 1)
                w = slice(512 * (j % 2), 512 * (j % 2) + 512)
                V.done(dve.tensor_tensor(htok_lo[:, j // 2, w], pw[j][:, :], htok_hi[:, j // 2, w].bitcast(F32),
                                         ALU.subtract), S("h_turned_lo"))

            for q in range(TT):
                V.fence()
                V.done(dve.tensor_reduce(top, lg[:, q, 0:4], AX.X, ALU.max))
                V.fence()
                V.done(dve.tensor_scalar(gmx, top, -1.0, None, ALU.mult), S("group_max"))
                first_of(gmask, lg[:, q, 0:4], top, 4, count[:, 0:4])
                for g in range(4):
                    V.fence()
                    el = lg[:, q, 4 + 8 * g:12 + 8 * g]
                    if g == 0:
                        V.done(dve.tensor_scalar(sel, el, gmask[:, 0:1], None, ALU.mult))
                    else:
                        V.done(dve.scalar_tensor_tensor(sel, el, gmask[:, g:g + 1], sel, ALU.mult, ALU.add))
                V.fence()
                V.done(dve.tensor_reduce(m1, sel, AX.X, ALU.max))
                first_of(f1, sel, m1, 8, count)
                V.fence()
                V.done(dve.scalar_tensor_tensor(sel2, f1, NEG, sel, ALU.mult, ALU.add))
                V.fence()
                V.done(dve.tensor_reduce(m2, sel2, AX.X, ALU.max))
                first_of(f2, sel2, m2, 8, count)
                V.fence()
                V.done(dve.tensor_tensor(gap, m2, m1, ALU.subtract), S("expert_gap"))
                dve.wait_ge(S("expert_exp"), q + 1)
                V.done(dve.reciprocal(gw, gsum))
                V.done(dve.tensor_scalar(w1, e2, 1.0, None, ALU.add))
                V.fence()
                V.done(dve.reciprocal(w1, w1))
                V.fence()
                V.done(dve.tensor_tensor(w1, w1, gw, ALU.mult))
                V.fence()
                V.done(dve.tensor_tensor(w2, w1, e2, ALU.mult))
                V.fence()
                V.done(dve.tensor_scalar(f1, f1, w1, None, ALU.mult))
                V.fence()
                V.done(dve.scalar_tensor_tensor(f1, f2, w2, f1, ALU.mult, ALU.add))
                for g in range(4):
                    V.fence()
                    V.done(dve.tensor_scalar(gates[:, q, 8 * g:8 * g + 8], f1, gmask[:, g:g + 1], None, ALU.mult))
                V.fence()
                V.done(dve.tensor_scalar(chosen[:, q, :], gates[:, q, :], 0.0, None, ALU.is_gt), S("chosen"))
                h_by_token_lo(2 * q)
                h_by_token_lo(2 * q + 1)
            V.done(dve.memset(zeros[:].bitcast(F32), 0.0), S("zeros"))
            dve.wait_ge(S("places"), 1)
            V.done(dve.tensor_tensor(place[:].rearrange("p q e -> p (q e)"), acc[2][:, 0:TT * NE],
                                     chosen[:].rearrange("p q e -> p (q e)"), ALU.mult))
            V.done(dve.tensor_reduce(most[:], acc[2][:, TT * NE:(TT + 1) * NE], AX.X, ALU.max))
            V.fence()
            V.done(dve.tensor_scalar(overflow[:], most[:], float(CAP), None, ALU.is_gt), S("overflow_known"))

            def make_onehot(g):
                if g.base >= 2:
                    dve.wait_ge(S("slots_turned"), g.of(lambda n: 2 * n - 2))
                for q in range(TT):
                    at = place[:, q, 4 * g.base:4 * g.base + 4] if g.i is None else \
                        place[:, q, bass.ds(g.i * (4 * g.step) + 4 * g.base, 4)]
                    V.done(dve.tensor_tensor(onehot[:, g.base % 2, q, :].rearrange("p (e s) -> p e s", e=4),
                                             slot_no.unsqueeze(1).broadcast_to([P, 4, CAP]),
                                             at.unsqueeze(2).broadcast_to([P, 4, CAP]), ALU.is_equal), S("onehot"))

            make_onehot(At(0))

            def gather_lo(j):
                dve.wait_ge(S("gathered_hi"), (j + 1).of(lambda n: n))
                c, par = 4 * (j.base % 4), j.base // 4 % 2
                V.done(dve.tensor_tensor(both_of_pairs(xg_lo[:, par, c:c + 4, :]),
                                         pw[gather_bank(j.base)][:, :].rearrange("p (n e s) -> p n e s", n=4, e=2),
                                         both_of_pairs(xg_hi[:, par, c:c + 4, :]).bitcast(F32), ALU.subtract),
                       S("gathered_lo"))

            def y_lo(pp, h):
                dve.wait_ge(S("expert_out_hi"), pp.of(lambda n: 2 * n + h + 1))
                w = slice(512 * h, 512 * h + 512)
                V.done(dve.tensor_tensor(ye_lo[:, w], pw[2 + h][:, :], ye_hi[:, w].bitcast(F32), ALU.subtract),
                       S("expert_out_lo"))

            def turned_lo(p):
                dve.wait_ge(S("hidden_turned_hi"), (p + 1).of(lambda n: n))
                V.done(dve.tensor_tensor(both_of_pairs(ht_lo[:]),
                                         pw[2][:, :].rearrange("p (n e s) -> p n e s", n=4, e=2),
                                         both_of_pairs(ht_hi[:]).bitcast(F32), ALU.subtract),
                       S("hidden_turned_lo"))

            def period(p, i):
                pp = per_trip(p, i)
                for n in range(24 if p else 16):
                    split(At(gu_slab(p) + n + AHEAD, 96 if i is not None else 0, i))
                    if p >= 2 and n < 2:
                        y_lo(pp + -2, n)
                    if p % 2 == 0 and p < 14 and n == 2:
                        make_onehot(At(p // 2 + 1, 2 if i is not None else 0, i))
                    if p >= 1 and n == 4:
                        turned_lo(pp + -1)
                    if p < 14 and n in (8, 10):
                        gather_lo(At(4 + 2 * p + (n == 10), 8 if i is not None else 0, i))
                    if n == 12:
                        dve.wait_ge(S("slots_turned_out"), (pp + 1).of(lambda n: n))
                        for e in range(2):
                            sl = slice(CAP * e, CAP * e + CAP)
                            V.done(dve.tensor_copy(slot_gate[sl, p % 2:p % 2 + 1], pw[3][sl, T + e:T + e + 1]),
                                   S("slot_gates"))
                    if n == 15:
                        dve.wait_ge(S("silu"), (pp + 1).of(lambda n: n))
                        if p:
                            dve.wait_ge(S("hidden_turned"), pp.of(lambda n: n))
                        dve.wait_ge(S("slot_gates"), (pp + 1).of(lambda n: 2 * n))
                        V.done(dve.scalar_tensor_tensor(hide[:], silu[:], slot_gate[:, p % 2:p % 2 + 1], pw[1][:, :], ALU.mult, ALU.mult),
                               S("hidden_done"))

            for j in range(4):
                gather_lo(At(j))
            moe_schedule(V, {w_lo_v: 48, S("expert_out_lo"): 8, S("hidden_turned_lo"): 4, S("gathered_lo"): 8,
                             S("hidden_done"): 4, S("slot_gates"): 8, S("onehot"): 4}, w_lo_v, period)
            last = PAIRS_E - 1
            y_lo(At(last - 1), 0)
            y_lo(At(last - 1), 1)
            turned_lo(At(last))
            splits(NSLAB - 8, 8)
            y_lo(At(last), 0)
            y_lo(At(last), 1)
            dve.wait_ge(S("scattered"), PAIRS_E)
            over = dve.value_load(overflow[0:1, 0:1], min_val=0, max_val=1)
            with dve.If(over > 0):
                with dve.Fori(0, NE) as i:
                    for q in range(TT):
                        dve.wait_ge(S("dense_silu"), i * 2 + (q + 1))
                        dve.scalar_tensor_tensor(dense_hid[:, q, :], dense_silu[:, q, :], gates[:, q, bass.ds(i, 1)],
                                                 pw[2 * q + 1][:, :], ALU.mult, ALU.mult) \
                            .then_inc(S("dense_hidden"), 1)
                dve.wait_ge(S("dense_down"), NE + 2)
            V.fence()
            take_sums("moe")
            norm_mean("out")
            norm_spread("out", rstd_b[:])
            V.fence()
            for c in range(KC):
                V.done(dve.scalar_tensor_tensor(x[:, c, :], x[:, c, :], col("g_final", c), rstd_b[:],
                                                ALU.mult, ALU.mult), S("x_final"))

        @block.tensor
        def _(pe):
            def tile3(dst, s, n, hi, lo, start, stop, **kw):
                w = slice(n * P, n * P + P)
                pe.matmul(dst, wh[:, s.base % SPLIT, w], hi, start=start, stop=False, **kw)
                pe.matmul(dst, wl[:, s.base % SPLIT, w], hi, start=False, stop=False, **kw)
                return pe.matmul(dst, wh[:, s.base % SPLIT, w], lo, start=False, stop=stop, **kw)

            def norm_sums(name, src, ready):
                for c in range(KC):
                    ready(min(c + 1, KC - 1) if c == 0 else c)
                    for q in range(TT):
                        last = pe.matmul(acc[0][:, q:q + 1], src[:, c, q * P:q * P + P], ones[:, 0:1],
                                         start=(c == 0 and q == 0), stop=(c == KC - 1), skip_group_check=True)
                last.then_inc(stat_full, 1)

            def sq_sums(name):
                norm_sums(name, sq, lambda c: pe.wait_ge(sq_ready, KC * (NORMS[name] - (NORMS[name] > NORMS["lnmean"]))
                                                         + c + 1))

            def norm_spread(name):
                pe.wait_ge(diag_ready, TT * (NORMS[name] + 1))
                for q in range(TT):
                    last = pe.matmul(acc[0][:, T + q * P:T + q * P + P], ones[:], diag[:, q, :], start=True, stop=True)
                last.then_inc(bc_full, 1)

            def drain(u):
                for who, sem in (("v", empty_v), ("a", empty_a)):
                    if u and emptied(u - 1, who):
                        pe.wait_ge(sem, emptied(u - 1, who))

            def col_slab(s, u, hi, lo, wait_n=None, first_ready=None):
                wait_split(pe, s)
                if wait_n is not None:
                    pe.wait_ge(empty_v, wait_n)
                for k in range(KC):
                    if first_ready is not None:
                        first_ready(k)
                    last = tile3(pw[u % 4][:, 0:T], s, k, hi[:, k, :], lo[:, k, :], k == 0, k == KC - 1)
                last.then_inc(slab_done, 1)

            def col_phase(name, n, hi, lo, ready=None, hook=None, straight=None, s_off=0, u_off=0):
                s0, u0 = S0[name] + s_off, USE0[name] + u_off
                straight = straight or (8 if n == 8 else 4)
                v0 = emptied(u0 - 1, "v") if u0 else 0
                drain(u0)
                for k in range(straight):
                    col_slab(At(s0 + k), u0 + k, hi, lo, v0 + k - 3 if k >= 4 else None, ready if k == 0 else None)
                    if hook:
                        hook(k)
                if n > straight:
                    with pe.Fori(0, (n - straight) // 4) as i:
                        for j in range(straight, straight + 4):
                            col_slab(At(s0 + j, 4, i), u0 + j, hi, lo, i * 4 + (v0 + j - 3))

            def row_slab(s, k, first, last, start_acc=None):
                wait_split(pe, s)
                for n in range(KC):
                    ins = tile3(acc_of(n), s, n, yh[:, k, :], yl[:, k, :], first and n % 2 == 0, last,
                                skip_group_check=True)
                    if last and n < KC - 1:
                        ins.then_inc(acc_full, 1)
                ins.then_inc(slab_done, 1)

            def row_phase(name, order, ready, norm):
                if ACCS[name]:
                    pe.wait_ge(acc_out, KC * ACCS[name])
                if norm is not None:
                    pe.wait_ge(rstd_b_ready, NORMS[norm] + 1)
                for n, k in enumerate(order):
                    ready(k)
                    row_slab(At(S0[name] + n), k, n == 0, n == len(order) - 1)

            def pair_ready(pair):
                return lambda k: pe.wait_ge(pair_lo, KC * PAIRS[pair] + k + 1)

            def values(s0, u0, hi, lo, half):
                for kk in range(4):
                    s = At(s0 + 4 * half + kk)
                    wait_split(pe, s)
                    if kk == 0:
                        for q in range(TT):
                            wait_emptied(pe, u0 + 2 * half + q - 4)
                    for e in range(2):
                        k = 2 * kk + e
                        w = slice(e * 512, e * 512 + 512)
                        for q in range(TT):
                            dst = pw[(u0 + 2 * half + q) % 4][:, :]
                            tk = slice(q * P, q * P + P)
                            slot = s.base % SPLIT
                            pe.matmul(dst, hi[:, k, tk], wh[:, slot, w], start=(k == 0), stop=False)
                            pe.matmul(dst, hi[:, k, tk], wl[:, slot, w], start=False, stop=False)
                            last = pe.matmul(dst, lo[:, k, tk], wh[:, slot, w], start=False, stop=(k == KC - 1))
                    last.then_inc(slab_done, 1)

            def cross(l):
                name, n_u = f"x{l}", USE0[f"x{l}"]
                wait_emptied(pe, n_u - 1)
                for h in range(XH + 1):
                    if h < XH:
                        for qt in range(TT):
                            u = n_u + x_score(h) + qt
                            wait_emptied(pe, u - 4)
                            for c in range(2):
                                last = pe.matmul(pw[u % 4][:, 0:T], q_t[:, 2 * h + c, qt * P:qt * P + P],
                                                 k_t[:, 2 * h + c, :], start=(c == 0), stop=(c == 1))
                            last.then_inc(mm_done, 1)
                    if h >= 1:
                        g = h - 1
                        for qt in range(TT):
                            u = n_u + x_turn(g) + qt
                            wait_emptied(pe, u - 4)
                            pe.wait_ge(S(name + "_prob"), 2 * g + qt + 1)
                            for kt in range(TT):
                                last = pe.transpose(pw[u % 4][:, kt * P:kt * P + P],
                                                    prob[:, g % 2, qt, kt * P:kt * P + P], ident[:])
                            last.then_inc(mm_done, 1)
                        u = n_u + x_turn(g) + 2
                        wait_emptied(pe, u - 4)
                        wait_emptied(pe, u - 1)
                        for dc in range(2):
                            for kt in range(TT):
                                last = pe.matmul(pw[u % 4][:, dc * T:dc * T + T],
                                                 v_m[:, kt, h_cols(g, dc)], pt[:, g % 2, kt, :],
                                                 start=(kt == 0), stop=(kt == TT - 1))
                        last.then_inc(mm_done, 1)

            def h_cols(h, dc):
                return slice(h * 256 + dc * P, h * 256 + dc * P + P)

            def glu(name, J, pair, hook=None):
                base, u0 = S0[name], USE0[name]
                v0 = emptied(u0 - 1, "v")
                drain(u0)

                def bank_free(j, jj, kind):
                    if j < 2:
                        return
                    pe.wait_ge(empty_v, (jj + -2).of(lambda n: v0 + 2 * n + (1 if kind == "g" else 2)))

                def row(j, jj, s, last=False):
                    pe.wait_ge(S(name + "_hid_lo"), (jj + 1).of(lambda n: n))
                    row_slab(s, j % 4, j == 0, last)

                def step(j, i=None):
                    st, st4 = (12, 4) if i is not None else (0, 0)
                    g, jj = At(glu_slab(base, J, "g", j), st, i), At(j, st4, i)
                    bank_free(j, jj, "g")
                    col_slab(g, u0 + 2 * j, ah, al, None, pair_ready(pair) if j == 0 else None)
                    bank_free(j, jj, "u")
                    col_slab(g + 1, u0 + 2 * j + 1, ah, al)
                    if j == 0 and hook:
                        hook()
                    if j >= 2:
                        if j == 2:
                            pe.wait_ge(acc_out, KC * ACCS[name])
                            pe.wait_ge(rstd_b_ready, NORMS[name] + 1)
                        row(j - 2, jj + -2, g + 2)

                trips, rest = glu_steps(J)
                for j in range(4):
                    step(j)
                with pe.Fori(0, trips) as i:
                    for j in range(4, 8):
                        step(j, i)
                for j in range(rest, J):
                    step(j)
                for j in (J - 2, J - 1):
                    row(j, At(j), At(glu_slab(base, J, "d", j)), last=(j == J - 1))

            pe.wait_ge(S("ones"), 1)
            sq_sums("ab")

            def abin_hook(k):
                if k == 1:
                    norm_spread("ab")
                if k == 2:
                    sq_sums_mem()
                if k == 6:
                    norm_spread("mem")

            def sq_sums_mem():
                pe.wait_ge(rstd_b_ready, NORMS["ab"] + 1)
                sq_sums("mem")

            col_phase("abin", 20, ah, al, pair_ready("abin"), abin_hook, straight=8)
            col_phase("k0", 8, mh, ml, lambda k: pe.wait_ge(S("m_lo"), k + 1))
            for n in range(4):
                s = At(S0["gates"] + n)
                wait_split(pe, s)
                for e in range(2):
                    h, u = 2 * n + e, USE0["gates"] + 3 * n + e
                    wait_emptied(pe, u - 4)
                    pe.wait_ge(S("xr_lo"), h + 1)
                    for g in range(2):
                        last = tile3(pw[u % 4][:, g * T:g * T + T], s, 2 * e + g, yh[:, h, :], yl[:, h, :],
                                     True, True)
                    last.then_inc(S("gate_products"), 1)
                u = USE0["gates"] + 3 * n + 2
                wait_emptied(pe, u - 4)
                pe.wait_ge(S("pooled_lo"), n + 1)
                tile3(pw[u % 4][:, 0:T], s, 4, yh[:, 8 + n, :], yl[:, 8 + n, :], True, True) \
                    .then_inc(slab_done, 1)
            for half in range(2):
                values(S0["v0"], USE0["v0"], mh, ml, half)
            row_phase("about", [8, 9, 10, 11, 0, 1, 2, 3, 4, 5, 6, 7],
                      lambda k: pe.wait_ge(S("yb_lo"), k - 7) if k >= 8 else pe.wait_ge(S("ya_lo"), k + 1), "mem")

            def spread_hook(name):
                return lambda k=1: norm_spread(name) if k == 1 else None

            def cross_layer(l):
                sq_sums(f"xa{l}")
                col_phase(f"q{l}", 8, ah, al, pair_ready(f"q{l}"), spread_hook(f"xa{l}"))
                cross(l)
                row_phase(f"wo{l}", range(8),
                          lambda k: wait_emptied(pe, USE0[f"x{l}"] + x_turn(k // 2) + 2), f"xa{l}")
                sq_sums(f"f{l}")
                glu(f"f{l}", FJ, f"f{l}", lambda: norm_spread(f"f{l}"))

            cross_layer(0)
            sq_sums("c")
            col_phase("pw1", 16, ah, al, pair_ready("pw1"), spread_hook("c"))
            col_phase("k1", 8, mh, ml, lambda k: pe.wait_ge(S("m_lo"), KC + k + 1))
            for half in range(2):
                values(S0["v1"], USE0["v1"], mh, ml, half)
            pe.wait_ge(rstd_b_ready, NORMS["c"] + 1)
            norm_sums("lnmean", cv, lambda c: pe.wait_ge(S("conv_out"), c + 1))
            norm_spread("lnmean")
            sq_sums("ln")
            norm_spread("ln")
            row_phase("pw2", range(8), lambda k: pe.wait_ge(S("ln_lo"), k + 1), "ln")
            cross_layer(1)
            sq_sums("final")
            norm_spread("final")
            sq_sums("mix")
            col_phase("win", 32, ah, al, pair_ready("win"), spread_hook("mix"))
            for b in range(3):
                values(S0["win"] + 32 + 4 * b, USE0["win"] + 32 + 2 * b, ah, al, 0)
            s, u = At(S0["win"] + 44), USE0["win"] + 38
            wait_emptied(pe, u - 4)
            col_slab(s, u, ah, al)
            s, u = s + 1, u + 1
            wait_split(pe, s)
            for q in range(TT):
                wait_emptied(pe, u + q - 4)
                dst, slot, tk = pw[(u + q) % 4][:, 0:P], s.base % SPLIT, slice(q * P, q * P + P)
                for k in range(KC):
                    w = slice(k * P, k * P + P)
                    pe.matmul(dst, ah[:, k, tk], wh[:, slot, w], start=(k == 0), stop=False)
                    pe.matmul(dst, ah[:, k, tk], wl[:, slot, w], start=False, stop=False)
                    last = pe.matmul(dst, al[:, k, tk], wh[:, slot, w], start=False, stop=(k == KC - 1))
            last.then_inc(slab_done, 1)
            col_phase("win", 16, ah, al, s_off=46, u_off=41)
            n_u = USE0["attn2"]
            for m in range(len(HEADS2) + 1):
                if m < len(HEADS2):
                    kind, h = HEADS2[m]
                    for qt in range(TT):
                        nk = P * (qt + 1)
                        for g in range(groups(kind)):
                            u = n_u + a_score(m) + qt * groups(kind) + g
                            qc, kc, half = heads_at(kind, h, g)
                            wait_emptied(pe, u - 4)
                            pe.matmul(pw[u % 4][:, 0:nk], q2[half:half + 64, qc, qt * P:qt * P + P],
                                      k2[half:half + 64, kc, 0:nk], start=True, stop=True).then_inc(mm_done, 1)
                if m >= 1:
                    kind, h = HEADS2[m - 1]
                    G_ = groups(kind)
                    pe.wait_ge(S("attn2_prob"), 2 * m)
                    for g in range(G_):
                        u = n_u + a_turn(m - 1) + g
                        wait_emptied(pe, u - 4)
                        b, s_ap = pw[u % 4], sc[:, (m - 1) % 2, :]
                        pe.transpose(b[:, 0:P], s_ap[:, g * P:g * P + P], ident[:])
                        for kt in range(2):
                            a = 3 * P + g * 2 * P + kt * P
                            last = pe.transpose(b[:, (1 + kt) * P:(2 + kt) * P], s_ap[:, a:a + P], ident[:])
                        last.then_inc(mm_done, 1)
                    u = n_u + a_turn(m - 1) + G_
                    wait_emptied(pe, u - 4)
                    wait_emptied(pe, u - 1)
                    c, half = mixed_at(kind, h)
                    for g in range(G_):
                        va = 512 * g + 64 * h if kind == "d" else 1536 + 64 * (h // 8)
                        dst = pw[u % 4][half:half + 64, :]
                        pe.matmul(dst[:, 0:T], v2[:, 0, va:va + 64], pt2[:, g, 0:T], start=(g == 0), stop=False,
                                  skip_group_check=True)
                        last = pe.matmul(dst[:, P:T], v2[:, 1, va:va + 64], pt2[:, g, T:3 * P], start=False,
                                         stop=(g == G_ - 1), skip_group_check=True)
                    last.then_inc(mm_done, 1)
            row_phase("brd", range(4), lambda k: wait_emptied(pe, n_u + a_turn(2 * k + 1) + 3), "mix")
            row_phase("brs", range(4, 12), lambda k: wait_emptied(pe, n_u + a_turn(8 + 8 + k - 4) + 1), None)
            row_phase("wout", range(8), lambda k: pe.wait_ge(S("mixed_lo"), k + 1), None)
            sq_sums("moe")
            norm_spread("moe")
            pe.wait_ge(S("router_in"), 16)
            pe.wait_ge(S("h_ready"), KC)
            for q in range(TT):
                for c in range(KC):
                    last = pe.matmul(acc[1][:, 64 * q:64 * q + 36], hf[:, c, q * P:q * P + P], rw[:, c, :],
                                     start=(c == 0), stop=(c == KC - 1))
            last.then_inc(S("router_full"), 1)
            drain(USE0["attn2"] + len(_attn2_uses()))
            for j in range(4):
                for n in range(4):
                    last = pe.transpose(pw[j][:, n * P:n * P + P],
                                        hf[:, 4 * (j % 2) + n, (j // 2) * P:(j // 2) * P + P], ident[:])
                last.then_inc(S("h_turned"), 1)
            pe.wait_ge(S("chosen"), 1)
            pe.matmul(acc[2][:, 0:NE], until, chosen[:, 0, :], start=True, stop=True)
            pe.wait_ge(S("chosen"), 2)
            pe.matmul(acc[2][:, NE:2 * NE], ones[:], chosen[:, 0, :], start=True, stop=False)
            pe.matmul(acc[2][:, NE:2 * NE], until, chosen[:, 1, :], start=False, stop=True)
            pe.matmul(acc[2][:, 2 * NE:3 * NE], ones[:], chosen[:, 0, :], start=True, stop=False)
            pe.matmul(acc[2][:, 2 * NE:3 * NE], ones[:], chosen[:, 1, :], start=False, stop=True) \
                .then_inc(S("places"), 1)

            def gather(j):
                for n in range(2):
                    c = 2 * (j.base % 4) + n
                    for q in range(TT):
                        for part in (htok_hi, htok_lo):
                            last = pe.matmul(pw[gather_bank(j.base)][:, n * T:n * T + T],
                                             part[:, q, c * P:c * P + P], onehot[:, j.base // 4 % 2, q, :],
                                             start=(q == 0 and part is htok_hi), stop=(q == 1 and part is htok_lo))
                last.then_inc(S("gathered"), 1)

            def rows3(dst, hi, lo, slot, w, first, last):
                pe.matmul(dst, hi, wh[:, slot, w], start=first, stop=False, skip_group_check=True)
                pe.matmul(dst, hi, wl[:, slot, w], start=False, stop=False, skip_group_check=True)
                return pe.matmul(dst, lo, wh[:, slot, w], start=False, stop=last, skip_group_check=True)

            def turn(p):
                pe.wait_ge(S("hidden_done"), (p + 1).of(lambda n: n))
                for c in range(DE // P):
                    last = pe.transpose(pw[2][:, c * P:c * P + P], hide[:, c * P:c * P + P], ident[:])
                last.then_inc(S("hidden_turned"), 1)

            def turn_slots(p):
                w = slice(2 * CAP * (p.base % 2), 2 * CAP * (p.base % 2) + 2 * CAP)
                hot = [onehot[:, p.base // 2 % 2, q, w].bitcast(F32) for q in range(TT)]
                for q in range(TT):
                    pe.transpose(pw[3][:, q * P:q * P + P], hot[q], ident[:])
                for q in range(TT):
                    g = gates[:, q, 2 * p.base:2 * p.base + 2] if p.i is None else \
                        gates[:, q, bass.ds(p.i * (2 * p.step) + 2 * p.base, 2)]
                    last = pe.matmul(pw[3][:, T:T + 2], hot[q], g, start=(q == 0), stop=(q == 1))
                last.then_inc(S("slots_turned"), 1)

            def zero_sums(first):
                for c in range(KC):
                    last = pe.matmul(acc_of(c), zeros[:, 0:P], zeros[:], start=(first and c % 2 == 0),
                                     stop=not first, skip_group_check=True)
                return last

            def scatter(p, i):
                pp = per_trip(p, i)
                pe.wait_ge(S("expert_out_lo"), pp.of(lambda n: 2 * n + 2))
                pe.wait_ge(S("slots_turned_out"), (pp + 1).of(lambda n: n))
                for c in range(KC):
                    for part in (ye_hi, ye_lo):
                        last = pe.matmul(acc_of(c), part[:, c * P:c * P + P], back[:, p % 2, :],
                                         start=False, stop=(p == PAIRS_E - 1 and part is ye_lo),
                                         skip_group_check=True)
                last.then_inc(S("scattered"), 1)

            def down(p, s0, i):
                for n in range(8):
                    s = At(s0 + n, 96 if i is not None else 0, i)
                    e, k = n // 4, n % 4
                    wait_split(pe, s)
                    sl = slice(CAP * e, CAP * e + P)
                    for h in range(2):
                        last = rows3(pw[2 + h][:, :], ht_hi[:, k, sl], ht_lo[:, k, sl], s.base % SPLIT,
                                     slice(512 * h, 512 * h + 512), n == 0, n == 7)
                    last.then_inc(slab_done, 1)

            def period(p, i):
                pp = per_trip(p, i)
                if p:
                    pe.wait_ge(S("hidden_done"), pp.of(lambda n: n))
                if p % 2 == 0:
                    pe.wait_ge(S("gathered_lo"), pp.of(lambda n: 2 * n + 4))
                par = p // 2 % 2
                for n in range(16):
                    s = At(gu_slab(p) + n, 96 if i is not None else 0, i)
                    e, k = n // 8, n % 8
                    wait_split(pe, s)
                    m, sl = 2 * k + p % 2, slice(CAP * e, CAP * e + P)
                    for h in range(2):
                        last = rows3(pw[h][:, :], xg_hi[:, par, m, sl], xg_lo[:, par, m, sl],
                                     s.base % SPLIT, slice(512 * h, 512 * h + 512), n == 0, n == 15)
                    last.then_inc(slab_done, 1)
                    if n == 3 and p >= 1:
                        if p >= 2:
                            pe.wait_ge(S("expert_out_lo"), pp.of(lambda n: 2 * n - 2))
                        else:
                            pe.wait_ge(S("gathered_lo"), 6)
                        turn(pp + -1)
                    if n == 5 and p == 1:
                        zero_sums(True)
                    if n == 5 and p >= 2:
                        scatter(p - 2, i)
                    if n == 7 and p < 14:
                        if p % 2 == 0:
                            pe.wait_ge(S("onehot"), pp.of(lambda n: n + 4))
                        if p:
                            pe.wait_ge(S("slot_gates"), pp.of(lambda n: 2 * n))
                        gather(At(4 + 2 * p, 8 if i is not None else 0, i))
                    if n == 9 and p < 14:
                        if p >= 1:
                            pe.wait_ge(S("hidden_turned_lo"), pp.of(lambda n: n))
                        gather(At(5 + 2 * p, 8 if i is not None else 0, i))
                    if n == 11:
                        if p < 14:
                            pe.wait_ge(S("gathered_lo"), pp.of(lambda n: 2 * n + 5))
                        turn_slots(pp)
                if p >= 1:
                    pe.wait_ge(S("hidden_turned_lo"), pp.of(lambda n: n))
                    if p < 14:
                        pe.wait_ge(S("gathered_lo"), pp.of(lambda n: 2 * n + 6))
                    pe.wait_ge(S("slots_turned_out"), (pp + 1).of(lambda n: n))
                    pe.wait_ge(S("slot_gates"), (pp + 1).of(lambda n: 2 * n))
                    down(p - 1, gu_slab(p) + 16, i)

            pe.wait_ge(S("h_turned_lo"), 4)
            pe.wait_ge(S("zeros"), 1)
            pe.wait_ge(S("pads"), 4)
            pe.wait_ge(S("onehot"), 2)
            for j in range(4):
                gather(At(j))
            period(0, None)
            period(1, None)
            with pe.Fori(0, 3) as i:
                for p in range(2, 6):
                    period(p, i)
            period(14, None)
            period(15, None)
            last_p = PAIRS_E - 1
            pe.wait_ge(S("expert_out_lo"), 2 * last_p)
            turn(At(last_p))
            scatter(last_p - 1, None)
            pe.wait_ge(S("hidden_turned_lo"), PAIRS_E)
            down(last_p, NSLAB - 8, None)
            scatter(last_p, None)
            over = pe.value_load(overflow[0:1, 0:1], min_val=0, max_val=1)
            with pe.If(over > 0):
                last = zero_sums(True)
                last.then_inc(S("dense_down"), 1)
                with pe.Fori(0, NE) as i:
                    pe.wait_ge(S("dense_in"), i * (16 * EXPERT) + 16 * EXPERT)
                    for q in range(TT):
                        for h in range(2):
                            for k in range(KC):
                                last = pe.matmul(pw[2 * q + h][:, :], hf[:, k, q * P:q * P + P],
                                                 raw[:, k, 512 * h:512 * h + 512], start=(k == 0), stop=(k == KC - 1))
                    last.then_inc(S("dense_products"), 1)
                    pe.wait_ge(S("dense_hidden"), i * 2 + 2)
                    for c in range(DE // P):
                        for q in range(TT):
                            a = (c % 2) * T + q * P
                            last = pe.transpose(pw[c // 2][:, a:a + P], dense_hid[:, q, c * P:c * P + P], ident[:])
                    last.then_inc(S("dense_turns"), 1)
                    pe.wait_ge(S("dense_turned"), i * 2 + 2)
                    for k in range(DE // P):
                        for c in range(KC):
                            last = pe.matmul(acc_of(c), raw[:, 8 + k, c * P:c * P + P], dense_turned[:, k, :],
                                             start=False, stop=False, skip_group_check=True)
                    last.then_inc(S("dense_down"), 1)
                last = zero_sums(False)
                last.then_inc(S("dense_down"), 1)
            sq_sums("out")
            norm_spread("out")


def x_score(h):
    return 0 if h == 0 else 2 + 5 * (h - 1)


def x_turn(h):
    return 2 + 5 * h + (2 if h < XH - 1 else 0)


def a_score(m):
    n = 0
    for k in range(m):
        n += 2 * groups(HEADS2[k][0]) + (groups(HEADS2[k - 1][0]) + 1 if k >= 1 else 0)
    return n


def a_turn(m):
    return a_score(m + 1) + (2 * groups(HEADS2[m + 1][0]) if m + 1 < len(HEADS2) else 0)


def heads_at(kind, h, g):
    if kind == "d":
        n = 8 * g + h
        return n // 2, n // 2, 64 * (n % 2)
    return 12 + h % 8, 12, 64 * (h // 8)


def mixed_at(kind, h):
    return (h // 2, 64 * (h % 2)) if kind == "d" else (4 + h % 8, 64 * (h // 8))


def _channels(v):
    return np.asarray(v).reshape(-1, P).T


def _col_slabs(w):
    k, n = w.shape
    return w.reshape(k // P, P, n // P, P).transpose(2, 1, 0, 3).reshape(n // P, P, SLAB)


def _row_slabs(w):
    return w.reshape(-1, P, SLAB)


def _value_slabs(w):
    return w.reshape(4, 2, P, -1, 512).transpose(3, 0, 2, 1, 4).reshape(-1, P, SLAB)


def _glu_slabs(g, u, d, J):
    out = np.empty((3 * J, P, SLAB), np.float32)
    for j in range(J):
        out[glu_slab(0, J, "g", j)] = g[j]
        out[glu_slab(0, J, "u", j)] = u[j]
        out[glu_slab(0, J, "d", j)] = d[j]
    return out


def _taps(w):
    k = w.shape[0]
    return w.reshape(k, -1, P).transpose(2, 1, 0).reshape(P, -1)


def _layout(i):
    a = {k: np.asarray(v) for k, v in i.items()}
    w_in = a["ab_w_in"][0]
    gates = np.zeros((4, P, SLAB), np.float32)
    for n in range(4):
        for e in range(2):
            gates[n, :, (2 * e) * P:(2 * e + 1) * P] = a["a_gate_x_w"][0, 2 * n + e]
            gates[n, :, (2 * e + 1) * P:(2 * e + 2) * P] = a["a_gate_a_w"][0, 2 * n + e]
        gates[n, :, 4 * P:5 * P] = a["b_group_w"][0, n]
    pw1 = _col_slabs(a["c_w_pw1"][0])
    pw1 = np.stack([pw1[:8], pw1[8:]], 1).reshape(16, P, SLAB)
    w2 = a["w_in_2"][0]
    at = np.cumsum([0, 1536, 1536, 1536, 1024, 128, 128, 1024, 1024])
    qd, kd, vd, qs, ks, vs, gd, gs = (w2[:, at[n]:at[n + 1]] for n in range(8))
    qs = qs.reshape(D, 2, 8, 64).transpose(0, 2, 1, 3).reshape(D, D)
    win = [_col_slabs(qd), _col_slabs(kd), _col_slabs(qs), _value_slabs(vd), _col_slabs(ks), _col_slabs(vs),
           _col_slabs(gd), _col_slabs(gs)]
    br_swa = a["w_br_swa_2"][0].reshape(2, 8, 64, D).transpose(1, 0, 2, 3).reshape(D, D)
    about = _row_slabs(a["ab_w_out"][0])[[8, 9, 10, 11, 0, 1, 2, 3, 4, 5, 6, 7]]

    def ffn(l):
        up = _col_slabs(a["f_w_up"][l])
        return _glu_slabs(up[:FJ], up[FJ:], _row_slabs(a["f_w_down"][l]), FJ)

    both = np.concatenate([a["w_e_gate_2"][0], a["w_e_up_2"][0]], 2).reshape(NE, KC, P, SLAB)
    experts = np.concatenate([both, a["w_e_down_2"][0].reshape(NE, DE // P, P, SLAB)], 1).reshape(-1, P, SLAB)
    parts = [_col_slabs(w_in), _col_slabs(a["xa_wk"][0]), gates, _value_slabs(a["xa_wv"][0]), about,
             _col_slabs(a["xa_wq"][0]), _row_slabs(a["xa_wo"][0]), ffn(0), pw1, _col_slabs(a["xa_wk"][1]),
             _value_slabs(a["xa_wv"][1]), _row_slabs(a["c_w_pw2"][0]), _col_slabs(a["xa_wq"][1]),
             _row_slabs(a["xa_wo"][1]), ffn(1), *win, _row_slabs(a["w_br_dil_2"][0]), _row_slabs(br_swa),
             _row_slabs(a["w_out_2"][0]), experts]
    stream = np.concatenate(parts)
    assert stream.shape == (NSLAB, P, SLAB), stream.shape
    rows = np.broadcast_to
    cols = {"ab_norm": _channels(a["ab_norm"][0]), "a_conv_w": _taps(a["a_conv_w"][0]),
            "a_conv_b": _channels(a["a_conv_b"][0]), "a_gate_x_b": _channels(a["a_gate_x_b"][0]),
            "a_gate_a_b": _channels(a["a_gate_a_b"][0]), "a_lambda": _channels(a["a_lambda"][0]),
            "b_group_b": _channels(a["b_group_b"][0]), "b_scale": _channels(a["b_scale"][0]),
            "c_norm": _channels(a["c_norm"][0]), "c_b_pw1": _channels(a["c_b_pw1"][0]),
            "c_dw_w": _taps(a["c_dw_w"][0]), "c_dw_b": _channels(a["c_dw_b"][0]),
            "c_ln_g": _channels(a["c_ln_g"][0]), "c_ln_b": _channels(a["c_ln_b"][0]),
            "c_b_pw2": _channels(a["c_b_pw2"][0]),
            "final_norm": _channels(a["final_norm"]), "g_mix": _channels(a["g_mix_2"][0]),
            "g_ffn": _channels(a["g_ffn_2"][0]), "g_final": _channels(a["g_final_2"]),
            "sinks": rows(a["sinks_2"][0], (P, 16)),
            "r_bias": rows(np.concatenate([a["b_group_2"][0], a["b_router_2"][0]]), (P, 36))}
    for l in range(2):
        cols[f"xa_norm{l}"] = _channels(a["xa_norm"][l])
        cols[f"mem_norm{l}"] = _channels(a["xa_mem_norm"][l])
        cols[f"f_norm{l}"] = _channels(a["f_norm"][l])
        cols[f"f_dw_w{l}"] = _taps(a["f_dw_w"][l])
        cols[f"f_dw_b{l}"] = _channels(a["f_dw_b"][l])
    packed = np.concatenate([cols[name] for name, _ in COLS], 1)
    tok = np.arange(T)
    inv = np.stack([1.0 / np.minimum(tok + 1, w) for w in POOLS]).reshape(1, -1)
    konst = np.concatenate([np.eye(P), np.broadcast_to(inv, (P, 4 * T))], 1).astype(np.float32)
    dist = tok[:, None] - tok[None, :]
    kinds = [(dist >= 0) & (dist <= 128), (dist >= 0) & (dist % 4 == 0), (dist >= 0) & (dist % 16 == 0),
             (dist >= 0) & (dist <= 127)]
    masks = np.empty((P, 4, 3 * P), np.float32)
    for n, ok in enumerate(kinds):
        m = np.where(ok, dist, -NEG)
        masks[:, n, :P] = m[:P, :P]
        masks[:, n, P:] = m[P:, :]
    def turned(v):
        return np.ascontiguousarray(np.asarray(v)[0].T.reshape(KC, P, T).transpose(1, 0, 2))

    router = np.concatenate([a["w_group_2"][0], a["w_router_2"][0]], 1).reshape(KC, P, 36).transpose(1, 0, 2)
    router = np.concatenate([router.reshape(P, -1), np.triu(np.ones((P, P), np.float32)),
                             np.broadcast_to(np.arange(1, CAP + 1, dtype=np.float32), (P, CAP))], 1)
    return {"stream": stream, "cols": packed, "konst": konst, "masks": masks, "x": turned(a["x"]),
            "mem": turned(a["mem"]), "router": router}


def kernel(**inputs):
    import concourse.bacc as bacc
    from concourse.bass_utils import run_bass_kernel_spmd

    nc = bacc.Bacc("TRN2", target_bir_lowering=False, num_devices=1)
    arrays, args = {}, []
    for name, a in _layout(inputs).items():
        arrays[f"in_{name}"] = np.ascontiguousarray(a)
        args.append(nc.dram_tensor(f"in_{name}", a.shape, F32, kind="ExternalInput").ap())
    args.append(nc.dram_tensor("out", (P, KC, T), F32, kind="ExternalOutput").ap())
    program(nc, *args)
    got = run_bass_kernel_spmd(nc, [arrays], core_ids=[0]).results[0]["out"]
    return got.transpose(1, 0, 2).reshape(D, T).T[None]
```

```python
from contextlib import ExitStack, contextmanager

import numpy as np

import concourse.bass as bass
from concourse import mybir

F32 = mybir.dt.float32
F32R = mybir.dt.float32r
ACT = mybir.ActivationFunctionType
ALU = mybir.AluOpType
AX = mybir.AxisListType

P = 128
T = 256
TT = T // P
D = 1024
KC = D // P
SLAB = 1024
EPS = 1e-6
NEG = -1e30
FF = 3 * D
FJ = FF // P
NE = 32
DE = 512
CAP = 64
PAIRS_E = NE // 2
EXPERT = 12
CONV_A, CONV_C, CONV_F = 4, 31, 3
POOL_CONV = 2
XH = 4
POOLS = (2, 4, 8, 16)
RAW = 12
HALF = RAW // 2
SPLIT = 4
AHEAD = 3
SLOPES_DIL = [2.0 ** (-8.0 * (h + 1) / 24) for h in range(24)]
SLOPES_SWA = [2.0 ** (-8.0 * (h + 1) / 16) for h in range(16)]

PHASES = [("abin", 20), ("k0", 8), ("gv", 12), ("about", 12), ("q0", 8), ("wo0", 8),
          ("f0", 3 * FJ), ("pw1", 16), ("k1", 8), ("v1", 8), ("pw2", 8), ("q1", 8), ("wo1", 8),
          ("f1", 3 * FJ), ("win", 62), ("brd", 4), ("brs", 8), ("wout", 8), ("moe", EXPERT * NE)]
S0, _n = {}, 0
for _name, _k in PHASES:
    S0[_name] = _n
    _n += _k
NSLAB = _n

COLS = [("ab_norm", 8), ("a_conv_w", 8 * CONV_A), ("a_conv_b", 8), ("a_gate_x_b", 8), ("a_gate_a_b", 8),
        ("a_lambda", 8), ("b_group_b", 4), ("b_scale", 4), ("c_norm", 8), ("c_b_pw1", 16),
        ("c_dw_w", 8 * CONV_C), ("c_dw_b", 8), ("c_ln_g", 8), ("c_ln_b", 8), ("c_b_pw2", 8),
        ("xa_norm0", 8), ("xa_norm1", 8), ("mem_norm0", 8), ("mem_norm1", 8), ("f_norm0", 8), ("f_norm1", 8),
        ("f_dw_w0", FJ * CONV_F), ("f_dw_w1", FJ * CONV_F), ("f_dw_b0", FJ), ("f_dw_b1", FJ),
        ("final_norm", 8), ("g_mix", 8), ("g_ffn", 8), ("g_final", 8), ("sinks", 16), ("r_bias", 36)]
C0, _n = {}, 0
for _name, _k in COLS:
    C0[_name] = _n
    _n += _k
NCOL = _n

USES, USE0 = [], {}


def _uses(name, who):
    USE0[name] = len(USES)
    USES.extend(who)


def _attn_uses(n):
    out = []
    for h in range(n + 1):
        if h < n:
            out += ["a", "a"]
        if h >= 1:
            out += ["a", "a", "v"]
    return out


HEADS2 = [("d", h) for h in range(8)] + [("s", h // 2 + 8 * (h % 2)) for h in range(16)]


def groups(kind):
    return 3 if kind == "d" else 1


def fill2(m):
    if m < 8:
        return [("win", 46 + 2 * m), ("win", 47 + 2 * m)]
    if m in (9, 10):
        return [("brd", 2 * m - 18), ("brd", 2 * m - 17)]
    if m >= 12 and m % 2 == 0:
        return [("brs", (m - 12) // 2)]
    return []


A2, A2MM, _a2 = {}, {}, []
for _m in range(len(HEADS2) + 1):
    _steps = []
    if _m < len(HEADS2):
        _steps += [(("score", _m, _q, _g), "v") for _q in range(TT) for _g in range(groups(HEADS2[_m][0]))]
    _fills = [(("fill", _n), "v") for _p, _n in fill2(_m) if _p == "win"]
    if _m >= 1:
        _steps += [(("turn", _m - 1, _g), "a") for _g in range(groups(HEADS2[_m - 1][0]))] + _fills[:1]
        _steps += [(("mix", _m - 1), "v")] + _fills[1:]
    else:
        _steps += _fills
    for _key, _who in _steps:
        A2[_key] = len(_a2)
        A2MM[_key] = sum(1 for _k in A2 if _k[0] != "fill")
        _a2.append(_who)

_uses("abin", "v" * 20)
_uses("k0", "v" * 8)
_uses("gates", "aav" * 4)
_uses("q0", "v" * 8)
_uses("x0", _attn_uses(XH))
_uses("f0", "vv" * FJ)
_uses("pw1", "v" * 16)
_uses("k1", "v" * 8)
_uses("v1", "v" * 4)
_uses("q1", "v" * 8)
_uses("x1", _attn_uses(XH))
_uses("f1", "vv" * FJ)
_uses("win", "v" * (32 + 6 + 3))
_uses("attn2", _a2)


def emptied(u, who=None):
    who = who or USES[u]
    return sum(1 for w in USES[:u + 1] if w == who)


MM0 = {}
_n = 0
for _name, _k in (("x0", len(_attn_uses(XH))), ("x1", len(_attn_uses(XH))), ("attn2", sum(1 for _k in A2 if _k[0] != "fill"))):
    MM0[_name] = _n
    _n += _k

NORMS = {n: i for i, n in enumerate(
    ["ab", "mem", "xa0", "f0", "c", "lnmean", "ln", "xa1", "f1", "final", "mix", "moe", "out"])}


def spread_no(name):
    return NORMS[name] + (name != "out")


PAIRS = {n: i for i, n in enumerate(["abin", "q0", "f0", "pw1", "q1", "f1", "win", "moe"])}
ACCS = {n: i for i, n in enumerate(["about", "wo0", "f0", "pw2", "wo1", "f1", "brd", "brs", "wout", "moe"])}

KB = 1024
MAP = [("raw", 48), ("wh", 16), ("wl", 16), ("x", 8), ("ah", 8), ("al", 8), ("mh", 8), ("ml", 8),
       ("yh", 12), ("yl", 12), ("arena", 46), ("konst", 6.5), ("cols", 3.25), ("tmp", 7), ("memr", 1)]
OFF, _o = {}, 0
for _name, _k in MAP:
    OFF[_name] = _o
    _o += int(_k * KB)


def glu_slab(base, J, kind, j):
    if kind == "d":
        return base + (6 + 3 * j if j <= J - 3 else 3 * J - (J - j))
    g = 2 * j if j < 2 else 4 + 3 * (j - 2)
    return base + g + (kind == "u")


def gate_slab(n):
    return S0["gv"] + 3 * n


def v0_slab(k):
    return S0["gv"] + 3 * (k // 2) + 1 + k % 2


SHORT0, SHORT1 = -(-S0["win"] // RAW) * RAW, S0["moe"] // RAW * RAW


def slot_of(s):
    return s % (HALF if SHORT0 <= s < SHORT1 else RAW)


def fills_of(s):
    if s < SHORT0:
        return s // RAW + 1
    if s < SHORT1:
        return SHORT0 // RAW + (s - SHORT0) // HALF + 1
    return s // RAW + 1 + ((SHORT1 - SHORT0) // HALF - (SHORT1 - SHORT0) // RAW if s % RAW < HALF
                           else -((SHORT1 - SHORT0) // RAW))


def back_to_same(s):
    if SHORT0 + HALF <= s < SHORT1 + HALF:
        return HALF
    return SHORT1 - SHORT0 + RAW if SHORT1 + HALF <= s < SHORT1 + RAW else RAW


class At:

    def __init__(self, base, step=0, i=None):
        self.base, self.step, self.i = base, step, i

    def __add__(self, k):
        return At(self.base + k, self.step, self.i)

    def of(self, f):
        a = f(self.base)
        if self.i is None:
            return a
        return self.i * (f(self.base + self.step) - a) + a


class Program:

    def __init__(self, eng, chain):
        self.eng, self.chain, self.count, self.last, self.before = eng, chain, {}, None, []

    def done(self, ins, sem=None):
        sem = self.chain if sem is None else sem
        if self.last is not None:
            self.before = self.before[-1:] + [(self.last, self.count[self.last.name])]
        ins.then_inc(sem, 1)
        base, k = self.count.get(sem.name, (None, 0))
        self.count[sem.name] = (base, k + 1)
        self.last = sem

    def fence(self, back=0):
        if self.last is not None:
            sem, (base, k) = self.before[-back] if back else (self.last, self.count[self.last.name])
            self.eng.wait_ge(sem, k if base is None else base + k)

    @contextmanager
    def loop(self, trips, raised, last):
        self.fence()
        before = {s.name: self.count.get(s.name, (None, 0))[1] for s in raised}
        with self.eng.Fori(0, trips) as i:
            for s, k in raised.items():
                self.count[s.name] = (i * k + before[s.name], 0)
            self.last = last
            yield i
            for s, k in raised.items():
                assert self.count[s.name][1] == k, (s.name, self.count[s.name][1], k)
        for s, k in raised.items():
            self.count[s.name] = (None, before[s.name] + k * trips)
        self.last = last


def program(nc, stream, cols_in, konst_in, masks_in, x_in, mem_in, router_in, out):
    ctx = ExitStack()
    with ctx:
        first_free = (nc.sbuf_base + 63) // 64 * 64

        def sb(name, where, at_kb, shape, dt=F32):
            return nc.alloc_sbuf_tensor_at(name, shape, dt, offset=first_free + OFF[where] + int(at_kb * KB))

        sems = {}

        def S(name):
            if name not in sems:
                sems[name] = ctx.enter_context(nc.semaphore(name))
            return sems[name]

        raw = sb("raw", "raw", 0, [P, RAW, SLAB])
        wh = sb("wh", "wh", 0, [P, SPLIT, SLAB], F32R)
        wl = sb("wl", "wl", 0, [P, SPLIT, SLAB], F32R)
        x = sb("x_res", "x", 0, [P, KC, T])
        ah = sb("ah", "ah", 0, [P, KC, T], F32R)
        al = sb("al", "al", 0, [P, KC, T], F32R)
        mh = sb("mh", "mh", 0, [P, KC, T], F32R)
        ml = sb("ml", "ml", 0, [P, KC, T], F32R)
        yh = sb("yh", "yh", 0, [P, 12, T], F32R)
        yl = sb("yl", "yl", 0, [P, 12, T], F32R)
        mem = sb("mem_t", "yh", 4, [P, KC, T])
        cols = sb("cols", "cols", 0, [P, NCOL])
        ident = sb("ident", "konst", 0, [P, P])
        inv = sb("inv_count", "konst", 0.5, [P, 4, T])
        masks = sb("masks", "konst", 0.5, [P, 4, 3 * P])
        q_t = sb("q_t", "arena", 0, [P, KC, T])
        sq = sb("sq", "arena", 0, [P, KC, T])
        k_t = sb("k_t", "arena", 8, [P, KC, T])
        v_m = sb("v_m", "arena", 16, [P, TT, D])
        z = sb("z", "arena", 24, [P, 20, T])
        xr = sb("xr", "ah", 0, [P, KC, T])
        a_t = sb("a_t", "al", 0, [P, KC, T])
        pt = sb("pt", "arena", 24, [P, 2, TT, T])
        prob = sb("prob", "arena", 28, [P, 2, TT, T])
        hpad = sb("hpad", "arena", 24, [P, KC, T + CONV_C - 1])
        tap = sb("tap_products", "arena", 42, [P, 4, T])
        cv = sb("cv", "arena", 34, [P, KC, T])
        gpad = sb("gpad", "arena", 24, [P, 2, T + 2])
        cf = sb("cf", "arena", 27, [P, 2, T])
        uf = sb("uf", "arena", 29, [P, 2, T])
        hid = sb("hid", "arena", 31, [P, 2, T])
        q2 = sb("q2", "arena", 0, [P, 20, T])
        k2 = sb("k2", "arena", 20, [P, 13, T])
        v2 = sb("v2", "arena", 33, [P, TT, 1664])
        gt = sb("gt", "mh", 0, [P, 16, T])
        sc = sb("sc", "raw", 24, [P, 2, 9 * P])
        pt2 = sb("pt2", "raw", 33, [P, 3, 3 * P])
        hf = sb("hf", "arena", 37, [P, KC, T])
        htok_hi = sb("h_by_token_hi", "arena", 0, [P, TT, D], F32R)
        htok_lo = sb("h_by_token_lo", "arena", 8, [P, TT, D], F32R)
        onehot = sb("onehot", "arena", 16, [P, 2, TT, 4 * CAP], F32R)
        silu = sb("silu", "arena", 20, [P, DE])
        hide = sb("hidden_e", "arena", 22, [P, DE])
        ht_hi = sb("hidden_turned_hi", "arena", 24, [P, DE // P, 3 * CAP], F32R)
        ht_lo = sb("hidden_turned_lo", "arena", 27, [P, DE // P, 3 * CAP], F32R)
        back = sb("slots_to_tokens", "arena", 30, [P, 2, T], F32R)
        xg_hi = sb("gathered_hi", "ah", 0, [P, 2, 2 * KC, 3 * CAP], F32R)
        xg_lo = sb("gathered_lo", "ah", 24, [P, 2, 2 * KC, 3 * CAP], F32R)
        ye_hi = sb("expert_out_hi", "yl", 4, [P, D], F32R)
        ye_lo = sb("expert_out_lo", "yl", 8, [P, D], F32R)
        dense_silu = sb("dense_silu", "arena", 0, [P, TT, DE])
        dense_hid = sb("dense_hidden", "arena", 4, [P, TT, DE])
        dense_turned = sb("dense_turned", "arena", 8, [P, DE // P, T])
        zeros = sb("zeros", "arena", 45, [P, T], F32R)
        rk = sb("router_konst", "konst", 0.5, [P, KC * 36 + P + CAP])
        rw = rk[:, 0:KC * 36].rearrange("p (k n) -> p k n", k=KC)
        until = rk[:, KC * 36:KC * 36 + P]
        slot_no = rk[:, KC * 36 + P:KC * 36 + P + CAP]
        place = sb("place", "konst", 2.5, [P, TT, NE])
        gates = sb("gates", "konst", 2.75, [P, TT, NE])
        chosen = sb("chosen", "konst", 3, [P, TT, NE])
        slot_gate = sb("slot_gate", "konst", 3.25, [P, 2])
        most = sb("most", "konst", 3.375, [P, 1])
        overflow = sb("overflow", "konst", 3.5, [P, 1], mybir.dt.int32)
        lg = sb("logits", "konst", 5, [P, TT, 36])
        rt = sb("router_tmp", "konst", 5.5, [P, TT, 60])
        ones = sb("ones", "tmp", 0, [P, P])
        t = [sb(f"t{n}", "tmp", 0.5 + n, [P, T]) for n in range(5)]
        diag = sb("diag", "tmp", 4.5, [P, TT, P])
        rstd_b = sb("rstd_b", "tmp", 5.5, [P, T])
        sm = sb("small", "tmp", 6.5, [P, 128])
        ms, rcol, mhalf = sm[:, 0:2], sm[:, 2:4], sm[:, 4:6]
        nmax, den, rec, esink = sm[:, 6:8], sm[:, 8:10], sm[:, 10:12], sm[:, 12:14]
        sp8, n4sp, p4sp, hbx, hba, hbc = (sm[:, 16 + 8 * n:24 + 8 * n] for n in range(6))
        nsink = sm[:, 64:80]
        lam_a, lam_e, lam_z, lam_q = (sm[:, 80 + 8 * n:88 + 8 * n] for n in range(4))

        mem_rstd = sb("mem_rstd", "memr", 0, [P, T])

        pw = [ctx.enter_context(nc.psum_tensor(f"pw{n}", [P, 512], F32)) for n in range(4)]
        acc = [ctx.enter_context(nc.psum_tensor(f"acc{n}", [P, 512], F32)) for n in range(4)]

        def acc_of(n):
            return acc[n // 2][:, (n % 2) * T:(n % 2) * T + T]

        def col(name, n=0, step=0, i=None):
            if i is None:
                return cols[:, C0[name] + n:C0[name] + n + 1]
            return cols[:, bass.ds(i * step + (C0[name] + n), 1)]

        raw_in = [S(f"raw_in{n}") for n in range(RAW)]
        w_hi, w_lo_v, w_lo_p = S("w_hi"), S("w_lo_vector"), S("w_lo_pool")
        slab_done, mm_done = S("slab_done"), S("products_done")
        empty_v, empty_a = S("bank_emptied_vector"), S("bank_emptied_scalar")
        acc_full, acc_out = S("sum_full"), S("sum_taken")
        sq_ready, stat_full, ms_ready = S("squares"), S("sums_full"), S("mean_square")
        rstd_ready, diag_ready, bc_full = S("rstd_column"), S("diagonal"), S("spread_full")
        rstd_b_ready = S("rstd_spread")
        pair_hi, pair_lo = S("a_hi"), S("a_lo")
        block = ctx.enter_context(nc.Block())

        def wait_split(eng, s):
            if s.base % 2 == 0:
                eng.wait_ge(w_lo_v, s.of(lambda n: n // 2 + 1))
            else:
                eng.wait_ge(w_lo_p, s.of(lambda n: (n + 1) // 2))

        def wait_slab(eng, s):
            eng.wait_ge(slab_done, s.of(lambda n: n + 1))

        def wait_emptied(eng, u):
            eng.wait_ge(empty_v if USES[u] == "v" else empty_a, emptied(u))

        def wait_acc(eng, phase, n):
            n |= 1
            if n < KC - 1:
                eng.wait_ge(acc_full, (KC - 1) * ACCS[phase] + n + 1)
            else:
                wait_slab(eng, At(S0[phase] + dict(PHASES)[phase] - 1))

        def wait_new_x(eng, phase, c):
            eng.wait_ge(acc_out, KC * ACCS[phase] + c + 1)

        def gather_bank(j):
            return j if j < 4 else 3 - j % 2

        def taps_until(n):
            return POOL_CONV * CONV_C * max(n - 4, 0) // 27

        def both_of_pairs(tile):
            return tile.rearrange("p n (t s) -> p n t s", t=3)[:, :, 0:3:2, :]

        def gu_slab(p):
            return S0["moe"] + (24 * p - 8 if p else 0)

        def moe_schedule(prog, raised, last, period):
            period(0, None)
            period(1, None)
            with prog.loop(3, raised, last) as i:
                for p in range(2, 6):
                    period(p, i)
            period(14, None)
            period(15, None)

        def per_trip(p, i):
            return At(p, 4 if i is not None else 0, i)

        def glu_steps(J):
            trips = (J - 6) // 4
            return trips, 4 + 4 * trips

        @block.sync
        def _(sp):
            def load(s, d=None):
                b, d = s.base, d or s
                if b >= RAW:
                    wait_split(sp, s + -back_to_same(b))
                if b == SHORT1 + HALF:
                    sp.wait_ge(S("attn2_hi"), len(HEADS2))
                src = stream[d.base] if d.i is None else \
                    stream[bass.ds(d.i * d.step + d.base, 1), :, :].rearrange("a p n -> (a p) n")
                sp.dma_start(raw[:, slot_of(b), :], src).then_inc(raw_in[slot_of(b)], 16)

            sp.dma_start(x[:], x_in).then_inc(S("x_in"), 16)
            for s in range(2 * RAW):
                load(At(s))
            with sp.Fori(0, SHORT0 // RAW - 2) as i:
                for j in range(RAW):
                    load(At(2 * RAW + j, RAW, i))
            for s in range(SHORT0, SHORT0 + RAW):
                load(At(s))
            with sp.Fori(0, (SHORT1 - SHORT0) // RAW - 1) as i:
                for j in range(RAW):
                    load(At(SHORT0 + RAW + j, RAW, i))
            for s in range(SHORT1, S0["moe"]):
                load(At(s))

            def inputs_at(p):
                return [S0["moe"] + EXPERT * (2 * p + e) + k for e in range(2) for k in range(8)]

            def outputs_at(p):
                return [S0["moe"] + EXPERT * (2 * p + e) + 8 + k for e in range(2) for k in range(4)]

            for n, d in enumerate(inputs_at(0)):
                load(At(S0["moe"] + n), At(d))
            with sp.Fori(0, PAIRS_E - 1) as i:
                for n, d in enumerate(inputs_at(1) + outputs_at(0)):
                    load(At(S0["moe"] + 16 + n, 24, i), At(d, 24, i))
            for n, d in enumerate(outputs_at(PAIRS_E - 1)):
                load(At(NSLAB - 8 + n), At(d))

            sp.wait_ge(S("overflow_known"), 1)
            over = sp.value_load(overflow[0:1, 0:1], min_val=0, max_val=1)
            with sp.If(over > 0):
                for s in range(NSLAB - 2, NSLAB):
                    wait_split(sp, At(s))
                with sp.Fori(0, NE) as i:
                    sp.wait_ge(S("dense_down"), i + 1)
                    for j in range(EXPERT):
                        sp.dma_start(raw[:, j, :], stream[bass.ds(i * EXPERT + (S0["moe"] + j), 1), :, :]
                                     .rearrange("a p n -> (a p) n")).then_inc(S("dense_in"), 16)
            sp.wait_ge(S("x_final"), KC)
            sp.dma_start(out, x[:]).then_inc(S("out_done"), 16)
            sp.wait_ge(S("out_done"), 16)

        @block.scalar
        def _(act):
            A = Program(act, S("scalar_chain"))

            def split(s):
                if s.base >= NSLAB:
                    return
                act.wait_ge(raw_in[slot_of(s.base)], s.of(lambda n: 16 * fills_of(n)))
                if s.base >= SPLIT:
                    wait_slab(act, s + -SPLIT)
                A.done(act.activation(wh[:, s.base % SPLIT, :], raw[:, slot_of(s.base), :], ACT.Copy), w_hi)

            def squares(src, ready, gain=None, name=None):
                for c in range(KC):
                    ready(c)
                    A.done(act.activation(sq[:, c, :], src[:, c, :], ACT.Square), sq_ready)
                    if gain is not None:
                        A.done(act.activation(ah[:, c, :], src[:, c, :], ACT.Copy, scale=col(gain, c)), pair_hi)

            act.dma_start(cols[:], cols_in).then_inc(S("cols_in"), 16)
            act.dma_start(ident[:], konst_in[:, 0:P]).then_inc(S("const_in"), 16)
            act.dma_start(inv[:], konst_in[:, P:P + 4 * T].rearrange("p (g t) -> p g t", g=4)) \
                .then_inc(S("const_in"), 16)
            act.dma_start(mem[:], mem_in).then_inc(S("mem_in"), 16)
            act.wait_ge(S("cols_in"), 16)
            act.wait_ge(S("x_in"), 16)
            squares(x, lambda c: None, "ab_norm")
            for s in range(AHEAD):
                split(At(s))
            act.wait_ge(S("mem_in"), 16)
            act.wait_ge(stat_full, 1)
            squares(mem, lambda c: None)
            A.done(act.activation(lam_a, cols[:, C0["a_lambda"]:C0["a_lambda"] + 8], ACT.Abs), S("decay_abs"))
            A.fence()
            A.done(act.activation(lam_e, lam_a, ACT.Exp, scale=-1.0), S("decay_exp"))

            def mem_pair(l):
                for c in range(KC):
                    act.wait_ge(S("mem_normed_again" if l else "mem_normed"), c + 1)
                    A.done(act.activation(mh[:, c, :], mem[:, c, :], ACT.Copy, scale=col(f"mem_norm{l}", c)),
                           S("m_hi"))

            for n in range(20):
                split(At(S0["abin"] + n + AHEAD))
                if n == 9:
                    mem_pair(0)
                if 12 <= n:
                    wait_emptied(act, USE0["abin"] + 4 + n - 12)
                    A.done(act.activation(z[:, n - 12, :], z[:, n - 12, :], ACT.Gelu_apprx_tanh), S("gate_gelu"))
            for n in range(8):
                split(At(S0["k0"] + n + AHEAD))
                act.wait_ge(S("xr_ready"), n + 1)
                A.done(act.activation(yh[:, n, :], xr[:, n, :], ACT.Copy), S("xr_hi"))
                if n >= 4:
                    act.wait_ge(S("pooled"), n - 3)
                    A.done(act.activation(yh[:, 4 + n, :], z[:, 12 + n, :], ACT.Copy), S("pooled_hi"))
            act.wait_ge(S("decay"), 1)
            for n in range(4):
                split(At(gate_slab(n) + AHEAD))
                for h in (2 * n, 2 * n + 1):
                    u = USE0["gates"] + 3 * n + h % 2
                    act.wait_ge(S("gate_products"), h + 1)
                    if h >= 2:
                        act.wait_ge(S("root_in"), h - 1)
                    A.fence()
                    A.done(act.activation(t[h % 2][:], pw[u % 4][:, 0:T], ACT.Tanh, bias=hbx[:, h:h + 1], scale=0.5))
                    A.done(act.activation(t[2 + h % 2][:], pw[u % 4][:, T:2 * T], ACT.Tanh, bias=hba[:, h:h + 1],
                                          scale=0.5), empty_a)
                    A.fence()
                    A.done(act.activation(a_t[:, h, :], t[2 + h % 2][:], ACT.Exp, bias=n4sp[:, h:h + 1],
                                          scale=n4sp[:, h:h + 1]))
                    A.done(act.activation(z[:, 8 + h, :], t[2 + h % 2][:], ACT.Tanh, bias=p4sp[:, h:h + 1],
                                          scale=p4sp[:, h:h + 1]), S("gates_through"))
                split(At(v0_slab(2 * n) + AHEAD))
                wait_emptied(act, USE0["gates"] + 3 * n + 2)
                A.done(act.activation(yh[:, 8 + n, :], z[:, 16 + n, :], ACT.Copy), S("yb_hi"))
                split(At(v0_slab(2 * n + 1) + AHEAD))
            act.wait_ge(S("root_in"), 8)
            A.done(act.activation(z[:, 8:16, :], z[:, 8:16, :], ACT.Sqrt, scale=0.25), S("root"))
            for n in range(8):
                split(At(S0["about"] + n + AHEAD))
                act.wait_ge(S("ya_ready"), n + 1)
                A.done(act.activation(yh[:, n, :], xr[:, n, :], ACT.Copy), S("ya_hi"))
            act.dma_start(masks[:], masks_in).then_inc(S("masks_in"), 16)

            def row_splits(phase):
                for n in range(dict(PHASES)[phase]):
                    split(At(S0[phase] + n + AHEAD))

            def cross(l):
                name, n_u = f"x{l}", USE0[f"x{l}"]
                for h in range(XH + 1):
                    if h < XH:
                        for qt in range(TT):
                            r, b = 2 * h + qt, pw[(n_u + x_score(h) + qt) % 4]
                            act.wait_ge(S(name + "_max"), r + 1)
                            A.done(act.activation(prob[:, h % 2, qt, :], b[:, 0:T], ACT.Exp,
                                                  bias=nmax[:, qt:qt + 1], accum_out=den[:, qt:qt + 1]), empty_a)
                    if h >= 1:
                        for qt in range(TT):
                            k = x_turn(h - 1) + qt
                            act.wait_ge(mm_done, MM0[name] + k + 1)
                            A.done(act.activation(pt[:, (h - 1) % 2, :, qt * P:qt * P + P],
                                                  pw[(n_u + k) % 4][:, 0:T].rearrange("p (a q) -> p a q", a=TT),
                                                  ACT.Copy), empty_a)
                        k = x_turn(h - 1) + 2
                        act.wait_ge(mm_done, MM0[name] + k + 1)
                        A.done(act.activation(yh[:, 2 * h - 2:2 * h, :],
                                              pw[(n_u + k) % 4][:, :].rearrange("p (a q) -> p a q", a=2),
                                              ACT.Copy), S(name + "_hi"))

            def glu(name, J):
                base = S0[name]

                def step(j, i=None):
                    def slab(kind):
                        return At(glu_slab(base, J, kind, j), 12 if i is not None else 0, i)
                    jj = At(j, 4 if i is not None else 0, i)
                    split(slab("g") + AHEAD)
                    split(slab("u") + AHEAD)
                    act.wait_ge(S(name + "_conv"), (jj + 1).of(lambda n: n))
                    A.done(act.activation(cf[:, j % 2, :], cf[:, j % 2, :], ACT.Gelu_apprx_tanh), S(name + "_act"))
                    if j >= 2:
                        split(At(slab("u").base + 1 + AHEAD, 12 if i is not None else 0, i))
                    act.wait_ge(S(name + "_hidden"), (jj + 1).of(lambda n: n))
                    A.done(act.activation(yh[:, j % 4, :], hid[:, j % 2, :], ACT.Copy), S(name + "_hid_hi"))

                trips, rest = glu_steps(J)
                for j in range(4):
                    step(j)
                raised = {w_hi: 12, S(name + "_hid_hi"): 4, S(name + "_act"): 4}
                with A.loop(trips, raised, S(name + "_hid_hi")) as i:
                    for j in range(4, 8):
                        step(j, i)
                for j in range(rest, J):
                    step(j)
                for n in range(2):
                    split(At(base + 3 * J - 2 + n + AHEAD))

            for n in range(8, 12):
                split(At(S0["about"] + n + AHEAD))
            squares(x, lambda c: wait_new_x(act, "about", c), "xa_norm0")
            row_splits("q0")
            cross(0)
            row_splits("wo0")
            squares(x, lambda c: wait_new_x(act, "wo0", c), "f_norm0")
            act.dma_start(mem[:], mem_in).then_inc(S("mem_again"), 16)
            glu("f0", FJ)
            squares(x, lambda c: wait_new_x(act, "f0", c), "c_norm")
            def glu_tanh(c):
                wait_emptied(act, USE0["pw1"] + 2 * c + 1)
                tb = t[2 * (c % 2) + 1][:]
                A.done(act.activation(tb, tb, ACT.Tanh, bias=hbc[:, c:c + 1], scale=0.5), S("glu_tanh"))

            done_taps = 0
            for n in range(32):
                split(At(S0["pw1"] + n + AHEAD))
                if n % 2 == 0 and 2 <= n <= 16:
                    glu_tanh(n // 2 - 1)
                if n == 10:
                    mem_pair(1)
                if n == 5:
                    act.wait_ge(S("glu_out"), POOL_CONV)
                upto = taps_until(n)
                for m in range(done_taps, upto):
                    c, k = m % POOL_CONV, m // POOL_CONV
                    w, src = col("c_dw_w", c * CONV_C + k), hpad[:, c, k:k + T]
                    if m - 4 >= POOL_CONV:
                        act.wait_ge(S("tap_added"), m - 4 - POOL_CONV + 1)
                    if k == 0:
                        A.done(act.activation(cv[:, c, :], src, ACT.Identity, scale=w, bias=col("c_dw_b", c)),
                               S("tap_product"))
                    else:
                        A.done(act.activation(tap[:, m % 4, :], src, ACT.Copy, scale=w), S("tap_product"))
                done_taps = upto
            squares(cv, lambda c: act.wait_ge(S("ln_centred"), c + 1))
            for c in range(KC):
                act.wait_ge(S("ln_scaled"), c + 1)
                A.done(act.activation(cv[:, c, :], cv[:, c, :], ACT.Silu, bias=col("c_ln_b", c),
                                      scale=col("c_ln_g", c)), S("ln_silu"))
                A.fence()
                A.done(act.activation(yh[:, c, :], cv[:, c, :], ACT.Copy), S("ln_hi"))
            row_splits("pw2")
            squares(x, lambda c: wait_new_x(act, "pw2", c), "xa_norm1")
            row_splits("q1")
            cross(1)
            row_splits("wo1")
            squares(x, lambda c: wait_new_x(act, "wo1", c), "f_norm1")
            glu("f1", FJ)
            squares(x, lambda c: wait_new_x(act, "f1", c))
            squares(x, lambda c: act.wait_ge(S("x_normed"), c + 1), "g_mix")
            for n in range(46):
                split(At(S0["win"] + n + AHEAD))
            for m in range(len(HEADS2) + 1):
                for phase, n in fill2(m)[:1]:
                    split(At(S0[phase] + n + AHEAD))
                if m >= 1:
                    kind, h = HEADS2[m - 1]
                    for g in range(groups(kind)):
                        key = ("turn", m - 1, g)
                        act.wait_ge(mm_done, MM0["attn2"] + A2MM[key])
                        A.done(act.activation(pt2[:, g, :], pw[(USE0["attn2"] + A2[key]) % 4][:, 0:3 * P], ACT.Copy),
                               empty_a)
                if m < len(HEADS2):
                    kind, h = HEADS2[m]
                    for qt in range(TT):
                        at, n = (0, P) if qt == 0 else (3 * P, 2 * P)
                        act.wait_ge(S("attn2_max"), 2 * m + qt + 1)
                        s_ap = sc[:, m % 2, at:at + n * groups(kind)]
                        A.fence()
                        if kind == "s":
                            A.done(act.activation(esink[:, qt:qt + 1], col("sinks", h), ACT.Exp,
                                                  bias=nmax[:, qt:qt + 1]))
                        A.done(act.activation(s_ap, s_ap, ACT.Exp, bias=nmax[:, qt:qt + 1],
                                              accum_out=den[:, qt:qt + 1]), S("attn2_exp"))
                for phase, n in fill2(m)[1:]:
                    split(At(S0[phase] + n + AHEAD))
                if 1 <= m <= 8:
                    for _, n in fill2(m - 1):
                        wait_emptied(act, USE0["attn2"] + A2["fill", n])
                        A.done(act.activation(gt[:, n - 46, :], gt[:, n - 46, :], ACT.Tanh, scale=0.5),
                               S("mix_gates"))
                if m >= 1:
                    kind, h = HEADS2[m - 1]
                    key = ("mix", m - 1)
                    c, half = mixed_at(kind, h)
                    act.wait_ge(mm_done, MM0["attn2"] + A2MM[key])
                    A.done(act.activation(yh[half:half + 64, c, :],
                                          pw[(USE0["attn2"] + A2[key]) % 4][half:half + 64, 0:T], ACT.Copy),
                           S("attn2_hi"))
            act.dma_start(rk[:], router_in).then_inc(S("router_in"), 16)
            split(At(S0["brs"] + 7 + AHEAD))
            for c in range(KC):
                act.wait_ge(S("mixed"), c + 1)
                A.done(act.activation(yh[:, c, :], gt[:, c, :], ACT.Copy, scale=0.5), S("mixed_hi"))
            row_splits("wout")
            squares(x, lambda c: wait_new_x(act, "wout", c))
            act.wait_ge(rstd_ready, NORMS["moe"] + 1)
            for j in range(4):
                act.wait_ge(S("h_turned"), j + 1)
                A.done(act.activation(htok_hi[:, j // 2, 512 * (j % 2):512 * (j % 2) + 512], pw[j][:, :], ACT.Copy,
                                      scale=rcol[:, j // 2:j // 2 + 1]), S("h_turned_hi"))

            def router_exps():
                for q in range(TT):
                    act.wait_ge(S("group_max"), q + 1)
                    A.done(act.activation(rt[:, q, 4:8], lg[:, q, 0:4], ACT.Exp, bias=rt[:, q, 0:1],
                                          accum_out=rt[:, q, 1:2]), S("group_exp"))
                for q in range(TT):
                    act.wait_ge(S("expert_gap"), q + 1)
                    A.done(act.activation(rt[:, q, 2:3], rt[:, q, 3:4], ACT.Exp), S("expert_exp"))

            router_exps()
            def gather_hi(j):
                act.wait_ge(S("gathered"), (j + 1).of(lambda n: n))
                c = 4 * (j.base % 4)
                A.done(act.activation(both_of_pairs(xg_hi[:, j.base // 4 % 2, c:c + 4, :]),
                                      pw[gather_bank(j.base)][:, :].rearrange("p (n e s) -> p n e s", n=4, e=2),
                                      ACT.Copy), S("gathered_hi"))

            def y_hi(p, i, h):
                if h == 0:
                    wait_slab(act, At(gu_slab(p + 1) + 23, 96 if i is not None else 0, i) if p + 1 < PAIRS_E
                              else At(NSLAB - 1))
                A.done(act.activation(ye_hi[:, 512 * h:512 * h + 512], pw[2 + h][:, :], ACT.Copy), S("expert_out_hi"))

            def turned_hi(p):
                act.wait_ge(S("hidden_turned"), (p + 1).of(lambda n: n))
                A.done(act.activation(both_of_pairs(ht_hi[:]), pw[2][:, :].rearrange("p (n e s) -> p n e s", n=4, e=2),
                                      ACT.Copy), S("hidden_turned_hi"))

            def back_out(p):
                act.wait_ge(S("slots_turned"), (p + 1).of(lambda n: n))
                A.done(act.activation(back[:, p.base % 2, :], pw[3][:, 0:T], ACT.Copy), S("slots_turned_out"))

            def period(p, i):
                pp = per_trip(p, i)
                for n in range(24 if p else 16):
                    s = At(gu_slab(p) + n, 96 if i is not None else 0, i)
                    split(s + AHEAD)
                    if p >= 2 and n < 2:
                        y_hi(p - 2, i, n)
                    if p >= 1 and n == 4:
                        turned_hi(pp + -1)
                    if p < 14 and n in (8, 10):
                        gather_hi(At(4 + 2 * p + (n == 10), 8 if i is not None else 0, i))
                    if n == 12:
                        back_out(pp)
                    if n == 15:
                        wait_slab(act, s)
                        if p:
                            act.wait_ge(S("hidden_done"), pp.of(lambda n: n))
                        A.done(act.activation(silu[:], pw[0][:, :], ACT.Silu), S("silu"))

            for j in range(4):
                gather_hi(At(j))
            moe_schedule(A, {w_hi: 96, S("expert_out_hi"): 8, S("hidden_turned_hi"): 4, S("gathered_hi"): 8,
                             S("slots_turned_out"): 4, S("silu"): 4}, w_hi, period)
            last = PAIRS_E - 1
            split(At(NSLAB - 8 + AHEAD))
            y_hi(last - 1, None, 0)
            y_hi(last - 1, None, 1)
            turned_hi(At(last))
            for n in range(1, 8):
                split(At(NSLAB - 8 + n + AHEAD))
            y_hi(last, None, 0)
            y_hi(last, None, 1)
            act.wait_ge(S("overflow_known"), 1)
            over = act.value_load(overflow[0:1, 0:1], min_val=0, max_val=1)
            with act.If(over > 0):
                with act.Fori(0, NE) as i:
                    act.wait_ge(S("dense_products"), i + 1)
                    for q in range(TT):
                        act.activation(dense_silu[:, q, :], pw[2 * q][:, :], ACT.Silu, scale=rcol[:, q:q + 1]) \
                            .then_inc(S("dense_silu"), 1)
                    act.wait_ge(S("dense_turns"), i + 1)
                    for n in range(2):
                        act.activation(dense_turned[:, 2 * n:2 * n + 2, :],
                                       pw[n][:, :].rearrange("p (c t) -> p c t", c=2), ACT.Copy) \
                            .then_inc(S("dense_turned"), 1)
            squares(x, lambda c: wait_new_x(act, "moe", c))

        @block.gpsimd
        def _(pool):
            G = Program(pool, S("pool_chain"))

            def split(s):
                if s.base >= NSLAB or s.base % 2 == 0:
                    return
                pool.wait_ge(w_hi, s.of(lambda n: n + 1))
                G.done(pool.tensor_tensor(wl[:, s.base % SPLIT, :], raw[:, slot_of(s.base), :],
                                          wh[:, s.base % SPLIT, :].bitcast(F32), ALU.subtract), w_lo_p)

            def splits(s, n):
                for k in range(n):
                    split(At(s + k + AHEAD))

            def rstd(name, mean=False):
                pool.wait_ge(ms_ready, NORMS[name] + 1)
                G.fence()
                if mean:
                    G.done(pool.tensor_copy(rcol, ms), rstd_ready)
                else:
                    G.done(pool.tensor_tensor(rcol, ms, mhalf, ALU.pow), rstd_ready)

            pool.wait_ge(S("constants"), 1)
            rstd("ab")
            for s in range(AHEAD):
                split(At(s))
            for n in range(20):
                split(At(S0["abin"] + n + AHEAD))
                if n == 4:
                    rstd("mem")
                if n in (7, 10, 13, 16):
                    g = (n - 7) // 3
                    wait_emptied(pool, USE0["abin"] + g)
                    src = z[:, 16 + g, :]
                    for j in range(g + 1):
                        d, dst = 1 << j, t[2 + j % 2][:]
                        G.fence()
                        G.done(pool.tensor_copy(dst[:, 0:d], src[:, 0:d]))
                        G.done(pool.tensor_tensor(dst[:, d:T], src[:, d:T], src[:, 0:T - d], ALU.add))
                        src = dst
                    G.fence()
                    G.done(pool.tensor_tensor(src, src, inv[:, g, :], ALU.mult))
                    G.fence()
                    G.done(pool.tensor_tensor(z[:, 16 + g, :], src, z[:, 16 + g, :], ALU.subtract), S("pooled"))
            splits(S0["k0"], 8)
            for n in range(4):
                split(At(gate_slab(n) + AHEAD))
                pool.wait_ge(S("pooled_hi"), n + 1)
                G.done(pool.tensor_tensor(yl[:, 8 + n, :], z[:, 16 + n, :], yh[:, 8 + n, :].bitcast(F32),
                                          ALU.subtract), S("pooled_lo"))
                split(At(v0_slab(2 * n) + AHEAD))
                split(At(v0_slab(2 * n + 1) + AHEAD))
            splits(S0["about"], 12)
            rstd("xa0")
            splits(S0["q0"], 8)
            splits(S0["wo0"], 8)
            rstd("f0")

            def glu(name, J):
                base = S0[name]

                def step(j, i=None):
                    st = 12 if i is not None else 0
                    g = At(glu_slab(base, J, "g", j), st, i)
                    jj = At(j, 4 if i is not None else 0, i)
                    split(g + AHEAD)
                    split(g + (1 + AHEAD))
                    if j >= 2:
                        split(g + (2 + AHEAD))
                    pool.wait_ge(S(name + "_hid_hi"), (jj + 1).of(lambda n: n))
                    G.done(pool.tensor_tensor(yl[:, j % 4, :], hid[:, j % 2, :], yh[:, j % 4, :].bitcast(F32),
                                              ALU.subtract), S(name + "_hid_lo"))

                trips, rest = glu_steps(J)
                for j in range(4):
                    step(j)
                with G.loop(trips, {w_lo_p: 6, S(name + "_hid_lo"): 4}, S(name + "_hid_lo")) as i:
                    for j in range(4, 8):
                        step(j, i)
                for j in range(rest, J):
                    step(j)
                splits(base + 3 * J - 2, 2)

            glu("f0", FJ)
            pool.wait_ge(S("mem_again"), 16)
            pool.wait_ge(rstd_b_ready, NORMS["mem"] + 1)
            pool.wait_ge(acc_out, KC * ACCS["f0"] + 1)

            def mem_again(c):
                G.done(pool.tensor_tensor(mem[:, c, :], mem[:, c, :], mem_rstd[:], ALU.mult), S("mem_normed_again"))

            rstd("c")
            done_taps = 0
            for n in range(32):
                split(At(S0["pw1"] + n + AHEAD))
                if n < 4:
                    mem_again(2 * n)
                    mem_again(2 * n + 1)
                upto = taps_until(n)
                for m in range(max(done_taps, POOL_CONV), upto):
                    c = m % POOL_CONV
                    pool.wait_ge(S("tap_product"), m + 1)
                    G.fence(POOL_CONV - 1)
                    G.done(pool.tensor_tensor(cv[:, c, :], cv[:, c, :], tap[:, m % 4, :], ALU.add), S("tap_added"))
                done_taps = upto
            rstd("lnmean", mean=True)
            rstd("ln")
            splits(S0["pw2"], 8)
            rstd("xa1")
            splits(S0["q1"], 16)
            rstd("f1")
            glu("f1", FJ)
            rstd("final")
            rstd("mix")
            splits(S0["win"], 62 + 20)
            wait_slab(pool, At(S0["wout"] + 7))
            for tile in (xg_hi, xg_lo):
                G.done(pool.memset(tile[:].rearrange("p a n s -> p (a n) s")[:, :, CAP:2 * CAP].bitcast(F32), 0.0),
                       S("pads"))
            for tile in (ht_hi, ht_lo):
                G.done(pool.memset(tile[:, :, CAP:2 * CAP].bitcast(F32), 0.0), S("pads"))
            rstd("moe")
            moe_schedule(G, {w_lo_p: 48}, w_lo_p, lambda p, i: [
                split(At(gu_slab(p) + n + AHEAD, 96 if i is not None else 0, i)) for n in range(24 if p else 16)])
            splits(NSLAB - 8, 8)
            rstd("out")

        @block.vector
        def _(dve):
            V = Program(dve, S("vector_chain"))

            def split(s):
                if s.base >= NSLAB or s.base % 2 == 1:
                    return
                dve.wait_ge(w_hi, s.of(lambda n: n + 1))
                V.done(dve.tensor_tensor(wl[:, s.base % SPLIT, :], raw[:, slot_of(s.base), :],
                                         wh[:, s.base % SPLIT, :].bitcast(F32), ALU.subtract), w_lo_v)

            def splits(s, n):
                for k in range(n):
                    split(At(s + k + AHEAD))

            def norm_mean(name, eps=EPS):
                dve.wait_ge(stat_full, NORMS[name] + 1)
                V.fence()
                V.done(dve.tensor_scalar(ms, acc[0][:, 0:2], 1.0 / D, eps, ALU.mult, ALU.add), ms_ready)

            def norm_spread(name, dst):
                dve.wait_ge(rstd_ready, NORMS[name] + 1)
                V.fence()
                for q in range(TT):
                    V.done(dve.tensor_scalar(diag[:, q, :], ident[:], rcol[:, q:q + 1], None, ALU.mult), diag_ready)
                dve.wait_ge(bc_full, spread_no(name))
                V.fence()
                V.done(dve.tensor_copy(dst, acc[0][:, T:2 * T]), rstd_b_ready)
                V.fence()

            def pair_lo_parts(pair, gain):
                for c in range(KC):
                    dve.wait_ge(pair_hi, KC * PAIRS[pair] + c + 1)
                    V.done(dve.scalar_tensor_tensor(al[:, c, :], x[:, c, :], col(gain, c),
                                                    ah[:, c, :].bitcast(F32), ALU.mult, ALU.subtract), pair_lo)

            def take_sums(phase, bias=None):
                for c in range(KC):
                    if phase != "moe":
                        wait_acc(dve, phase, c)
                    if c == 0:
                        V.fence()
                    if bias is None:
                        ins = dve.tensor_tensor(x[:, c, :], acc_of(c), x[:, c, :], ALU.add)
                    else:
                        ins = dve.scalar_tensor_tensor(x[:, c, :], acc_of(c), col(bias, c), x[:, c, :],
                                                       ALU.add, ALU.add)
                    V.done(ins, acc_out)

            def col_out(name, n, dst, scale=None, by=None, slab=None):
                u = USE0[name] + n
                wait_slab(dve, At(S0[name] + (n if slab is None else slab)))
                b = pw[u % 4][:, 0:T]
                if by is None:
                    ins = dve.tensor_copy(dst, b)
                elif scale is None:
                    ins = dve.tensor_tensor(dst, b, by, ALU.mult)
                else:
                    ins = dve.scalar_tensor_tensor(dst, b, scale, by, ALU.mult, ALU.mult)
                V.done(ins, empty_v)

            dve.memset(ones[:], 1.0).then_inc(S("ones"), 1)
            V.done(dve.memset(mhalf, -0.5), S("constants"))
            dve.wait_ge(S("cols_in"), 16)
            dve.wait_ge(S("const_in"), 32)
            dve.wait_ge(S("x_in"), 16)
            pair_lo_parts("abin", "ab_norm")
            for s in range(AHEAD):
                split(At(s))
            norm_mean("ab")
            dve.wait_ge(S("decay_exp"), 1)
            lam = cols[:, C0["a_lambda"]:C0["a_lambda"] + 8]
            V.done(dve.tensor_scalar(lam_z, lam_e, 2.0, None, ALU.add))
            V.fence()
            V.done(dve.reciprocal(lam_z, lam_z))
            V.fence()
            V.done(dve.tensor_tensor(lam_z, lam_z, lam_e, ALU.mult))
            V.fence()
            V.done(dve.tensor_tensor(lam_q, lam_z, lam_z, ALU.mult))
            V.done(dve.memset(sp8, 1.0 / 19))
            for k in range(8, -1, -1):
                V.fence()
                V.done(dve.tensor_tensor(sp8, sp8, lam_q, ALU.mult))
                V.fence()
                V.done(dve.tensor_scalar(sp8, sp8, 1.0 / (2 * k + 1), None, ALU.add))
            V.fence()
            V.done(dve.scalar_tensor_tensor(sp8, sp8, 2.0, lam_z, ALU.mult, ALU.mult))
            V.done(dve.tensor_scalar(lam_q, lam, -1.0, 0.0, ALU.mult, ALU.max))
            V.fence()
            V.done(dve.tensor_tensor(sp8, sp8, lam_q, ALU.add))
            V.fence()
            V.done(dve.tensor_scalar(n4sp, sp8, -4.0, None, ALU.mult))
            V.done(dve.tensor_scalar(p4sp, sp8, 4.0, None, ALU.mult))
            V.done(dve.tensor_scalar(hbx, cols[:, C0["a_gate_x_b"]:C0["a_gate_x_b"] + 8], 0.5, None, ALU.mult))
            V.done(dve.tensor_scalar(hba, cols[:, C0["a_gate_a_b"]:C0["a_gate_a_b"] + 8], 0.5, None, ALU.mult))
            V.done(dve.tensor_scalar(hbc, cols[:, C0["c_b_pw1"] + 8:C0["c_b_pw1"] + 16], 0.5, None, ALU.mult))
            V.done(dve.tensor_scalar(nsink, cols[:, C0["sinks"]:C0["sinks"] + 16], -1.0, None, ALU.mult), S("decay"))
            norm_spread("ab", rstd_b[:])

            def mem_lo(l, c):
                dve.wait_ge(S("m_hi"), KC * l + c + 1)
                V.done(dve.scalar_tensor_tensor(ml[:, c, :], mem[:, c, :], col(f"mem_norm{l}", c),
                                                mh[:, c, :].bitcast(F32), ALU.mult, ALU.subtract), S("m_lo"))

            for n in range(20):
                split(At(S0["abin"] + n + AHEAD))
                if n == 4:
                    norm_mean("mem")
                if n == 7:
                    norm_spread("mem", mem_rstd[:])
                    V.fence()
                    for c in range(KC):
                        V.done(dve.tensor_tensor(mem[:, c, :], mem[:, c, :], mem_rstd[:], ALU.mult), S("mem_normed"))
                if n >= 11 and n < 19:
                    mem_lo(0, n - 11)
                col_out("abin", n, z[:, (n - 4) % 20, :], by=rstd_b[:])
            def xr_tap(n, k, between):
                w, lag = col("a_conv_w", n * CONV_A + CONV_A - 1 - k), k
                V.fence(1 if between else 0)
                if k == 0:
                    V.done(dve.tensor_scalar(xr[:, n, :], z[:, 8 + n, :], w, col("a_conv_b", n), ALU.mult, ALU.add))
                else:
                    V.done(dve.scalar_tensor_tensor(xr[:, n, lag:T], z[:, 8 + n, 0:T - lag], w, xr[:, n, lag:T],
                                                    ALU.mult, ALU.add), S("xr_ready") if k == CONV_A - 1 else None)

            def xr_lo(n):
                dve.wait_ge(S("xr_hi"), n + 1)
                V.done(dve.tensor_tensor(yl[:, n, :], xr[:, n, :], yh[:, n, :].bitcast(F32), ALU.subtract),
                       S("xr_lo"))

            for n in range(8):
                s = At(S0["k0"] + n + AHEAD)
                xr_tap(n, 0, False)
                split(s)
                xr_tap(n, 1, s.base % 2 == 0)
                col_out("k0", n, k_t[:, n, :])
                xr_tap(n, 2, True)
                if n:
                    xr_lo(n - 1)
                xr_tap(n, 3, n > 0)
            xr_lo(7)

            def v0_out(half):
                wait_slab(dve, At(v0_slab(4 * half + 3)))
                for q in range(TT):
                    V.done(dve.tensor_copy(v_m[:, q, half * 512:half * 512 + 512], acc[2 * (1 - half) + q][:, :]),
                           S("v0_out"))

            for n in range(4):
                split(At(gate_slab(n) + AHEAD))
                if n == 3:
                    v0_out(0)
                for h in (2 * n, 2 * n + 1):
                    dve.wait_ge(S("gates_through"), h + 1)
                    V.fence()
                    V.done(dve.tensor_tensor(diag[:].rearrange("p a b -> p (a b)"), a_t[:, h, :], a_t[:, h, :],
                                             ALU.mult))
                    V.fence()
                    V.done(dve.scalar_tensor_tensor(z[:, 8 + h, :], diag[:].rearrange("p a b -> p (a b)"), 1.0,
                                                    z[:, 8 + h, :], ALU.add, ALU.mult))
                    V.done(dve.scalar_tensor_tensor(xr[:, h, :], t[h % 2][:], 1.0, xr[:, h, :], ALU.add, ALU.mult),
                           S("root_in"))
                u = USE0["gates"] + 3 * n + 2
                wait_slab(dve, At(gate_slab(n)))
                V.done(dve.tensor_scalar(z[:, 16 + n, :], pw[u % 4][:, 0:T], col("b_group_b", n), col("b_scale", n),
                                         ALU.add, ALU.mult), empty_v)
                dve.wait_ge(S("yb_hi"), n + 1)
                V.done(dve.tensor_tensor(yl[:, 8 + n, :], z[:, 16 + n, :], yh[:, 8 + n, :].bitcast(F32),
                                         ALU.subtract), S("yb_lo"))
                split(At(v0_slab(2 * n) + AHEAD))
                split(At(v0_slab(2 * n + 1) + AHEAD))
            v0_out(1)

            def values_out(name, half):
                wait_slab(dve, At(S0[name] + 4 * half + 3))
                for q in range(TT):
                    u = USE0[name] + 2 * half + q
                    V.done(dve.tensor_copy(v_m[:, q, half * 512:half * 512 + 512], pw[u % 4][:, :]), empty_v)

            for n in range(8):
                split(At(S0["about"] + n + AHEAD))
                dve.wait_ge(S("root"), 1)
                V.fence()
                V.done(dve.tensor_tensor(xr[:, n, :], xr[:, n, :], z[:, 8 + n, :], ALU.mult))
                V.fence()
                V.done(dve.tensor_tensor_scan(z[:, 8 + n, :], a_t[:, n, :], xr[:, n, :], 0.0, ALU.mult, ALU.add))
                V.fence()
                dve.wait_ge(S("gate_gelu"), n + 1)
                V.done(dve.tensor_tensor(xr[:, n, :], z[:, 8 + n, :], z[:, n, :], ALU.mult), S("ya_ready"))
                dve.wait_ge(S("ya_hi"), n + 1)
                V.done(dve.tensor_tensor(yl[:, n, :], xr[:, n, :], yh[:, n, :].bitcast(F32), ALU.subtract),
                       S("ya_lo"))
            splits(S0["about"] + 8, 4)
            take_sums("about")

            def normed_pair(name, pair, gain):
                pair_lo_parts(pair, gain)
                norm_mean(name)

            def queries(l):
                for n in range(8):
                    split(At(S0[f"q{l}"] + n + AHEAD))
                    if n == 2:
                        norm_spread(f"xa{l}", rstd_b[:])
                        for k in range(3):
                            col_out(f"q{l}", k, q_t[:, k, :], 1.0 / 16, rstd_b[:])
                    elif n > 2:
                        col_out(f"q{l}", n, q_t[:, n, :], 1.0 / 16, rstd_b[:])

            def cross(l):
                name, n_u = f"x{l}", USE0[f"x{l}"]
                for h in range(XH + 1):
                    if h < XH:
                        for qt in range(TT):
                            k = x_score(h) + qt
                            dve.wait_ge(mm_done, MM0[name] + k + 1)
                            V.fence()
                            V.done(dve.tensor_reduce(nmax[:, qt:qt + 1], pw[(n_u + k) % 4][:, 0:T], AX.X, ALU.max,
                                                     negate=True), S(name + "_max"))
                        for qt in range(TT):
                            wait_emptied(dve, n_u + x_score(h) + qt)
                            V.done(dve.reciprocal(rec[:, qt:qt + 1], den[:, qt:qt + 1]))
                            V.fence()
                            V.done(dve.tensor_scalar(prob[:, h % 2, qt, :], prob[:, h % 2, qt, :], rec[:, qt:qt + 1],
                                                     None, ALU.mult), S(name + "_prob"))
                    if h >= 1:
                        k = x_turn(h - 1) + 2
                        dve.wait_ge(S(name + "_hi"), h)
                        V.done(dve.tensor_tensor(yl[:, 2 * h - 2:2 * h, :],
                                                 pw[(n_u + k) % 4][:, :].rearrange("p (a q) -> p a q", a=2),
                                                 yh[:, 2 * h - 2:2 * h, :].bitcast(F32), ALU.subtract), empty_v)

            def glu(name, J):
                base, l = S0[name], name[-1]

                def step(j, i=None):
                    st, st4 = (12, 4) if i is not None else (0, 0)
                    g = At(glu_slab(base, J, "g", j), st, i)
                    jj = At(j, st4, i)
                    u = USE0[name] + 2 * j
                    if j == 1:
                        norm_spread(name, rstd_b[:])
                        gate(0, At(0), At(base), None)
                        up(0, At(0), At(base + 1), USE0[name] + 1)
                    split(g + AHEAD)
                    if j >= 1:
                        gate(j, jj, g, i)
                    split(g + (1 + AHEAD))
                    if j >= 1:
                        up(j, jj, g + 1, u + 1)
                    if j >= 2:
                        split(g + (2 + AHEAD))

                def gate(j, jj, g, i):
                    wait_slab(dve, g)
                    V.fence()
                    V.done(dve.tensor_tensor(gpad[:, j % 2, 2:T + 2], pw[(USE0[name] + 2 * j) % 4][:, 0:T],
                                             rstd_b[:], ALU.mult), empty_v)
                    for k in range(CONV_F):
                        w = col(f"f_dw_w{l}", j * CONV_F + CONV_F - 1 - k, 4 * CONV_F, i)
                        V.fence()
                        if k == 0:
                            V.done(dve.tensor_scalar(cf[:, j % 2, :], gpad[:, j % 2, 2:T + 2], w,
                                                     col(f"f_dw_b{l}", j, 4, i), ALU.mult, ALU.add))
                        else:
                            V.done(dve.scalar_tensor_tensor(cf[:, j % 2, :], gpad[:, j % 2, 2 - k:T + 2 - k], w,
                                                            cf[:, j % 2, :], ALU.mult, ALU.add),
                                   S(name + "_conv") if k == CONV_F - 1 else None)

                def up(j, jj, s, u):
                    wait_slab(dve, s)
                    if j >= 2:
                        dve.wait_ge(S(name + "_hid_lo"), (jj + -1).of(lambda n: n))
                    V.fence()
                    V.done(dve.tensor_tensor(uf[:, j % 2, :], pw[u % 4][:, 0:T], rstd_b[:], ALU.mult), empty_v)
                    V.fence()
                    dve.wait_ge(S(name + "_act"), (jj + 1).of(lambda n: n))
                    V.done(dve.tensor_tensor(hid[:, j % 2, :], cf[:, j % 2, :], uf[:, j % 2, :], ALU.mult),
                           S(name + "_hidden"))

                V.fence()
                V.done(dve.memset(gpad[:, :, 0:2], 0.0))
                trips, rest = glu_steps(J)
                for j in range(4):
                    step(j)
                raised = {w_lo_v: 6, S(name + "_hidden"): 4, empty_v: 8, S(name + "_conv"): 4, S("vector_chain"): 8}
                last = w_lo_v if glu_slab(base, J, "u", 7) % 2 == 0 else S(name + "_hidden")
                with V.loop(trips, raised, last) as i:
                    for j in range(4, 8):
                        step(j, i)
                for j in range(rest, J):
                    step(j)
                splits(base + 3 * J - 2, 2)

            normed_pair("xa0", "q0", "xa_norm0")
            queries(0)
            cross(0)
            splits(S0["wo0"], 8)
            take_sums("wo0")
            normed_pair("f0", "f0", "f_norm0")
            glu("f0", FJ)
            take_sums("f0")
            normed_pair("c", "pw1", "c_norm")
            V.fence()
            V.done(dve.memset(hpad[:, :, 0:CONV_C - 1], 0.0), S("conv_padding"))
            groups_c = [(2, 3), (4, 5), (6, 7)]
            taps = [(c, k, len(g)) for g in groups_c for k in range(CONV_C) for c in g]

            def conv_taps(lo, hi):
                for c, k, size in taps[lo:hi]:
                    w = col("c_dw_w", c * CONV_C + k)
                    src = hpad[:, c, k:k + T]
                    V.fence(size - 1)
                    if k == 0:
                        V.done(dve.tensor_scalar(cv[:, c, :], src, w, col("c_dw_b", c), ALU.mult, ALU.add))
                    else:
                        V.done(dve.scalar_tensor_tensor(cv[:, c, :], src, w, cv[:, c, :], ALU.mult, ALU.add),
                               S("conv_out") if k == CONV_C - 1 else None)

            done_taps = 0
            for n in range(32):
                s = S0["pw1"] + n
                split(At(s + AHEAD))
                if n == 2:
                    norm_spread("c", rstd_b[:])
                if 2 <= n < 18:
                    for k in ([0, 1, 2] if n == 2 else [n] if n < 16 else []):
                        c, ta, tb = k // 2, t[2 * (k // 2 % 2)][:], t[2 * (k // 2 % 2) + 1][:]
                        V.fence()
                        col_out("pw1", k, tb if k % 2 else ta, by=rstd_b[:])
                        if k % 2:
                            dve.wait_ge(S("glu_tanh"), c + 1)
                            V.done(dve.tensor_scalar(tb, tb, 0.5, 0.5, ALU.mult, ALU.add))
                            V.fence()
                            V.done(dve.scalar_tensor_tensor(hpad[:, c, CONV_C - 1:], ta, col("c_b_pw1", c), tb,
                                                            ALU.add, ALU.mult), S("glu_out"))
                if 11 <= n < 15:
                    mem_lo(1, 2 * (n - 11))
                    mem_lo(1, 2 * (n - 11) + 1)
                if 16 <= n < 24:
                    col_out("k1", n - 16, k_t[:, n - 16, :])
                if n in (27, 31):
                    values_out("v1", (n - 27) // 4)
                upto = min(len(taps) * max(n - 6, 0) // 25, 2 * CONV_C * max((min(n, 15) + 1) // 4 - 1, 0))
                conv_taps(done_taps, upto)
                done_taps = upto
            conv_taps(done_taps, len(taps))
            norm_mean("lnmean", 0.0)
            norm_spread("lnmean", t[0][:])
            V.fence()
            for c in range(KC):
                V.done(dve.tensor_tensor(cv[:, c, :], cv[:, c, :], t[0][:], ALU.subtract), S("ln_centred"))
            norm_mean("ln")
            norm_spread("ln", t[0][:])
            V.fence()
            for c in range(KC):
                V.done(dve.tensor_tensor(cv[:, c, :], cv[:, c, :], t[0][:], ALU.mult), S("ln_scaled"))
            for c in range(KC):
                dve.wait_ge(S("ln_hi"), c + 1)
                V.done(dve.tensor_tensor(yl[:, c, :], cv[:, c, :], yh[:, c, :].bitcast(F32), ALU.subtract),
                       S("ln_lo"))
            splits(S0["pw2"], 8)
            take_sums("pw2", "c_b_pw2")
            normed_pair("xa1", "q1", "xa_norm1")
            queries(1)
            cross(1)
            splits(S0["wo1"], 8)
            take_sums("wo1")
            normed_pair("f1", "f1", "f_norm1")
            glu("f1", FJ)
            take_sums("f1")
            norm_mean("final")
            norm_spread("final", rstd_b[:])
            V.fence()
            for c in range(KC):
                V.done(dve.scalar_tensor_tensor(x[:, c, :], x[:, c, :], col("final_norm", c), rstd_b[:],
                                                ALU.mult, ALU.mult), S("x_normed"))
            normed_pair("mix", "win", "g_mix")
            for n in range(46):
                split(At(S0["win"] + n + AHEAD))
                if n == 2:
                    norm_spread("mix", rstd_b[:])
                for k in ([0, 1, 2] if n == 2 else [n] if n > 2 else []):
                    if k < 12:
                        col_out("win", k, q2[:, k, :], 0.125, rstd_b[:])
                    elif k < 24:
                        col_out("win", k, k2[:, k - 12, :], by=rstd_b[:])
                    elif k < 32:
                        col_out("win", k, q2[:, k - 12, :], 0.125, rstd_b[:])
                    elif k < 44:
                        if k % 4 == 3:
                            b = (k - 32) // 4
                            wait_slab(dve, At(S0["win"] + k))
                            for q in range(TT):
                                u = USE0["win"] + 32 + 2 * b + q
                                V.done(dve.tensor_scalar(v2[:, q, 512 * b:512 * b + 512], pw[u % 4][:, :],
                                                         rcol[:, q:q + 1], None, ALU.mult), empty_v)
                    elif k == 44:
                        col_out("win", 38, k2[:, 12, :], by=rstd_b[:], slab=44)
                    elif k == 45:
                        wait_slab(dve, At(S0["win"] + 45))
                        for q in range(TT):
                            u = USE0["win"] + 39 + q
                            V.done(dve.tensor_scalar(v2[:, q, 1536:1664], pw[u % 4][:, 0:P], rcol[:, q:q + 1],
                                                     None, ALU.mult), empty_v)

            def branch_out(phase, first):
                for c in range(KC):
                    wait_acc(dve, phase, c)
                    V.done(dve.scalar_tensor_tensor(gt[:, first + c, :], gt[:, first + c, :], 1.0, acc_of(c),
                                                    ALU.add, ALU.mult), acc_out)

            dve.wait_ge(S("masks_in"), 16)
            def gates_out(slabs):
                for phase, n in slabs:
                    if phase == "win":
                        wait_slab(dve, At(S0["win"] + n))
                        u = USE0["attn2"] + A2["fill", n]
                        V.done(dve.tensor_tensor(gt[:, n - 46, :], pw[u % 4][:, 0:T], rstd_b[:], ALU.mult), empty_v)

            wait_split(dve, At(SHORT0 - 1))
            for m in range(len(HEADS2) + 1):
                for phase, n in fill2(m)[:1]:
                    split(At(S0[phase] + n + AHEAD))
                if m < len(HEADS2):
                    kind, h = HEADS2[m]
                    G_ = groups(kind)
                    for qt in range(TT):
                        at, nk = (0, P) if qt == 0 else (3 * P, 2 * P)
                        for g in range(G_):
                            key = ("score", m, qt, g)
                            slope = SLOPES_DIL[8 * g + h] if kind == "d" else SLOPES_SWA[h]
                            dve.wait_ge(mm_done, MM0["attn2"] + A2MM[key])
                            V.done(dve.scalar_tensor_tensor(
                                sc[:, m % 2, at + g * nk:at + g * nk + nk],
                                masks[:, g if kind == "d" else 3, (0 if qt == 0 else P):(P if qt == 0 else 3 * P)],
                                -slope, pw[(USE0["attn2"] + A2[key]) % 4][:, 0:nk], ALU.mult, ALU.add), empty_v)
                        V.fence()
                        mx = nmax[:, qt:qt + 1]
                        V.done(dve.tensor_reduce(mx, sc[:, m % 2, at:at + G_ * nk], AX.X, ALU.max, negate=True),
                               S("attn2_max") if kind == "d" else None)
                        if kind == "s":
                            V.fence()
                            V.done(dve.tensor_scalar(mx, mx, nsink[:, h:h + 1], None, ALU.min), S("attn2_max"))
                if m < len(HEADS2):
                    for qt in range(TT):
                        at, nk = (0, P) if qt == 0 else (3 * P, 2 * P)
                        dve.wait_ge(S("attn2_exp"), 2 * m + qt + 1)
                        r = rec[:, qt:qt + 1]
                        if kind == "s":
                            V.fence()
                            V.done(dve.tensor_tensor(den[:, qt:qt + 1], den[:, qt:qt + 1], esink[:, qt:qt + 1],
                                                     ALU.add))
                        V.fence()
                        V.done(dve.reciprocal(r, den[:, qt:qt + 1]))
                        V.fence()
                        s_ap = sc[:, m % 2, at:at + G_ * nk]
                        V.done(dve.tensor_scalar(s_ap, s_ap, r, None, ALU.mult), S("attn2_prob"))
                gates_out(fill2(m)[:1])
                for phase, n in fill2(m)[1:]:
                    split(At(S0[phase] + n + AHEAD))
                if m >= 1:
                    kind, h = HEADS2[m - 1]
                    u = USE0["attn2"] + A2["mix", m - 1]
                    c, half = mixed_at(kind, h)
                    dve.wait_ge(S("attn2_hi"), m)
                    V.done(dve.tensor_tensor(yl[half:half + 64, c, :], pw[u % 4][half:half + 64, 0:T],
                                             yh[half:half + 64, c, :].bitcast(F32), ALU.subtract), empty_v)
                gates_out(fill2(m)[1:])
                if m == 11:
                    dve.wait_ge(S("mix_gates"), 16)
                    branch_out("brd", 0)
            split(At(S0["brs"] + 7 + AHEAD))
            branch_out("brs", 8)
            V.fence()
            for c in range(KC):
                V.done(dve.tensor_tensor(gt[:, c, :], gt[:, c, :], gt[:, 8 + c, :], ALU.add), S("mixed"))
            for c in range(KC):
                dve.wait_ge(S("mixed_hi"), c + 1)
                V.done(dve.scalar_tensor_tensor(yl[:, c, :], gt[:, c, :], 0.5, yh[:, c, :].bitcast(F32),
                                                ALU.mult, ALU.subtract), S("mixed_lo"))
            splits(S0["wout"], 8)
            take_sums("wout")
            V.fence()
            for c in range(KC):
                V.done(dve.tensor_scalar(hf[:, c, :], x[:, c, :], col("g_ffn", c), None, ALU.mult), S("h_ready"))
            norm_mean("moe")
            def each(op, sem=None):
                for q in range(TT):
                    V.fence(1)
                    V.done(op(q), sem)

            def first_of(dst, values, top, count):
                each(lambda q: dve.tensor_scalar(dst(q), values(q), top(q), None, ALU.is_equal))
                each(lambda q: dve.tensor_tensor_scan(count(q), ones[:, 0:count(q).free_size()], dst(q), 0.0,
                                                      ALU.mult, ALU.add))
                each(lambda q: dve.tensor_scalar(count(q), count(q), 1.0, None, ALU.is_equal))
                each(lambda q: dve.tensor_tensor(dst(q), dst(q), count(q), ALU.mult))

            def tmp(a, b):
                return lambda q: rt[:, q, a:b]

            gmx, gsum, e2, gap, gmask = tmp(0, 1), tmp(1, 2), tmp(2, 3), tmp(3, 4), tmp(8, 12)
            m1, m2, w1, gw, sel = tmp(12, 13), tmp(13, 14), tmp(14, 15), tmp(15, 16), tmp(16, 24)
            f1, f2, sel2, w2, top, count = tmp(24, 32), tmp(32, 40), tmp(40, 48), tmp(48, 49), tmp(49, 50), tmp(50, 58)

            def h_by_token_lo(j):
                dve.wait_ge(S("h_turned_hi"), j + 1)
                q, w = j // 2, slice(512 * (j % 2), 512 * (j % 2) + 512)
                V.done(dve.scalar_tensor_tensor(htok_lo[:, q, w], pw[j][:, :], rcol[:, q:q + 1],
                                                htok_hi[:, q, w].bitcast(F32), ALU.mult, ALU.subtract),
                       S("h_turned_lo"))

            dve.wait_ge(S("router_full"), 1)
            dve.wait_ge(rstd_ready, NORMS["moe"] + 1)
            for q in range(TT):
                V.done(dve.scalar_tensor_tensor(lg[:, q, :], acc[1][:, 64 * q:64 * q + 36], rcol[:, q:q + 1],
                                                cols[:, C0["r_bias"]:C0["r_bias"] + 36], ALU.mult, ALU.add))
            each(lambda q: dve.tensor_reduce(top(q), lg[:, q, 0:4], AX.X, ALU.max))
            each(lambda q: dve.tensor_scalar(gmx(q), top(q), -1.0, None, ALU.mult), S("group_max"))
            first_of(gmask, lambda q: lg[:, q, 0:4], top, lambda q: count(q)[:, 0:4])
            each(lambda q: dve.tensor_scalar(sel(q), lg[:, q, 4:12], gmask(q)[:, 0:1], None, ALU.mult))
            for g in range(1, 4):
                each(lambda q: dve.scalar_tensor_tensor(sel(q), lg[:, q, 4 + 8 * g:12 + 8 * g],
                                                        gmask(q)[:, g:g + 1], sel(q), ALU.mult, ALU.add))
            each(lambda q: dve.tensor_reduce(m1(q), sel(q), AX.X, ALU.max))
            first_of(f1, sel, m1, count)
            each(lambda q: dve.scalar_tensor_tensor(sel2(q), f1(q), NEG, sel(q), ALU.mult, ALU.add))
            each(lambda q: dve.tensor_reduce(m2(q), sel2(q), AX.X, ALU.max))
            each(lambda q: dve.tensor_tensor(gap(q), m2(q), m1(q), ALU.subtract), S("expert_gap"))
            first_of(f2, sel2, m2, count)
            dve.wait_ge(S("expert_exp"), TT)
            each(lambda q: dve.reciprocal(gw(q), gsum(q)))
            each(lambda q: dve.tensor_scalar(w1(q), e2(q), 1.0, None, ALU.add))
            each(lambda q: dve.reciprocal(w1(q), w1(q)))
            each(lambda q: dve.tensor_tensor(w1(q), w1(q), gw(q), ALU.mult))
            each(lambda q: dve.tensor_tensor(w2(q), w1(q), e2(q), ALU.mult))
            each(lambda q: dve.tensor_scalar(f1(q), f1(q), w1(q), None, ALU.mult))
            each(lambda q: dve.scalar_tensor_tensor(f1(q), f2(q), w2(q), f1(q), ALU.mult, ALU.add))
            for g in range(4):
                each(lambda q: dve.tensor_scalar(gates[:, q, 8 * g:8 * g + 8], f1(q), gmask(q)[:, g:g + 1], None,
                                                 ALU.mult))
            V.fence()
            V.done(dve.tensor_scalar(chosen[:], gates[:], 0.0, None, ALU.is_gt), S("chosen"))
            V.done(dve.memset(zeros[:].bitcast(F32), 0.0), S("zeros"))
            for j in range(2):
                h_by_token_lo(j)
            dve.wait_ge(S("places"), 1)
            V.done(dve.tensor_tensor(place[:].rearrange("p q e -> p (q e)"), acc[2][:, 0:TT * NE],
                                     chosen[:].rearrange("p q e -> p (q e)"), ALU.mult))
            V.done(dve.tensor_reduce(most[:], acc[2][:, TT * NE:(TT + 1) * NE], AX.X, ALU.max))
            V.fence()
            V.done(dve.tensor_scalar(overflow[:], most[:], float(CAP), None, ALU.is_gt), S("overflow_known"))

            def make_onehot(g):
                if g.base >= 2:
                    dve.wait_ge(S("slots_turned"), g.of(lambda n: 2 * n - 2))
                for q in range(TT):
                    at = place[:, q, 4 * g.base:4 * g.base + 4] if g.i is None else \
                        place[:, q, bass.ds(g.i * (4 * g.step) + 4 * g.base, 4)]
                    V.done(dve.tensor_tensor(onehot[:, g.base % 2, q, :].rearrange("p (e s) -> p e s", e=4),
                                             slot_no.unsqueeze(1).broadcast_to([P, 4, CAP]),
                                             at.unsqueeze(2).broadcast_to([P, 4, CAP]), ALU.is_equal), S("onehot"))

            make_onehot(At(0))
            for j in range(2, 4):
                h_by_token_lo(j)

            def gather_lo(j):
                dve.wait_ge(S("gathered_hi"), (j + 1).of(lambda n: n))
                c, par = 4 * (j.base % 4), j.base // 4 % 2
                V.done(dve.tensor_tensor(both_of_pairs(xg_lo[:, par, c:c + 4, :]),
                                         pw[gather_bank(j.base)][:, :].rearrange("p (n e s) -> p n e s", n=4, e=2),
                                         both_of_pairs(xg_hi[:, par, c:c + 4, :]).bitcast(F32), ALU.subtract),
                       S("gathered_lo"))

            def y_lo(pp, h):
                dve.wait_ge(S("expert_out_hi"), pp.of(lambda n: 2 * n + h + 1))
                w = slice(512 * h, 512 * h + 512)
                V.done(dve.tensor_tensor(ye_lo[:, w], pw[2 + h][:, :], ye_hi[:, w].bitcast(F32), ALU.subtract),
                       S("expert_out_lo"))

            def turned_lo(p):
                dve.wait_ge(S("hidden_turned_hi"), (p + 1).of(lambda n: n))
                V.done(dve.tensor_tensor(both_of_pairs(ht_lo[:]),
                                         pw[2][:, :].rearrange("p (n e s) -> p n e s", n=4, e=2),
                                         both_of_pairs(ht_hi[:]).bitcast(F32), ALU.subtract),
                       S("hidden_turned_lo"))

            def period(p, i):
                pp = per_trip(p, i)
                for n in range(24 if p else 16):
                    split(At(gu_slab(p) + n + AHEAD, 96 if i is not None else 0, i))
                    if p >= 2 and n < 2:
                        y_lo(pp + -2, n)
                    if p % 2 == 0 and p < 14 and n == 2:
                        make_onehot(At(p // 2 + 1, 2 if i is not None else 0, i))
                    if p >= 1 and n == 4:
                        turned_lo(pp + -1)
                    if p < 14 and n in (8, 10):
                        gather_lo(At(4 + 2 * p + (n == 10), 8 if i is not None else 0, i))
                    if n == 12:
                        dve.wait_ge(S("slots_turned_out"), (pp + 1).of(lambda n: n))
                        for e in range(2):
                            sl = slice(CAP * e, CAP * e + CAP)
                            V.done(dve.tensor_copy(slot_gate[sl, p % 2:p % 2 + 1], pw[3][sl, T + e:T + e + 1]),
                                   S("slot_gates"))
                    if n == 15:
                        dve.wait_ge(S("silu"), (pp + 1).of(lambda n: n))
                        if p:
                            dve.wait_ge(S("hidden_turned"), pp.of(lambda n: n))
                        dve.wait_ge(S("slot_gates"), (pp + 1).of(lambda n: 2 * n))
                        V.done(dve.scalar_tensor_tensor(hide[:], silu[:], slot_gate[:, p % 2:p % 2 + 1], pw[1][:, :], ALU.mult, ALU.mult),
                               S("hidden_done"))

            for j in range(4):
                gather_lo(At(j))
            moe_schedule(V, {w_lo_v: 48, S("expert_out_lo"): 8, S("hidden_turned_lo"): 4, S("gathered_lo"): 8,
                             S("hidden_done"): 4, S("slot_gates"): 8, S("onehot"): 4}, w_lo_v, period)
            last = PAIRS_E - 1
            y_lo(At(last - 1), 0)
            y_lo(At(last - 1), 1)
            turned_lo(At(last))
            splits(NSLAB - 8, 8)
            y_lo(At(last), 0)
            y_lo(At(last), 1)
            dve.wait_ge(S("scattered"), PAIRS_E)
            over = dve.value_load(overflow[0:1, 0:1], min_val=0, max_val=1)
            with dve.If(over > 0):
                for q in range(TT):
                    dve.tensor_scalar(gates[:, q, :], gates[:, q, :], rcol[:, q:q + 1], None, ALU.mult) \
                        .then_inc(S("dense_gates"), 1)
                dve.wait_ge(S("dense_gates"), TT)
                with dve.Fori(0, NE) as i:
                    for q in range(TT):
                        dve.wait_ge(S("dense_silu"), i * 2 + (q + 1))
                        dve.scalar_tensor_tensor(dense_hid[:, q, :], dense_silu[:, q, :], gates[:, q, bass.ds(i, 1)],
                                                 pw[2 * q + 1][:, :], ALU.mult, ALU.mult) \
                            .then_inc(S("dense_hidden"), 1)
                dve.wait_ge(S("dense_down"), NE + 2)
            V.fence()
            take_sums("moe")
            norm_mean("out")
            norm_spread("out", rstd_b[:])
            V.fence()
            for c in range(KC):
                V.done(dve.scalar_tensor_tensor(x[:, c, :], x[:, c, :], col("g_final", c), rstd_b[:],
                                                ALU.mult, ALU.mult), S("x_final"))

        @block.tensor
        def _(pe):
            def tile3(dst, s, n, hi, lo, start, stop, **kw):
                w = slice(n * P, n * P + P)
                pe.matmul(dst, wh[:, s.base % SPLIT, w], hi, start=start, stop=False, **kw)
                pe.matmul(dst, wl[:, s.base % SPLIT, w], hi, start=False, stop=False, **kw)
                return pe.matmul(dst, wh[:, s.base % SPLIT, w], lo, start=False, stop=stop, **kw)

            def norm_sums(name, src, ready):
                for c in range(KC):
                    ready(min(c + 1, KC - 1) if c == 0 else c)
                    for q in range(TT):
                        last = pe.matmul(acc[0][:, q:q + 1], src[:, c, q * P:q * P + P], ones[:, 0:1],
                                         start=(c == 0 and q == 0), stop=(c == KC - 1), skip_group_check=True)
                last.then_inc(stat_full, 1)

            def sq_sums(name):
                norm_sums(name, sq, lambda c: pe.wait_ge(sq_ready, KC * (NORMS[name] - (NORMS[name] > NORMS["lnmean"]))
                                                         + c + 1))

            def norm_spread(name):
                pe.wait_ge(diag_ready, TT * spread_no(name))
                for q in range(TT):
                    last = pe.matmul(acc[0][:, T + q * P:T + q * P + P], ones[:], diag[:, q, :], start=True, stop=True)
                last.then_inc(bc_full, 1)

            def drain(u):
                for who, sem in (("v", empty_v), ("a", empty_a)):
                    if u and emptied(u - 1, who):
                        pe.wait_ge(sem, emptied(u - 1, who))

            def col_slab(s, u, hi, lo, wait_n=None, first_ready=None):
                wait_split(pe, s)
                if wait_n is not None:
                    pe.wait_ge(empty_v, wait_n)
                for k in range(KC):
                    if first_ready is not None:
                        first_ready(k)
                    last = tile3(pw[u % 4][:, 0:T], s, k, hi[:, k, :], lo[:, k, :], k == 0, k == KC - 1)
                last.then_inc(slab_done, 1)

            def col_phase(name, n, hi, lo, ready=None, hook=None, straight=None, s_off=0, u_off=0):
                s0, u0 = S0[name] + s_off, USE0[name] + u_off
                straight = straight or (8 if n == 8 else 4)
                v0 = emptied(u0 - 1, "v") if u0 else 0
                drain(u0)
                for k in range(straight):
                    col_slab(At(s0 + k), u0 + k, hi, lo, v0 + k - 3 if k >= 4 else None, ready if k == 0 else None)
                    if hook:
                        hook(k)
                if n > straight:
                    with pe.Fori(0, (n - straight) // 4) as i:
                        for j in range(straight, straight + 4):
                            col_slab(At(s0 + j, 4, i), u0 + j, hi, lo, i * 4 + (v0 + j - 3))

            def row_slab(s, k, first, last):
                wait_split(pe, s)
                for n in range(KC):
                    ins = tile3(acc_of(n), s, n, yh[:, k, :], yl[:, k, :], first and n % 2 == 0, last,
                                skip_group_check=True)
                    if last and n < KC - 1:
                        ins.then_inc(acc_full, 1)
                ins.then_inc(slab_done, 1)

            def row_phase(name, order, ready, norm):
                if ACCS[name]:
                    pe.wait_ge(acc_out, KC * ACCS[name])
                if norm is not None:
                    pe.wait_ge(rstd_b_ready, NORMS[norm] + 1)
                for n, k in enumerate(order):
                    ready(k)
                    row_slab(At(S0[name] + n), k, n == 0, n == len(order) - 1)

            def pair_ready(pair):
                return lambda k: pe.wait_ge(pair_lo, KC * PAIRS[pair] + k + 1)

            def value_slab(s, kk, banks, hi, lo):
                wait_split(pe, s)
                slot = s.base % SPLIT
                for e in range(2):
                    k, w = 2 * kk + e, slice(e * 512, e * 512 + 512)
                    for q in range(TT):
                        dst, tk = banks[q][:, :], slice(q * P, q * P + P)
                        pe.matmul(dst, hi[:, k, tk], wh[:, slot, w], start=(k == 0), stop=False)
                        pe.matmul(dst, hi[:, k, tk], wl[:, slot, w], start=False, stop=False)
                        last = pe.matmul(dst, lo[:, k, tk], wh[:, slot, w], start=False, stop=(k == KC - 1))
                last.then_inc(slab_done, 1)

            def values(s0, u0, hi, lo, half):
                for q in range(TT):
                    wait_emptied(pe, u0 + 2 * half + q - 4)
                for kk in range(4):
                    value_slab(At(s0 + 4 * half + kk), kk, [pw[(u0 + 2 * half + q) % 4] for q in range(TT)], hi, lo)

            def cross(l):
                name, n_u = f"x{l}", USE0[f"x{l}"]
                wait_emptied(pe, n_u - 1)
                for h in range(XH + 1):
                    if h < XH:
                        for qt in range(TT):
                            u = n_u + x_score(h) + qt
                            wait_emptied(pe, u - 4)
                            for c in range(2):
                                last = pe.matmul(pw[u % 4][:, 0:T], q_t[:, 2 * h + c, qt * P:qt * P + P],
                                                 k_t[:, 2 * h + c, :], start=(c == 0), stop=(c == 1))
                            last.then_inc(mm_done, 1)
                    if h >= 1:
                        g = h - 1
                        for qt in range(TT):
                            u = n_u + x_turn(g) + qt
                            wait_emptied(pe, u - 4)
                            pe.wait_ge(S(name + "_prob"), 2 * g + qt + 1)
                            for kt in range(TT):
                                last = pe.transpose(pw[u % 4][:, kt * P:kt * P + P],
                                                    prob[:, g % 2, qt, kt * P:kt * P + P], ident[:])
                            last.then_inc(mm_done, 1)
                        u = n_u + x_turn(g) + 2
                        wait_emptied(pe, u - 4)
                        wait_emptied(pe, u - 1)
                        for dc in range(2):
                            for kt in range(TT):
                                last = pe.matmul(pw[u % 4][:, dc * T:dc * T + T],
                                                 v_m[:, kt, h_cols(g, dc)], pt[:, g % 2, kt, :],
                                                 start=(kt == 0), stop=(kt == TT - 1))
                        last.then_inc(mm_done, 1)

            def h_cols(h, dc):
                return slice(h * 256 + dc * P, h * 256 + dc * P + P)

            def glu(name, J, pair, hook=None):
                base, u0 = S0[name], USE0[name]
                v0 = emptied(u0 - 1, "v")
                drain(u0)

                def bank_free(j, jj, kind):
                    if j < 2:
                        return
                    pe.wait_ge(empty_v, (jj + -2).of(lambda n: v0 + 2 * n + (1 if kind == "g" else 2)))

                def row(j, jj, s, last=False):
                    pe.wait_ge(S(name + "_hid_lo"), (jj + 1).of(lambda n: n))
                    row_slab(s, j % 4, j == 0, last)

                def step(j, i=None):
                    st, st4 = (12, 4) if i is not None else (0, 0)
                    g, jj = At(glu_slab(base, J, "g", j), st, i), At(j, st4, i)
                    bank_free(j, jj, "g")
                    col_slab(g, u0 + 2 * j, ah, al, None, pair_ready(pair) if j == 0 else None)
                    bank_free(j, jj, "u")
                    col_slab(g + 1, u0 + 2 * j + 1, ah, al)
                    if j == 0 and hook:
                        hook()
                    if j >= 2:
                        if j == 2:
                            pe.wait_ge(acc_out, KC * ACCS[name])
                            pe.wait_ge(rstd_b_ready, NORMS[name] + 1)
                        row(j - 2, jj + -2, g + 2)

                trips, rest = glu_steps(J)
                for j in range(4):
                    step(j)
                with pe.Fori(0, trips) as i:
                    for j in range(4, 8):
                        step(j, i)
                for j in range(rest, J):
                    step(j)
                for j in (J - 2, J - 1):
                    row(j, At(j), At(glu_slab(base, J, "d", j)), last=(j == J - 1))

            pe.wait_ge(S("ones"), 1)
            sq_sums("ab")

            def abin_hook(k):
                if k == 1:
                    norm_spread("ab")
                if k == 2:
                    sq_sums_mem()
                if k == 6:
                    norm_spread("mem")

            def sq_sums_mem():
                pe.wait_ge(rstd_b_ready, NORMS["ab"] + 1)
                sq_sums("mem")

            col_phase("abin", 20, ah, al, pair_ready("abin"), abin_hook, straight=8)
            col_phase("k0", 8, mh, ml, lambda k: pe.wait_ge(S("m_lo"), k + 1))
            for n in range(4):
                s = At(gate_slab(n))
                wait_split(pe, s)
                for e in range(2):
                    h, u = 2 * n + e, USE0["gates"] + 3 * n + e
                    wait_emptied(pe, u - 4)
                    pe.wait_ge(S("xr_lo"), h + 1)
                    for g in range(2):
                        last = tile3(pw[u % 4][:, g * T:g * T + T], s, 2 * e + g, yh[:, h, :], yl[:, h, :],
                                     True, True)
                    last.then_inc(S("gate_products"), 1)
                u = USE0["gates"] + 3 * n + 2
                wait_emptied(pe, u - 4)
                pe.wait_ge(S("pooled_lo"), n + 1)
                tile3(pw[u % 4][:, 0:T], s, 4, yh[:, 8 + n, :], yl[:, 8 + n, :], True, True) \
                    .then_inc(slab_done, 1)
                if n == 0:
                    pe.wait_ge(rstd_b_ready, NORMS["mem"] + 1)
                half = n // 2
                for kk in (2 * (n % 2), 2 * (n % 2) + 1):
                    value_slab(At(v0_slab(2 * n + kk % 2)), kk, [acc[2 * (1 - half) + q] for q in range(TT)], mh, ml)
            pe.wait_ge(S("v0_out"), 2 * TT)
            row_phase("about", [8, 9, 10, 11, 0, 1, 2, 3, 4, 5, 6, 7],
                      lambda k: pe.wait_ge(S("yb_lo"), k - 7) if k >= 8 else pe.wait_ge(S("ya_lo"), k + 1), "mem")

            def spread_hook(name):
                return lambda k=1: norm_spread(name) if k == 1 else None

            def cross_layer(l):
                sq_sums(f"xa{l}")
                col_phase(f"q{l}", 8, ah, al, pair_ready(f"q{l}"), spread_hook(f"xa{l}"))
                cross(l)
                row_phase(f"wo{l}", range(8),
                          lambda k: wait_emptied(pe, USE0[f"x{l}"] + x_turn(k // 2) + 2), f"xa{l}")
                sq_sums(f"f{l}")
                glu(f"f{l}", FJ, f"f{l}", lambda: norm_spread(f"f{l}"))

            cross_layer(0)
            sq_sums("c")
            col_phase("pw1", 16, ah, al, pair_ready("pw1"), spread_hook("c"))
            col_phase("k1", 8, mh, ml, lambda k: pe.wait_ge(S("m_lo"), KC + k + 1))
            for half in range(2):
                values(S0["v1"], USE0["v1"], mh, ml, half)
            pe.wait_ge(rstd_b_ready, NORMS["c"] + 1)
            norm_sums("lnmean", cv, lambda c: pe.wait_ge(
                *((S("tap_added"), POOL_CONV * (CONV_C - 2) + c + 1) if c < POOL_CONV else
                  (S("conv_out"), c + 1 - POOL_CONV))))
            norm_spread("lnmean")
            sq_sums("ln")
            norm_spread("ln")
            row_phase("pw2", range(8), lambda k: pe.wait_ge(S("ln_lo"), k + 1), "ln")
            cross_layer(1)
            sq_sums("final")
            norm_spread("final")
            sq_sums("mix")
            col_phase("win", 32, ah, al, pair_ready("win"), spread_hook("mix"))
            for b in range(3):
                values(S0["win"] + 32 + 4 * b, USE0["win"] + 32 + 2 * b, ah, al, 0)
            s, u = At(S0["win"] + 44), USE0["win"] + 38
            wait_emptied(pe, u - 4)
            col_slab(s, u, ah, al)
            s, u = s + 1, u + 1
            wait_split(pe, s)
            for q in range(TT):
                wait_emptied(pe, u + q - 4)
                dst, slot, tk = pw[(u + q) % 4][:, 0:P], s.base % SPLIT, slice(q * P, q * P + P)
                for k in range(KC):
                    w = slice(k * P, k * P + P)
                    pe.matmul(dst, ah[:, k, tk], wh[:, slot, w], start=(k == 0), stop=False)
                    pe.matmul(dst, ah[:, k, tk], wl[:, slot, w], start=False, stop=False)
                    last = pe.matmul(dst, al[:, k, tk], wh[:, slot, w], start=False, stop=(k == KC - 1))
            last.then_inc(slab_done, 1)
            n_u = USE0["attn2"]

            def fill(slabs):
                for phase, n in slabs:
                    if phase == "win":
                        u = n_u + A2["fill", n]
                        wait_emptied(pe, u - 4)
                        col_slab(At(S0["win"] + n), u, ah, al)
                    else:
                        branch_slab(phase, n)

            def branch_slab(phase, n):
                if n == 0:
                    pe.wait_ge(acc_out, KC * ACCS[phase])
                    if phase == "brd":
                        pe.wait_ge(rstd_b_ready, NORMS["mix"] + 1)
                wait_emptied(pe, n_u + A2["mix", 2 * n + 1 + (8 if phase == "brs" else 0)])
                row_slab(At(S0[phase] + n), n + (4 if phase == "brs" else 0), n == 0,
                         n == dict(PHASES)[phase] - 1)

            for m in range(len(HEADS2) + 1):
                if m < len(HEADS2):
                    kind, h = HEADS2[m]
                    for qt in range(TT):
                        nk = P * (qt + 1)
                        for g in range(groups(kind)):
                            u = n_u + A2["score", m, qt, g]
                            qc, kc, half = heads_at(kind, h, g)
                            wait_emptied(pe, u - 4)
                            pe.matmul(pw[u % 4][:, 0:nk], q2[half:half + 64, qc, qt * P:qt * P + P],
                                      k2[half:half + 64, kc, 0:nk], start=True, stop=True).then_inc(mm_done, 1)
                if m >= 1:
                    kind, h = HEADS2[m - 1]
                    G_ = groups(kind)
                    pe.wait_ge(S("attn2_prob"), 2 * m)
                    for g in range(G_):
                        u = n_u + A2["turn", m - 1, g]
                        wait_emptied(pe, u - 4)
                        b, s_ap = pw[u % 4], sc[:, (m - 1) % 2, :]
                        pe.transpose(b[:, 0:P], s_ap[:, g * P:g * P + P], ident[:])
                        for kt in range(2):
                            a = 3 * P + g * 2 * P + kt * P
                            last = pe.transpose(b[:, (1 + kt) * P:(2 + kt) * P], s_ap[:, a:a + P], ident[:])
                        last.then_inc(mm_done, 1)
                fill(fill2(m)[:1])
                if m >= 1:
                    u = n_u + A2["mix", m - 1]
                    wait_emptied(pe, u - 4)
                    wait_emptied(pe, u - 1)
                    c, half = mixed_at(kind, h)
                    for g in range(G_):
                        va = 512 * g + 64 * h if kind == "d" else 1536 + 64 * (h // 8)
                        dst = pw[u % 4][half:half + 64, :]
                        pe.matmul(dst[:, 0:T], v2[:, 0, va:va + 64], pt2[:, g, 0:T], start=(g == 0), stop=False,
                                  skip_group_check=True)
                        last = pe.matmul(dst[:, P:T], v2[:, 1, va:va + 64], pt2[:, g, T:3 * P], start=False,
                                         stop=(g == G_ - 1), skip_group_check=True)
                    last.then_inc(mm_done, 1)
                fill(fill2(m)[1:])
            branch_slab("brs", 7)
            row_phase("wout", range(8), lambda k: pe.wait_ge(S("mixed_lo"), k + 1), None)
            sq_sums("moe")
            pe.wait_ge(S("router_in"), 16)
            pe.wait_ge(S("h_ready"), KC)
            for q in range(TT):
                for c in range(KC):
                    last = pe.matmul(acc[1][:, 64 * q:64 * q + 36], hf[:, c, q * P:q * P + P], rw[:, c, :],
                                     start=(c == 0), stop=(c == KC - 1))
            last.then_inc(S("router_full"), 1)
            drain(USE0["attn2"] + len(_a2))
            for j in range(4):
                for n in range(4):
                    last = pe.transpose(pw[j][:, n * P:n * P + P],
                                        hf[:, 4 * (j % 2) + n, (j // 2) * P:(j // 2) * P + P], ident[:])
                last.then_inc(S("h_turned"), 1)
            pe.wait_ge(S("chosen"), 1)
            pe.matmul(acc[2][:, 0:NE], until, chosen[:, 0, :], start=True, stop=True)
            pe.matmul(acc[2][:, NE:2 * NE], ones[:], chosen[:, 0, :], start=True, stop=False)
            pe.matmul(acc[2][:, NE:2 * NE], until, chosen[:, 1, :], start=False, stop=True)
            pe.matmul(acc[2][:, 2 * NE:3 * NE], ones[:], chosen[:, 0, :], start=True, stop=False)
            pe.matmul(acc[2][:, 2 * NE:3 * NE], ones[:], chosen[:, 1, :], start=False, stop=True) \
                .then_inc(S("places"), 1)

            def gather(j):
                for n in range(2):
                    c = 2 * (j.base % 4) + n
                    for q in range(TT):
                        for part in (htok_hi, htok_lo):
                            last = pe.matmul(pw[gather_bank(j.base)][:, n * T:n * T + T],
                                             part[:, q, c * P:c * P + P], onehot[:, j.base // 4 % 2, q, :],
                                             start=(q == 0 and part is htok_hi), stop=(q == 1 and part is htok_lo))
                last.then_inc(S("gathered"), 1)

            def rows3(dst, hi, lo, slot, w, first, last):
                pe.matmul(dst, hi, wh[:, slot, w], start=first, stop=False, skip_group_check=True)
                pe.matmul(dst, hi, wl[:, slot, w], start=False, stop=False, skip_group_check=True)
                return pe.matmul(dst, lo, wh[:, slot, w], start=False, stop=last, skip_group_check=True)

            def turn(p):
                pe.wait_ge(S("hidden_done"), (p + 1).of(lambda n: n))
                for c in range(DE // P):
                    last = pe.transpose(pw[2][:, c * P:c * P + P], hide[:, c * P:c * P + P], ident[:])
                last.then_inc(S("hidden_turned"), 1)

            def turn_slots(p):
                w = slice(2 * CAP * (p.base % 2), 2 * CAP * (p.base % 2) + 2 * CAP)
                hot = [onehot[:, p.base // 2 % 2, q, w].bitcast(F32) for q in range(TT)]
                for q in range(TT):
                    pe.transpose(pw[3][:, q * P:q * P + P], hot[q], ident[:])
                for q in range(TT):
                    g = gates[:, q, 2 * p.base:2 * p.base + 2] if p.i is None else \
                        gates[:, q, bass.ds(p.i * (2 * p.step) + 2 * p.base, 2)]
                    last = pe.matmul(pw[3][:, T:T + 2], hot[q], g, start=(q == 0), stop=(q == 1))
                last.then_inc(S("slots_turned"), 1)

            def zero_sums(first):
                for c in range(KC):
                    last = pe.matmul(acc_of(c), zeros[:, 0:P], zeros[:], start=(first and c % 2 == 0),
                                     stop=not first, skip_group_check=True)
                return last

            def scatter(p, i):
                pp = per_trip(p, i)
                pe.wait_ge(S("expert_out_lo"), pp.of(lambda n: 2 * n + 2))
                pe.wait_ge(S("slots_turned_out"), (pp + 1).of(lambda n: n))
                for c in range(KC):
                    for part in (ye_hi, ye_lo):
                        last = pe.matmul(acc_of(c), part[:, c * P:c * P + P], back[:, p % 2, :],
                                         start=False, stop=(p == PAIRS_E - 1 and part is ye_lo),
                                         skip_group_check=True)
                last.then_inc(S("scattered"), 1)

            def down(p, s0, i):
                for n in range(8):
                    s = At(s0 + n, 96 if i is not None else 0, i)
                    e, k = n // 4, n % 4
                    wait_split(pe, s)
                    sl = slice(CAP * e, CAP * e + P)
                    for h in range(2):
                        last = rows3(pw[2 + h][:, :], ht_hi[:, k, sl], ht_lo[:, k, sl], s.base % SPLIT,
                                     slice(512 * h, 512 * h + 512), n == 0, n == 7)
                    last.then_inc(slab_done, 1)

            def period(p, i):
                pp = per_trip(p, i)
                if p:
                    pe.wait_ge(S("hidden_done"), pp.of(lambda n: n))
                if p % 2 == 0:
                    pe.wait_ge(S("gathered_lo"), pp.of(lambda n: 2 * n + 4))
                par = p // 2 % 2
                for n in range(16):
                    s = At(gu_slab(p) + n, 96 if i is not None else 0, i)
                    e, k = n // 8, n % 8
                    wait_split(pe, s)
                    m, sl = 2 * k + p % 2, slice(CAP * e, CAP * e + P)
                    for h in range(2):
                        last = rows3(pw[h][:, :], xg_hi[:, par, m, sl], xg_lo[:, par, m, sl],
                                     s.base % SPLIT, slice(512 * h, 512 * h + 512), n == 0, n == 15)
                    last.then_inc(slab_done, 1)
                    if n == 3 and p >= 1:
                        if p >= 2:
                            pe.wait_ge(S("expert_out_lo"), pp.of(lambda n: 2 * n - 2))
                        else:
                            pe.wait_ge(S("gathered_lo"), 6)
                        turn(pp + -1)
                    if n == 5 and p == 1:
                        zero_sums(True)
                    if n == 5 and p >= 2:
                        scatter(p - 2, i)
                    if n == 7 and p < 14:
                        if p % 2 == 0:
                            pe.wait_ge(S("onehot"), pp.of(lambda n: n + 4))
                        if p:
                            pe.wait_ge(S("slot_gates"), pp.of(lambda n: 2 * n))
                        gather(At(4 + 2 * p, 8 if i is not None else 0, i))
                    if n == 9 and p < 14:
                        if p >= 1:
                            pe.wait_ge(S("hidden_turned_lo"), pp.of(lambda n: n))
                        gather(At(5 + 2 * p, 8 if i is not None else 0, i))
                    if n == 11:
                        if p < 14:
                            pe.wait_ge(S("gathered_lo"), pp.of(lambda n: 2 * n + 5))
                        turn_slots(pp)
                if p >= 1:
                    pe.wait_ge(S("hidden_turned_lo"), pp.of(lambda n: n))
                    if p < 14:
                        pe.wait_ge(S("gathered_lo"), pp.of(lambda n: 2 * n + 6))
                    pe.wait_ge(S("slots_turned_out"), (pp + 1).of(lambda n: n))
                    pe.wait_ge(S("slot_gates"), (pp + 1).of(lambda n: 2 * n))
                    down(p - 1, gu_slab(p) + 16, i)

            pe.wait_ge(S("h_turned_lo"), 4)
            pe.wait_ge(S("zeros"), 1)
            pe.wait_ge(S("pads"), 4)
            pe.wait_ge(S("onehot"), 2)
            for j in range(4):
                gather(At(j))
            period(0, None)
            period(1, None)
            with pe.Fori(0, 3) as i:
                for p in range(2, 6):
                    period(p, i)
            period(14, None)
            period(15, None)
            last_p = PAIRS_E - 1
            pe.wait_ge(S("expert_out_lo"), 2 * last_p)
            turn(At(last_p))
            scatter(last_p - 1, None)
            pe.wait_ge(S("hidden_turned_lo"), PAIRS_E)
            down(last_p, NSLAB - 8, None)
            scatter(last_p, None)
            over = pe.value_load(overflow[0:1, 0:1], min_val=0, max_val=1)
            with pe.If(over > 0):
                last = zero_sums(True)
                last.then_inc(S("dense_down"), 1)
                with pe.Fori(0, NE) as i:
                    pe.wait_ge(S("dense_in"), i * (16 * EXPERT) + 16 * EXPERT)
                    for q in range(TT):
                        for h in range(2):
                            for k in range(KC):
                                last = pe.matmul(pw[2 * q + h][:, :], hf[:, k, q * P:q * P + P],
                                                 raw[:, k, 512 * h:512 * h + 512], start=(k == 0), stop=(k == KC - 1))
                    last.then_inc(S("dense_products"), 1)
                    pe.wait_ge(S("dense_hidden"), i * 2 + 2)
                    for c in range(DE // P):
                        for q in range(TT):
                            a = (c % 2) * T + q * P
                            last = pe.transpose(pw[c // 2][:, a:a + P], dense_hid[:, q, c * P:c * P + P], ident[:])
                    last.then_inc(S("dense_turns"), 1)
                    pe.wait_ge(S("dense_turned"), i * 2 + 2)
                    for k in range(DE // P):
                        for c in range(KC):
                            last = pe.matmul(acc_of(c), raw[:, 8 + k, c * P:c * P + P], dense_turned[:, k, :],
                                             start=False, stop=False, skip_group_check=True)
                    last.then_inc(S("dense_down"), 1)
                last = zero_sums(False)
                last.then_inc(S("dense_down"), 1)
            sq_sums("out")
            norm_spread("out")


def x_score(h):
    return 0 if h == 0 else 2 + 5 * (h - 1)


def x_turn(h):
    return 2 + 5 * h + (2 if h < XH - 1 else 0)


def heads_at(kind, h, g):
    if kind == "d":
        n = 8 * g + h
        return n // 2, n // 2, 64 * (n % 2)
    return 12 + h % 8, 12, 64 * (h // 8)


def mixed_at(kind, h):
    return (h // 2, 64 * (h % 2)) if kind == "d" else (4 + h % 8, 64 * (h // 8))


def _channels(v):
    return np.asarray(v).reshape(-1, P).T


def _col_slabs(w):
    k, n = w.shape
    return w.reshape(k // P, P, n // P, P).transpose(2, 1, 0, 3).reshape(n // P, P, SLAB)


def _row_slabs(w):
    return w.reshape(-1, P, SLAB)


def _value_slabs(w):
    return w.reshape(4, 2, P, -1, 512).transpose(3, 0, 2, 1, 4).reshape(-1, P, SLAB)


def _glu_slabs(g, u, d, J):
    out = np.empty((3 * J, P, SLAB), np.float32)
    for j in range(J):
        out[glu_slab(0, J, "g", j)] = g[j]
        out[glu_slab(0, J, "u", j)] = u[j]
        out[glu_slab(0, J, "d", j)] = d[j]
    return out


def _taps(w):
    k = w.shape[0]
    return w.reshape(k, -1, P).transpose(2, 1, 0).reshape(P, -1)


def _layout(i):
    a = {k: np.asarray(v) for k, v in i.items()}
    w_in = a["ab_w_in"][0]
    gates = np.zeros((4, P, SLAB), np.float32)
    for n in range(4):
        for e in range(2):
            gates[n, :, (2 * e) * P:(2 * e + 1) * P] = a["a_gate_x_w"][0, 2 * n + e]
            gates[n, :, (2 * e + 1) * P:(2 * e + 2) * P] = a["a_gate_a_w"][0, 2 * n + e]
        gates[n, :, 4 * P:5 * P] = a["b_group_w"][0, n]
    gates_values = np.concatenate([gates[:, None], _value_slabs(a["xa_wv"][0]).reshape(4, 2, P, SLAB)], 1)
    gates_values = gates_values.reshape(12, P, SLAB)
    pw1 = _col_slabs(a["c_w_pw1"][0])
    pw1 = np.stack([pw1[:8], pw1[8:]], 1).reshape(16, P, SLAB)
    w2 = a["w_in_2"][0]
    at = np.cumsum([0, 1536, 1536, 1536, 1024, 128, 128, 1024, 1024])
    qd, kd, vd, qs, ks, vs, gd, gs = (w2[:, at[n]:at[n + 1]] for n in range(8))
    qs = qs.reshape(D, 2, 8, 64).transpose(0, 2, 1, 3).reshape(D, D)
    win = [_col_slabs(qd), _col_slabs(kd), _col_slabs(qs), _value_slabs(vd), _col_slabs(ks), _col_slabs(vs),
           _col_slabs(gd), _col_slabs(gs)]
    br_swa = a["w_br_swa_2"][0].reshape(2, 8, 64, D).transpose(1, 0, 2, 3).reshape(D, D)
    about = _row_slabs(a["ab_w_out"][0])[[8, 9, 10, 11, 0, 1, 2, 3, 4, 5, 6, 7]]

    def ffn(l):
        up = _col_slabs(a["f_w_up"][l])
        return _glu_slabs(up[:FJ], up[FJ:], _row_slabs(a["f_w_down"][l]), FJ)

    both = np.concatenate([a["w_e_gate_2"][0], a["w_e_up_2"][0]], 2).reshape(NE, KC, P, SLAB)
    experts = np.concatenate([both, a["w_e_down_2"][0].reshape(NE, DE // P, P, SLAB)], 1).reshape(-1, P, SLAB)
    parts = [_col_slabs(np.concatenate([w_in[:, 2 * D:], w_in[:, :2 * D]], 1)), _col_slabs(a["xa_wk"][0]), gates_values, about,
             _col_slabs(a["xa_wq"][0]), _row_slabs(a["xa_wo"][0]), ffn(0), pw1, _col_slabs(a["xa_wk"][1]),
             _value_slabs(a["xa_wv"][1]), _row_slabs(a["c_w_pw2"][0]), _col_slabs(a["xa_wq"][1]),
             _row_slabs(a["xa_wo"][1]), ffn(1), *win, _row_slabs(a["w_br_dil_2"][0]), _row_slabs(br_swa),
             _row_slabs(a["w_out_2"][0]), experts]
    stream = np.concatenate(parts)
    assert stream.shape == (NSLAB, P, SLAB), stream.shape
    rows = np.broadcast_to
    cols = {"ab_norm": _channels(a["ab_norm"][0]), "a_conv_w": _taps(a["a_conv_w"][0]),
            "a_conv_b": _channels(a["a_conv_b"][0]), "a_gate_x_b": _channels(a["a_gate_x_b"][0]),
            "a_gate_a_b": _channels(a["a_gate_a_b"][0]), "a_lambda": _channels(a["a_lambda"][0]),
            "b_group_b": _channels(a["b_group_b"][0]), "b_scale": _channels(a["b_scale"][0]),
            "c_norm": _channels(a["c_norm"][0]), "c_b_pw1": _channels(a["c_b_pw1"][0]),
            "c_dw_w": _taps(a["c_dw_w"][0]), "c_dw_b": _channels(a["c_dw_b"][0]),
            "c_ln_g": _channels(a["c_ln_g"][0]), "c_ln_b": _channels(a["c_ln_b"][0]),
            "c_b_pw2": _channels(a["c_b_pw2"][0]),
            "final_norm": _channels(a["final_norm"]), "g_mix": _channels(a["g_mix_2"][0]),
            "g_ffn": _channels(a["g_ffn_2"][0]), "g_final": _channels(a["g_final_2"]),
            "sinks": rows(a["sinks_2"][0], (P, 16)),
            "r_bias": rows(np.concatenate([a["b_group_2"][0], a["b_router_2"][0]]), (P, 36))}
    for l in range(2):
        cols[f"xa_norm{l}"] = _channels(a["xa_norm"][l])
        cols[f"mem_norm{l}"] = _channels(a["xa_mem_norm"][l])
        cols[f"f_norm{l}"] = _channels(a["f_norm"][l])
        cols[f"f_dw_w{l}"] = _taps(a["f_dw_w"][l])
        cols[f"f_dw_b{l}"] = _channels(a["f_dw_b"][l])
    packed = np.concatenate([cols[name] for name, _ in COLS], 1)
    tok = np.arange(T)
    inv = np.stack([1.0 / np.minimum(tok + 1, w) for w in POOLS]).reshape(1, -1)
    konst = np.concatenate([np.eye(P), np.broadcast_to(inv, (P, 4 * T))], 1).astype(np.float32)
    dist = tok[:, None] - tok[None, :]
    kinds = [(dist >= 0) & (dist <= 128), (dist >= 0) & (dist % 4 == 0), (dist >= 0) & (dist % 16 == 0),
             (dist >= 0) & (dist <= 127)]
    masks = np.empty((P, 4, 3 * P), np.float32)
    for n, ok in enumerate(kinds):
        m = np.where(ok, dist, -NEG)
        masks[:, n, :P] = m[:P, :P]
        masks[:, n, P:] = m[P:, :]
    def turned(v):
        return np.ascontiguousarray(np.asarray(v)[0].T.reshape(KC, P, T).transpose(1, 0, 2))

    router = np.concatenate([a["w_group_2"][0], a["w_router_2"][0]], 1).reshape(KC, P, 36).transpose(1, 0, 2)
    router = np.concatenate([router.reshape(P, -1), np.triu(np.ones((P, P), np.float32)),
                             np.broadcast_to(np.arange(1, CAP + 1, dtype=np.float32), (P, CAP))], 1)
    return {"stream": stream, "cols": packed, "konst": konst, "masks": masks, "x": turned(a["x"]),
            "mem": turned(a["mem"]), "router": router}


def kernel(**inputs):
    import concourse.bacc as bacc
    from concourse.bass_utils import run_bass_kernel_spmd

    nc = bacc.Bacc("TRN2", target_bir_lowering=False, num_devices=1)
    arrays, args = {}, []
    for name, a in _layout(inputs).items():
        arrays[f"in_{name}"] = np.ascontiguousarray(a)
        args.append(nc.dram_tensor(f"in_{name}", a.shape, F32, kind="ExternalInput").ap())
    args.append(nc.dram_tensor("out", (P, KC, T), F32, kind="ExternalOutput").ap())
    program(nc, *args)
    got = run_bass_kernel_spmd(nc, [arrays], core_ids=[0]).results[0]["out"]
    return got.transpose(1, 0, 2).reshape(D, T).T[None]
```
